# Optimizing a Trainium2 kernel written in Bass

```python
import math
import jax, jax.numpy as jnp
from jax import lax
import numpy as np

D_MODEL = 1024
BATCH = 1
SEQ = 2048
DEPTH = 1

CTX_LEN = 256
GRID_W = 64
RMS_EPS = 1e-6
ROPE_BASE = 10000.0

GDN_HEADS = 4
GDN_DK = 128
GDN_DV = 128
GDN_QK_W = GDN_HEADS * GDN_DK
GDN_V_W = GDN_HEADS * GDN_DV
CONV_W = 5
CHUNK = 64
N_DIR = 2

FNET_GROUPS = 4
FNET_GROUP_CH = 64
FNET_W = FNET_GROUPS * FNET_GROUP_CH

NA_HEADS = 4
NA_DH = 64
NA_W = NA_HEADS * NA_DH
WIN_R = 8
WIN_C = 16

N_BRANCH = 3

N_EXPERTS = 16
EC_CAPACITY_FACTOR = 2
D_EXPERT = 1024

IN_SPLITS = (GDN_QK_W, GDN_QK_W, GDN_V_W, GDN_V_W, N_DIR * GDN_HEADS, N_DIR * GDN_HEADS,
             FNET_W, NA_W, NA_W, NA_W, N_BRANCH * D_MODEL)
N_IN = sum(IN_SPLITS)

kernel_name = 'hybrid_gdn_fnet_natten_ec_moe_dit'

def split_cols(p):
    idx = np.cumsum(IN_SPLITS)[:-1].tolist()
    return jnp.split(p, idx, axis=-1)

def rmsnorm(x, w):
    xf = x.astype(jnp.float32)
    y = xf * lax.rsqrt(jnp.mean(xf * xf, axis=-1, keepdims=True) + RMS_EPS)
    return (y * w.astype(jnp.float32)).astype(x.dtype)

def l2norm(x):
    xf = x.astype(jnp.float32)
    return (xf * lax.rsqrt(jnp.sum(xf * xf, axis=-1, keepdims=True) + RMS_EPS)).astype(x.dtype)

def axial_rope(x):
    b_, t_, h_, dh = x.shape
    nf = dh // 4
    inv = ROPE_BASE ** (-jnp.arange(nf, dtype=jnp.float32) / nf)
    t = jnp.arange(t_)
    pos = jnp.stack([t // GRID_W, t % GRID_W], axis=-1).astype(jnp.float32)
    ang = pos[:, :, None] * inv
    cos = jnp.cos(ang)[None, :, None]
    sin = jnp.sin(ang)[None, :, None]
    xr = x.astype(jnp.float32).reshape(b_, t_, h_, 2, 2, nf)
    x1, x2 = xr[..., 0, :], xr[..., 1, :]
    out = jnp.stack([x1 * cos - x2 * sin, x2 * cos + x1 * sin], axis=-2)
    return out.reshape(b_, t_, h_, dh).astype(x.dtype)

def short_conv(u, w):
    ch = u.shape[-1]
    return lax.conv_general_dilated(u, w[:, None, :].astype(u.dtype), window_strides=(1,),
                                    padding=[(CONV_W // 2, CONV_W // 2)],
                                    dimension_numbers=('NWC', 'WIO', 'NWC'), feature_group_count=ch)

def gdn_prep(q, k, v, a, b, conv_w, a_log, dt_bias, rotary):
    b_, t_, _ = q.shape
    qkv = jax.nn.silu(short_conv(jnp.concatenate([q, k, v], axis=-1), conv_w))
    q, k, v = jnp.split(qkv, [GDN_QK_W, 2 * GDN_QK_W], axis=-1)
    q = l2norm(q.reshape(b_, t_, GDN_HEADS, GDN_DK))
    k = l2norm(k.reshape(b_, t_, GDN_HEADS, GDN_DK))
    if rotary:
        q = axial_rope(q)
        k = axial_rope(k)
    q = q * (GDN_DK ** -0.5)
    v = v.reshape(b_, t_, GDN_HEADS, GDN_DV)
    a = a.reshape(b_, t_, N_DIR, GDN_HEADS).astype(jnp.float32)
    g = -jnp.exp(a_log.astype(jnp.float32)) * jax.nn.softplus(a + dt_bias.astype(jnp.float32))
    beta = jax.nn.sigmoid(b.reshape(b_, t_, N_DIR, GDN_HEADS).astype(jnp.float32))
    return q, k, v, g, beta

def gdn_chunked(q, k, v, g, beta, s0):
    f32 = jnp.float32
    b_, t_, h_, _ = q.shape
    dv = v.shape[-1]
    n = t_ // CHUNK

    def chunks(a):
        a = a.astype(f32).reshape(b_, n, CHUNK, h_, *a.shape[3:])
        return jnp.moveaxis(jnp.moveaxis(a, 1, 0), 3, 2)

    qc, kc, vc = chunks(q), chunks(k), chunks(v)
    gc = jnp.cumsum(chunks(g), axis=-1)
    bc = chunks(beta)
    kb = kc * bc[..., None]
    vb = vc * bc[..., None]
    tri = jnp.tril(jnp.ones((CHUNK, CHUNK), bool))
    strict = jnp.tril(jnp.ones((CHUNK, CHUNK), bool), -1)
    diff = gc[..., :, None] - gc[..., None, :]
    decay = jnp.where(tri, jnp.exp(jnp.where(tri, diff, 0.0)), 0.0)
    m = jnp.where(strict, jnp.einsum('nbhik,nbhjk->nbhij', kb, kc) * decay, 0.0)
    a_mat = m + jnp.eye(CHUNK, dtype=f32)
    rhs = jnp.concatenate([vb, kb * jnp.exp(gc)[..., None]], axis=-1)
    sol = lax.linalg.triangular_solve(a_mat, rhs, left_side=True, lower=True, unit_diagonal=True)
    u, w = sol[..., :dv], sol[..., dv:]
    qk = jnp.where(tri, jnp.einsum('nbhik,nbhjk->nbhij', qc, kc) * decay, 0.0)
    qg = qc * jnp.exp(gc)[..., None]
    kg = kc * jnp.exp(gc[..., -1:] - gc)[..., None]
    g_last = jnp.exp(gc[..., -1])

    def step(s, inp):
        qg_i, kg_i, u_i, w_i, qk_i, gl_i = inp
        v_new = u_i - jnp.einsum('bhck,bhkv->bhcv', w_i, s)
        o = jnp.einsum('bhck,bhkv->bhcv', qg_i, s) + jnp.einsum('bhij,bhjv->bhiv', qk_i, v_new)
        s = s * gl_i[..., None, None] + jnp.einsum('bhck,bhcv->bhkv', kg_i, v_new)
        return s, o

    s_fin, o = lax.scan(step, s0.astype(f32), (qg, kg, u, w, qk, g_last))
    o = jnp.swapaxes(jnp.moveaxis(o, 0, 1), 2, 3).reshape(b_, t_, h_, dv)
    return o.astype(v.dtype), s_fin

def gdn_bidir(q, k, v, g, beta, s0_fwd, s0_bwd):
    o_f, s_f = gdn_chunked(q, k, v, g[:, :, 0], beta[:, :, 0], s0_fwd)
    fl = lambda a: jnp.flip(a, axis=1)
    o_b, s_b = gdn_chunked(fl(q), fl(k), fl(v), fl(g[:, :, 1]), fl(beta[:, :, 1]), s0_bwd)
    return o_f + fl(o_b), s_f, s_b

def gdn_out(o, z, norm_w):
    b_, t_, _, _ = o.shape
    zh = z.reshape(b_, t_, GDN_HEADS, GDN_DV)
    return (rmsnorm(o, norm_w) * jax.nn.silu(zh)).reshape(b_, t_, GDN_V_W)

def fourier_mix(u):
    b_, t_, _ = u.shape
    ug = u.astype(jnp.float32).reshape(b_, t_, FNET_GROUPS, FNET_GROUP_CH)
    y = jnp.fft.fftn(ug, axes=(1, 3), norm='ortho').real
    return y.reshape(b_, t_, FNET_W).astype(u.dtype)

def na_latent(q, k, v, k_ctx, v_ctx, rpb):
    b_, t_, h_, dh = q.shape
    rows = t_ // GRID_W
    kr = min(WIN_R, rows)
    qg = q.reshape(b_, rows, GRID_W, h_, dh)
    kg = k.reshape(b_, rows, GRID_W, h_, dh)
    vg = v.reshape(b_, rows, GRID_W, h_, dh)
    r_ids = jnp.arange(rows)
    c_ids = jnp.arange(GRID_W)
    r_start = jnp.clip(r_ids - kr // 2, 0, rows - kr)
    c_start = jnp.clip(c_ids - WIN_C // 2, 0, GRID_W - WIN_C)
    col_idx = c_start[:, None] + jnp.arange(WIN_C)
    dc = col_idx - c_ids[:, None] + (WIN_C - 1)
    scale = dh ** -0.5
    n_loc = kr * WIN_C

    def row_block(r):
        rs = r_start[r]
        q_r = lax.dynamic_index_in_dim(qg, r, axis=1, keepdims=False)
        k_r = lax.dynamic_slice_in_dim(kg, rs, kr, axis=1)[:, :, col_idx]
        v_r = lax.dynamic_slice_in_dim(vg, rs, kr, axis=1)[:, :, col_idx]
        dr = rs + jnp.arange(kr) - r + (WIN_R - 1)
        bias = jnp.transpose(rpb[:, dr][:, :, dc], (0, 2, 1, 3))
        s_loc = jnp.einsum('bjhd,bajchd->bhjac', q_r, k_r).astype(jnp.float32) * scale + bias.astype(jnp.float32)
        s_ctx = jnp.einsum('bjhd,blhd->bhjl', q_r, k_ctx).astype(jnp.float32) * scale
        s = jnp.concatenate([s_loc.reshape(b_, h_, GRID_W, n_loc), s_ctx], axis=-1)
        p = jax.nn.softmax(s, axis=-1).astype(v.dtype)
        p_loc = p[..., :n_loc].reshape(b_, h_, GRID_W, kr, WIN_C)
        return (jnp.einsum('bhjac,bajchd->bjhd', p_loc, v_r)
                + jnp.einsum('bhjl,blhd->bjhd', p[..., n_loc:], v_ctx))

    o = lax.map(row_block, r_ids)
    return jnp.transpose(o, (1, 0, 2, 3, 4)).reshape(b_, t_, h_ * dh)

def na_context(q, k, v):
    b_, l_, h_, dh = q.shape
    s = jnp.einsum('blhd,bmhd->bhlm', q, k).astype(jnp.float32) * (dh ** -0.5)
    p = jax.nn.softmax(s, axis=-1).astype(v.dtype)
    return jnp.einsum('bhlm,bmhd->blhd', p, v).reshape(b_, l_, h_ * dh)

def merge(g_raw, oa, ob, oc, w_br_a, w_br_b, w_br_c, w_out):
    ga, gb, gc = jnp.split(jax.nn.sigmoid(g_raw), N_BRANCH, axis=-1)
    y = ga * (oa @ w_br_a) + gb * (ob @ w_br_b) + gc * (oc @ w_br_c)
    return y @ w_out

def mixer(h, hc, w_in, conv_w, a_log, dt_bias, gdn_norm_w, na_qn_w, na_kn_w, na_rpb,
          w_br_a, w_br_b, w_br_c, w_out, need_ctx):
    b_, t_, _ = h.shape
    lc = hc.shape[1]
    qa, ka, va, za, aa, ba, ub, qn, kn, vn, gr = split_cols(h @ w_in)
    qac, kac, vac, zac, aac, bac, ubc, qnc, knc, vnc, grc = split_cols(hc @ w_in)
    ql, kl, vl, gl, bl = gdn_prep(qa, ka, va, aa, ba, conv_w, a_log, dt_bias, True)
    qc_, kc_, vc_, gc_, bc_ = gdn_prep(qac, kac, vac, aac, bac, conv_w, a_log, dt_bias, False)
    zero = jnp.zeros((b_, GDN_HEADS, GDN_DK, GDN_DV), jnp.float32)
    o_ac, s_f, s_b = gdn_bidir(qc_, kc_, vc_, gc_, bc_, zero, zero)
    o_al, _, _ = gdn_bidir(ql, kl, vl, gl, bl, s_f, s_b)
    heads = lambda u: u.reshape(u.shape[0], u.shape[1], NA_HEADS, NA_DH)
    k_ctx = rmsnorm(heads(knc), na_kn_w)
    v_ctx = heads(vnc)
    o_cl = na_latent(rmsnorm(heads(qn), na_qn_w), rmsnorm(heads(kn), na_kn_w), heads(vn), k_ctx, v_ctx, na_rpb)
    y_lat = merge(gr, gdn_out(o_al, za, gdn_norm_w), fourier_mix(ub), o_cl, w_br_a, w_br_b, w_br_c, w_out)
    if not need_ctx:
        return y_lat, None
    o_cc = na_context(rmsnorm(heads(qnc), na_qn_w), k_ctx, v_ctx)
    y_ctx = merge(grc, gdn_out(o_ac, zac, gdn_norm_w), fourier_mix(ubc), o_cc, w_br_a, w_br_b, w_br_c, w_out)
    return y_lat, y_ctx

def expert_choice_ffn(h, w_router, w_gate, w_up, w_down):
    b_, t_, _ = h.shape
    cap = EC_CAPACITY_FACTOR * t_ // N_EXPERTS
    aff = jax.nn.softmax(jnp.einsum('btd,de->bte', h, w_router).astype(jnp.float32), axis=-1)
    top_aff, top_idx = lax.top_k(jnp.swapaxes(aff, 1, 2), cap)
    bidx = jnp.arange(b_)[:, None, None]
    xe = h[bidx, top_idx]
    hid = jax.nn.silu(jnp.einsum('becd,edf->becf', xe, w_gate)) * jnp.einsum('becd,edf->becf', xe, w_up)
    ye = jnp.einsum('becf,efd->becd', hid, w_down) * top_aff[..., None].astype(h.dtype)
    return jnp.zeros_like(h).at[bidx, top_idx].add(ye)

def setup_inputs(seed: int = 0) -> dict:
    key = jax.random.key(seed)
    ks = jax.random.split(key, 26)
    f32 = jnp.float32
    L, D = DEPTH, D_MODEL
    nrm = lambda k, shape, s: jax.random.normal(k, shape, f32) * s
    dt = jnp.exp(jax.random.uniform(ks[11], (L, N_DIR, GDN_HEADS), f32, math.log(1e-3), math.log(1e-1)))
    return {
        'x': nrm(ks[0], (BATCH, SEQ, D), 1.0),
        'c': nrm(ks[1], (BATCH, D), 1.0),
        'ctx': nrm(ks[2], (BATCH, CTX_LEN, D), 1.0),
        'c_ctx': nrm(ks[3], (D,), 1.0),
        'w_mod': nrm(ks[4], (L, D, 6 * D), 0.5 * D ** -0.5),
        'b_mod': nrm(ks[5], (L, 6 * D), 0.01),
        'norm1_w': 1.0 + nrm(ks[6], (L, D), 0.1),
        'norm2_w': 1.0 + nrm(ks[7], (L, D), 0.1),
        'w_in': nrm(ks[8], (L, D, N_IN), D ** -0.5),
        'conv_w': nrm(ks[9], (L, CONV_W, 2 * GDN_QK_W + GDN_V_W), CONV_W ** -0.5),
        'a_log': jnp.log(jax.random.uniform(ks[10], (L, N_DIR, GDN_HEADS), f32, 1.0, 16.0)),
        'dt_bias': dt + jnp.log(-jnp.expm1(-dt)),
        'gdn_norm_w': 1.0 + nrm(ks[12], (L, GDN_DV), 0.1),
        'na_qn_w': 1.0 + nrm(ks[13], (L, NA_DH), 0.1),
        'na_kn_w': 1.0 + nrm(ks[14], (L, NA_DH), 0.1),
        'na_rpb': nrm(ks[15], (L, NA_HEADS, 2 * WIN_R - 1, 2 * WIN_C - 1), 0.1),
        'w_br_a': nrm(ks[16], (L, GDN_V_W, D), GDN_V_W ** -0.5),
        'w_br_b': nrm(ks[17], (L, FNET_W, D), FNET_W ** -0.5),
        'w_br_c': nrm(ks[18], (L, NA_W, D), NA_W ** -0.5),
        'w_out': nrm(ks[19], (L, D, D), D ** -0.5),
        'w_router': nrm(ks[20], (L, D, N_EXPERTS), D ** -0.5),
        'w_e_gate': nrm(ks[21], (L, N_EXPERTS, D, D_EXPERT), D ** -0.5),
        'w_e_up': nrm(ks[22], (L, N_EXPERTS, D, D_EXPERT), D ** -0.5),
        'w_e_down': nrm(ks[23], (L, N_EXPERTS, D_EXPERT, D), D_EXPERT ** -0.5),
    }

def reference(x, c, ctx, c_ctx, w_mod, b_mod, norm1_w, norm2_w, w_in, conv_w, a_log, dt_bias, gdn_norm_w,
              na_qn_w, na_kn_w, na_rpb, w_br_a, w_br_b, w_br_c, w_out, w_router, w_e_gate, w_e_up, w_e_down):
    for i in range(DEPTH):
        last = i == DEPTH - 1
        mod = jax.nn.silu(c) @ w_mod[i] + b_mod[i]
        mod_c = jax.nn.silu(c_ctx) @ w_mod[i] + b_mod[i]
        sh1, sc1, gt1, sh2, sc2, gt2 = jnp.split(mod[:, None, :], 6, axis=-1)
        csh1, csc1, cgt1, csh2, csc2, cgt2 = jnp.split(mod_c[None, None, :], 6, axis=-1)
        h = rmsnorm(x, norm1_w[i]) * (1 + sc1) + sh1
        hc = rmsnorm(ctx, norm1_w[i]) * (1 + csc1) + csh1
        y, yc = mixer(h, hc, w_in[i], conv_w[i], a_log[i], dt_bias[i], gdn_norm_w[i], na_qn_w[i], na_kn_w[i],
                      na_rpb[i], w_br_a[i], w_br_b[i], w_br_c[i], w_out[i], not last)
        x = x + gt1 * y
        h2 = rmsnorm(x, norm2_w[i]) * (1 + sc2) + sh2
        x = x + gt2 * expert_choice_ffn(h2, w_router[i], w_e_gate[i], w_e_up[i], w_e_down[i])
        if not last:
            ctx = ctx + cgt1 * yc
            hc2 = rmsnorm(ctx, norm2_w[i]) * (1 + csc2) + csh2
            ctx = ctx + cgt2 * expert_choice_ffn(hc2, w_router[i], w_e_gate[i], w_e_up[i], w_e_down[i])
    return x


_drawn_inputs = setup_inputs


def setup_inputs(seed=0):
    import zlib

    import numpy as np

    out = dict(_drawn_inputs(seed))
    spreads = {}
    factors = {'ctx': 4.319,
     'b_mod': 6.684,
     'norm2_w': 3.073,
     'a_log': 4.632,
     'gdn_norm_w': 5.456,
     'na_qn_w': 8.0,
     'na_kn_w': 8.0,
     'na_rpb': 8.0}
    for name, (base, spread) in spreads.items():
        noise = np.random.default_rng([zlib.crc32(name.encode()), seed]).standard_normal(out[name].shape)
        drawn = base * np.exp(spread * noise) if base else spread * noise
        out[name] = __import__('jax').numpy.asarray(drawn.astype(out[name].dtype))
    for name, factor in factors.items():
        out[name] = (out[name] * factor).astype(out[name].dtype)
    return out
```

```python
from collections import namedtuple
from contextlib import ExitStack

import numpy as np

import concourse.bass as bass
from concourse import mybir

F32 = mybir.dt.float32
U32 = mybir.dt.uint32
ACT = mybir.ActivationFunctionType
ALU = mybir.AluOpType
AX_X = mybir.AxisListType.X

P = 128
D = 1024
KD = D // P
CTX = 256
SEQ = 2048
T = CTX + SEQ
NT = T // P
CT = CTX // P
LT = SEQ // P
POS = NT + CT
EPS = 1e-6
H = 4
DK = 128
CONV = 5
PAD = CONV // 2
CONVW = T + 3 * PAD
CONVO = CONVW - 2 * PAD
GRID = 64
WR, WC = 8, 16
ROWS = SEQ // GRID
DH = 64
HP = 2
FN = 256
E = 16
CAP = 2 * SEQ // E
FE = 1024
BLOCKS = [(0, CTX)] + [(CTX + 512 * b, 512) for b in range(4)]
NEG = -1e30

C_ID, C_ONE, C_BLK, C_ROT = 0, P, 2 * P, 3 * P
C_DIR = 4 * P
N_DIRT = 2
C_LEV = C_DIR + 2 * N_DIRT * P
N_LEV = 7
C_WIN = C_LEV + 2 * N_LEV * P
C_W = C_WIN + GRID

F_C4 = 0
F_N1 = F_C4 + FN
F_TW = F_N1 + 3 * P
F_K2 = F_TW + 2 * (SEQ // P)
F_W = F_K2 + 2 * P


class Steps:

    def __init__(self, eng, sem, start=0):
        self.eng, self.sem, self.start, self.n = eng, sem, start, 0

    def done(self, ins):
        self.n += 1
        return ins.then_inc(self.sem, 1)

    def settle(self):
        self.eng.wait_ge(self.sem, self.start + self.n)


def hold(eng, sem):
    eng.sem_inc(sem, 1)


def sbuf(nc, c, name, shape, dt=F32):
    return c.enter_context(nc.sbuf_tensor("sb_" + name, shape, dt))


def psum(nc, c, name, shape=(P, 512), dt=F32):
    return c.enter_context(nc.psum_tensor(name, list(shape), dt))


def sems(nc, c, prefix, names):
    made = {n: nc.alloc_semaphore(prefix + "_" + n) for n in names.split()}


    def clear():
        nc.clear_and_free_semaphores(list(made.values()))
        nc.all_engine_barrier()
    c.callback(clear)
    return namedtuple("Semaphores", list(made))(**made)


def modulation(nc, g):
    with ExitStack() as c:
        cc = sbuf(nc, c, "cc", [P, KD, 2])
        cs = sbuf(nc, c, "cs", [P, KD, 2])
        csb = sbuf(nc, c, "csb", [P, KD, P])
        wcol = sbuf(nc, c, "wcol", [P, KD, 2 * D])
        bcol = sbuf(nc, c, "bcol", [P, 2 * KD])
        n1 = sbuf(nc, c, "n1", [P, KD])
        wrow = sbuf(nc, c, "wrow", [P, 2, 2 * D])
        rows = sbuf(nc, c, "rows", [P, 4, D])
        brow = sbuf(nc, c, "brow", [P, 4 * D])
        n2 = sbuf(nc, c, "n2", [P, D])
        ps = psum(nc, c, "mod_ps", (P, 8, 512))
        s = sems(nc, c, "mod", "small srow wcol w0 w1 silu bc col row fin rowfin st used")
        s_w = [s.w0, s.w1]
        pcol = ps[:, 0, 0:4 * KD].rearrange("p (m s) -> p m s", s=2)
        with nc.Block() as block:
            @block.sync
            def _(sp):
                sp.dma_start(cc[:], g.cc).then_inc(s.small, 16)
                sp.dma_start(bcol[:], g.b_mod_col).then_inc(s.small, 16)
                sp.dma_start(n1[:], g.norm1).then_inc(s.small, 16)
                sp.dma_start(wcol[:], g.w_mod_col).then_inc(s.wcol, 16)
                for k in range(2 * KD):
                    if k >= 2:
                        sp.wait_ge(s.used, k - 1)
                    sp.dma_start(wrow[:, k % 2], g.w_mod_row[k]).then_inc(s_w[k % 2], 16)
                sp.wait_ge(s.rowfin, 9)
                sp.dma_start(g.rows_d, rows[:]).then_inc(s.st, 16)
                sp.wait_ge(s.st, 16)

            @block.gpsimd
            def _(pool):
                pool.dma_start(brow[:], g.b_mod_row.partition_broadcast(P)).then_inc(s.srow, 16)
                pool.dma_start(n2[:], g.norm2.partition_broadcast(P)).then_inc(s.srow, 16)

            @block.scalar
            def _(act):
                act.wait_ge(s.small, 48)
                nc.scalar.activation(cs[:], cc[:], ACT.Silu).then_inc(s.silu, 1)

            @block.tensor
            def _(pe):
                pe.wait_ge(s.silu, 1)
                pe.wait_ge(s.wcol, 16)
                for m in range(2 * KD):
                    for k in range(KD):
                        last = nc.tensor.matmul(pcol[:, m], wcol[:, k, m * P:(m + 1) * P], cs[:, k],
                                                start=(k == 0), stop=(k == KD - 1))
                last.then_inc(s.col, 1)
                pe.wait_ge(s.bc, 1)
                pe.wait_ge(s.fin, 3)
                for half in range(2):
                    for k in range(KD):
                        n = half * KD + k
                        pe.wait_ge(s_w[n % 2], 16 * (n // 2 + 1))
                        for j in range(4):
                            last = nc.tensor.matmul(ps[:, half * 4 + j], csb[:, k], wrow[:, n % 2, j * 512:(j + 1) * 512],
                                                    start=(k == 0), stop=(k == KD - 1))
                        last.then_inc(s.used, 1)
                    last = None

            @block.vector
            def _(dve):
                own = Steps(dve, s.fin)
                dve.wait_ge(s.silu, 1)
                nc.vector.tensor_copy(csb[:], cs[:, :, 0:1].broadcast_to([P, KD, P])).then_inc(s.bc, 1)
                dve.wait_ge(s.small, 48)
                dve.wait_ge(s.srow, 32)
                dve.wait_ge(s.col, 1)
                own.done(nc.vector.tensor_tensor(g.mod1[:, 0], pcol[:, 0:KD], bcol[:, 0:KD, None].broadcast_to([P, KD, 2]), ALU.add))
                own.done(nc.vector.tensor_tensor(g.mod1[:, 1], pcol[:, KD:], bcol[:, KD:, None].broadcast_to([P, KD, 2]), ALU.add))
                own.settle()
                own.done(nc.vector.scalar_tensor_tensor(g.mod1[:, 1], g.mod1[:, 1], 1.0, n1[:, :, None].broadcast_to([P, KD, 2]),
                                                        ALU.add, ALU.mult))
                own = Steps(dve, s.rowfin)
                for half in range(2):
                    dve.wait_ge(s.used, (half + 1) * KD)
                    for j in range(half * 4, half * 4 + 4):
                        own.done(nc.vector.tensor_tensor(rows[:, j // 2, (j % 2) * 512:(j % 2 + 1) * 512], ps[:, j],
                                                         brow[:, j * 512:(j + 1) * 512], ALU.add))
                own.settle()
                own.done(nc.vector.scalar_tensor_tensor(rows[:, 2], rows[:, 2], 1.0, n2[:], ALU.add, ALU.mult))


def first_norm(nc, g):
    with ExitStack() as c:
        sq = sbuf(nc, c, "sq", [P, KD, 512])
        rs = sbuf(nc, c, "rs", [P, 512])
        ps = psum(nc, c, "n_ps")
        s = sems(nc, c, "n1", "ld0 ld1 ld2 ld3 ld4 sq sum root dve h st")
        ld = [s.ld0, s.ld1, s.ld2, s.ld3, s.ld4]
        with nc.Block() as block:
            @block.sync
            def _(sp):
                for b, (t0, w) in enumerate(BLOCKS):
                    sp.dma_start(g.hT[:, :, t0:t0 + w], g.xT[:, :, t0:t0 + w]).then_inc(ld[b], 16)
                for b, (t0, w) in enumerate(BLOCKS):
                    sp.wait_ge(s.h, KD * (b + 1))
                    sp.dma_start(g.h_d[:, :, t0:t0 + w], g.hT[:, :, t0:t0 + w]).then_inc(s.st, 16)
                sp.wait_ge(s.st, 16 * len(BLOCKS))

            @block.scalar
            def _(act):
                for b, (t0, w) in enumerate(BLOCKS):
                    act.wait_ge(ld[b], 16)
                    if b:
                        act.wait_ge(s.sum, b)
                    nc.scalar.activation(sq[:, :, 0:w], g.hT[:, :, t0:t0 + w], ACT.Square).then_inc(s.sq, 1)
                    act.wait_ge(s.sum, b + 1)
                    if b:
                        act.wait_ge(s.dve, 2 * b)
                    nc.scalar.activation(rs[:, 0:w], ps[:, 0:w], ACT.Sqrt, bias=g.eps[:, 0:1], scale=1.0 / D).then_inc(s.root, 1)
                    act.wait_ge(s.dve, 2 * b + 2)
                    which = 1 if b == 0 else 0
                    for k in range(KD):
                        nc.scalar.activation(g.hT[:, k, t0:t0 + w], g.hT[:, k, t0:t0 + w], ACT.Identity,
                                             bias=g.mod1[:, 0, k, which:which + 1],
                                             scale=g.mod1[:, 1, k, which:which + 1]).then_inc(s.h, 1)

            @block.tensor
            def _(pe):
                for b, (t0, w) in enumerate(BLOCKS):
                    pe.wait_ge(s.sq, b + 1)
                    if b:
                        pe.wait_ge(s.root, b)
                    for k in range(KD):
                        last = nc.tensor.matmul(ps[:, 0:w], g.ones, sq[:, k, 0:w], start=(k == 0), stop=(k == KD - 1))
                    last.then_inc(s.sum, 1)

            @block.vector
            def _(dve):
                own = Steps(dve, s.dve)
                for b, (t0, w) in enumerate(BLOCKS):
                    dve.wait_ge(s.root, b + 1)
                    own.done(nc.vector.reciprocal(rs[:, 0:w], rs[:, 0:w]))
                    own.settle()
                    own.done(nc.vector.tensor_tensor(g.hT[:, :, t0:t0 + w], g.hT[:, :, t0:t0 + w],
                                                     rs[:, None, 0:w].broadcast_to([P, KD, w]), ALU.mult))


BANKS = 3
NB = len(BLOCKS)
TG = [(j, min(4, NT - j)) for j in range(0, NT, 4)]
NG = len(TG)
NROT = NB - 1


def before(b):
    if b >= BANKS:
        return b - BANKS, 0
    return max(x for x in range(NB) if x % BANKS == b), 1


def staggered(eng, first, second):
    first(0, 0)
    with eng.Fori(0, H - 1) as h:
        for kind in range(3):
            first(h + (kind == 2), (kind + 1) % 3)
            second(h, kind)
    for kind in range(3):
        if kind < 2:
            first(H - 1, kind + 1)
        second(H - 1, kind)


def delta_inputs(nc, g):
    with ExitStack() as c:
        w = sbuf(nc, c, "wq", [P, 3, KD, P])
        raw = sbuf(nc, c, "raw", [P, CONVW])
        cv = sbuf(nc, c, "cv", [P, CONVO])
        sl = sbuf(nc, c, "sl", [P, 3, T])
        tt = sbuf(nc, c, "turned", [P, NT, P])
        rs = sbuf(nc, c, "rsb", [P, 2, 512])
        rope = sbuf(nc, c, "ropeb", [P, 2, SEQ])
        tmp = sbuf(nc, c, "tmp", [P, 512])
        cw = sbuf(nc, c, "cw", [P, H, 3, CONV])
        ps = psum(nc, c, "p_ps", (P, BANKS, 512))
        pn = psum(nc, c, "pn_ps", (P, 2, 512))
        pr = psum(nc, c, "pr_ps")
        pt = psum(nc, c, "pt_ps", (P, 2, 512))
        s = sems(nc, c, "di", "w0 w1 w2 tab zero conv proj rawp cdone silu sq sum root rec nrm perm mul rot tr trc stq stk stv stt")
        s_w = [s.w0, s.w1, s.w2]
        s_st = [s.stq, s.stk]
        dst = (g.q_d, g.k_d, g.kt_d, g.vt_d)

        with nc.Block() as block:
            @block.sync
            def _(sp):
                sp.dma_start(cw[:], g.conv_w).then_inc(s.tab, 16)
                sp.dma_start(rope[:], g.rope).then_inc(s.tab, 16)

                def store(h, tensor, src, sem):
                    sp.dma_start(tensor[0:NT, :, h].rearrange("n p c -> p n c"), src).then_inc(sem, 16)
                    sp.dma_start(tensor[NT:POS, :, h].rearrange("n p c -> p n c"), src[:, 0:CT]).then_inc(sem, 16)

                def stores(h):
                    for kind in range(2):
                        sp.wait_ge(s.rot, NROT * (2 * h + kind + 1))
                        store(h, dst[kind], sl[:, kind].rearrange("p (n c) -> p n c", c=P), s_st[kind])
                    for kind in range(2):
                        sp.wait_ge(s.trc, NG * (2 * h + kind + 1))
                        store(h, dst[2 + kind], tt[:], s.stt)
                with nc.sync.Fori(0, H) as h:
                    stores(h)
                for sem, n in ((s.stq, 32 * H), (s.stk, 32 * H), (s.stt, 64 * H)):
                    sp.wait_ge(sem, n)

            @block.gpsimd
            def _(pool):
                for kind in range(3):
                    pool.dma_start(w[:, kind], g.w_ch[kind * H]).then_inc(s_w[kind], 16)
                with nc.gpsimd.Fori(0, H - 1) as h:
                    for kind in range(3):
                        pool.wait_ge(s.proj, NB * (3 * h + kind + 1))
                        pool.dma_start(w[:, kind], g.w_ch[kind * H + h + 1]).then_inc(s_w[kind], 16)

            @block.tensor
            def _(pe):
                def project(h, kind):
                    t = 3 * h + kind
                    pe.wait_ge(s_w[kind], 16 * h + 16)
                    for b, (t0, wd) in enumerate(BLOCKS):
                        bb, back = before(b)
                        pe.wait_ge(s.rawp, NB * (t + 1 - back) + bb + 1)
                        for k in range(KD):
                            last = nc.tensor.matmul(ps[:, b % BANKS, 0:wd], w[:, kind, k], g.hT[:, k, t0:t0 + wd],
                                                    start=(k == 0), stop=(k == KD - 1))
                        last.then_inc(s.proj, 1)

                def finish(h, kind):
                    if kind < 2:
                        r = 2 * h + kind
                        pe.wait_ge(s.sq, r + 1)
                        for b, (t0, wd) in enumerate(BLOCKS):
                            pe.wait_ge(s.root, NB * r + max(b - 1, 0))
                            nc.tensor.matmul(pn[:, b % 2, 0:wd], g.ones, cv[:, t0:t0 + wd],
                                             start=True, stop=True).then_inc(s.sum, 1)
                        for b in range(NROT):
                            t0, wd = BLOCKS[b + 1]
                            pe.wait_ge(s.nrm, NB * r + b + 2)
                            pe.wait_ge(s.rot, NROT * r + b)
                            nc.tensor.matmul(pr[:, 0:wd], g.rot, sl[:, kind, t0:t0 + wd],
                                             start=True, stop=True).then_inc(s.perm, 1)
                    if kind > 0:
                        m = 2 * h + kind - 1
                        if kind == 1:
                            pe.wait_ge(s.rot, NROT * (2 * h + 2))
                        else:
                            pe.wait_ge(s.silu, 2 * (3 * h + 3))
                        for j, (n0, cnt) in enumerate(TG):
                            pe.wait_ge(s.trc, NG * m + max(j - 1, 0))
                            for i in range(cnt):
                                last = nc.tensor.transpose(pt[:, j % 2, i * P:(i + 1) * P],
                                                           sl[:, kind, (n0 + i) * P:(n0 + i + 1) * P], g.ident)
                            last.then_inc(s.tr, 1)
                staggered(nc.tensor, project, finish)

            @block.scalar
            def _(act):
                act.sem_inc(s.rawp, NB)
                act.wait_ge(s.zero, 1)

                def copy_raw(h, kind):
                    t = 3 * h + kind
                    act.wait_ge(s.cdone, t)
                    for b, (t0, wd) in enumerate(BLOCKS):
                        act.wait_ge(s.proj, NB * t + b + 1)
                        at = t0 + PAD * (1 if b == 0 else 2)
                        nc.scalar.activation(raw[:, at:at + wd], ps[:, b % BANKS, 0:wd], ACT.Copy).then_inc(s.rawp, 1)

                def activate(h, kind):
                    t = 3 * h + kind
                    act.wait_ge(s.cdone, t + 1)
                    if kind < 2:
                        act.wait_ge(s_st[kind], 32 * h)
                    if kind > 0:
                        act.wait_ge(s.tr, NG * (2 * h + kind - 1))
                    own = Steps(act, s.silu, 2 * t)
                    own.done(nc.scalar.activation(sl[:, kind, 0:CTX], cv[:, 0:CTX], ACT.Silu))
                    own.done(nc.scalar.activation(sl[:, kind, CTX:T], cv[:, CTX + PAD:CONVO], ACT.Silu))
                    if kind < 2:
                        own.settle()
                        nc.scalar.activation(cv[:, 0:T], sl[:, kind], ACT.Square).then_inc(s.sq, 1)

                def finish(h, kind):
                    if kind < 2:
                        r = 2 * h + kind
                        for b, (t0, wd) in enumerate(BLOCKS):
                            act.wait_ge(s.sum, NB * r + b + 1)
                            act.wait_ge(s.nrm, NB * r + max(b - 1, 0))
                            nc.scalar.activation(rs[:, b % 2, 0:wd], pn[:, b % 2, 0:wd], ACT.Sqrt,
                                                 bias=g.eps[:, 0:1]).then_inc(s.root, 1)
                    if kind > 0:
                        m = 2 * h + kind - 1
                        act.wait_ge(s.stt, 32 * m)
                        for j, (n0, cnt) in enumerate(TG):
                            act.wait_ge(s.tr, NG * m + j + 1)
                            nc.scalar.activation(tt[:, n0:n0 + cnt], pt[:, j % 2, 0:cnt * P], ACT.Copy).then_inc(s.trc, 1)

                copy_raw(0, 0)
                activate(0, 0)

                def step(h, kind, last):
                    if not last:
                        copy_raw(h + (kind == 2), (kind + 1) % 3)
                    finish(h, kind)
                    if not last:
                        activate(h + (kind == 2), (kind + 1) % 3)
                with nc.scalar.Fori(0, H - 1) as h:
                    for kind in range(3):
                        step(h, kind, False)
                for kind in range(3):
                    step(H - 1, kind, kind == 2)

            @block.vector
            def _(dve):
                nc.vector.memset(raw[:], 0.0).then_inc(s.zero, 1)
                dve.wait_ge(s.tab, 32)

                def convolve(h, kind):
                    t = 3 * h + kind
                    dve.wait_ge(s.rawp, NB * (t + 2))
                    dve.wait_ge(s.silu, 2 * t)
                    if kind == 1:
                        dve.wait_ge(s.sum, NB * (2 * h + 1))
                    if kind == 2:
                        dve.wait_ge(s.sum, NB * (2 * h + 2))
                    own = Steps(dve, s.conv, (CONV - 1) * t)
                    own.done(nc.vector.tensor_scalar(cv[:], raw[:, 0:CONVO], cw[:, h, kind, 0:1], None, ALU.mult))
                    for i in range(1, CONV):
                        own.settle()
                        ins = nc.vector.scalar_tensor_tensor(cv[:], raw[:, i:i + CONVO], cw[:, h, kind, i:i + 1], cv[:],
                                                             ALU.mult, ALU.add)
                        if i < CONV - 1:
                            own.done(ins)
                        else:
                            ins.then_inc(s.cdone, 1)

                def finish(h, kind):
                    if kind == 2:
                        return
                    r = 2 * h + kind
                    scale = DK ** -0.5 if kind == 0 else 1.0
                    for b, (t0, wd) in enumerate(BLOCKS):
                        dve.wait_ge(s.root, NB * r + b + 1)
                        nc.vector.reciprocal(rs[:, b % 2, 0:wd], rs[:, b % 2, 0:wd]).then_inc(s.rec, 1)
                        dve.wait_ge(s.rec, NB * r + b + 1)
                        nc.vector.scalar_tensor_tensor(sl[:, kind, t0:t0 + wd], rs[:, b % 2, 0:wd], scale,
                                                       sl[:, kind, t0:t0 + wd], ALU.mult, ALU.mult).then_inc(s.nrm, 1)
                    for b in range(NROT):
                        t0, wd = BLOCKS[b + 1]
                        n = NROT * r + b
                        dve.wait_ge(s.perm, n + 1)
                        own = Steps(dve, s.mul, 2 * n)
                        dve.wait_ge(s.rot, n)
                        own.done(nc.vector.tensor_tensor(tmp[:], pr[:], rope[:, 1, b * 512:(b + 1) * 512], ALU.mult))
                        own.done(nc.vector.tensor_tensor(sl[:, kind, t0:t0 + wd], sl[:, kind, t0:t0 + wd],
                                                         rope[:, 0, b * 512:(b + 1) * 512], ALU.mult))
                        own.settle()
                        nc.vector.tensor_tensor(sl[:, kind, t0:t0 + wd], sl[:, kind, t0:t0 + wd], tmp[:],
                                                ALU.add).then_inc(s.rot, 1)

                convolve(0, 0)

                def step(h, kind, last):
                    finish(h, kind)
                    if not last:
                        convolve(h + (kind == 2), (kind + 1) % 3)
                with nc.vector.Fori(0, H - 1) as h:
                    for kind in range(3):
                        step(h, kind, False)
                for kind in range(3):
                    step(H - 1, kind, kind == 2)


def mixer_inputs(nc, g):
    LB = BLOCKS[1:]
    NL = len(LB)
    REST = [(16, g.qn[:, 0], False), (17, g.qn[:, 1], False), (20, g.uT[:, 0], False), (21, g.uT[:, 1], False),
            (18, g.kn[:, 0], True), (19, g.kn[:, 1], True)]
    NORM = [(g.qn[:, j, 512 * b:512 * (b + 1)], 0) for j in range(HP) for b in range(NL)]
    NORM += [(g.kn[:, j, t0:t0 + wd], 1) for j in range(HP) for t0, wd in BLOCKS]
    assert len(NORM) == NT
    with ExitStack() as c:
        w = sbuf(nc, c, "wz", [P, 2, KD, P])
        wt = sbuf(nc, c, "wt", [P, KD, 2 * P + 16])
        zb = sbuf(nc, c, "zb", [P, 2, SEQ])
        vb = sbuf(nc, c, "vb", [P, NT, 2 * P])
        sq = sbuf(nc, c, "sqn", [P, 2, 512])
        rs = sbuf(nc, c, "rsn", [P, 2, 512])
        nw = sbuf(nc, c, "nw", [P, 2])
        ps = psum(nc, c, "z_ps", (P, 5, 512))
        pn = psum(nc, c, "zn_ps")
        pt = psum(nc, c, "zt_ps", (P, 2, 512))
        s = sems(nc, c, "mi", "w0 w1 wt blk blkc ev evc z0 z1 tok vcp acp sq sum root rec nrm st")
        s_w, s_z = [s.w0, s.w1], [s.z0, s.z1]
        NZ = H
        with nc.Block() as block:
            @block.sync
            def _(sp):
                sp.dma_start(nw[:], g.na_norm).then_inc(s.wt, 16)
                sp.dma_start(wt[:], g.w_tok).then_inc(s.wt, 16)
                with nc.sync.Fori(0, NZ // 2) as i:
                    for u in range(2):
                        sp.wait_ge(s.ev, NL * (2 * i + u + 2))
                        sp.dma_start(g.z_d[2 * i + u], zb[:, u]).then_inc(s_z[u], 16)
                sp.wait_ge(s.vcp, NT)
                sp.dma_start(g.v_d.rearrange("(n p) c -> p n c", p=P), vb[:]).then_inc(s.st, 16)
                sp.wait_ge(s.z0, 16 * NZ // 2)
                sp.wait_ge(s.z1, 16 * NZ // 2)
                sp.wait_ge(s.st, 16)

            @block.gpsimd
            def _(pool):
                for n in range(NZ + len(REST)):
                    if n >= 2:
                        pool.wait_ge(s.blk, NL * (n - 1))
                    pool.dma_start(w[:, n % 2], g.w_ch[12 + n if n < NZ else REST[n - NZ][0]]).then_inc(s_w[n % 2], 16)

            @block.tensor
            def _(pe):
                def project(u, b, t0, wd):
                    for k in range(KD):
                        last = nc.tensor.matmul(ps[:, b, 0:wd], w[:, u, k], g.hT[:, k, t0:t0 + wd],
                                                start=(k == 0), stop=(k == KD - 1))
                    return last

                with nc.tensor.Fori(0, NZ // 2) as i:
                    for u in range(2):
                        pe.wait_ge(s_w[u], 16 * i + 16)
                        for b, (t0, wd) in enumerate(LB):
                            pe.wait_ge(s.ev, NL * (2 * i + u) + b + 1)
                            project(u, b, t0, wd).then_inc(s.blk, 1)
                ctxs = 0
                for n, (_, _, ctx) in enumerate(REST, NZ):
                    pe.wait_ge(s_w[n % 2], 16 * (n // 2 + 1))
                    if ctx:
                        if ctxs:
                            pe.wait_ge(s.evc, ctxs)
                        project(n % 2, NL, *BLOCKS[0]).then_inc(s.blkc, 1)
                        ctxs += 1
                    for b, (t0, wd) in enumerate(LB):
                        pe.wait_ge(s.ev, NL * n + b + 1)
                        project(n % 2, b, t0, wd).then_inc(s.blk, 1)
                pe.wait_ge(s.wt, 32)
                for i in range(NT):
                    if i >= 2:
                        pe.wait_ge(s.vcp, i - 1)
                        pe.wait_ge(s.acp, i - 1)
                    for k in range(KD):
                        last = nc.tensor.matmul(pt[:, i % 2, 0:2 * P + 16], g.hT[:, k, i * P:(i + 1) * P], wt[:, k],
                                                start=(k == 0), stop=(k == KD - 1))
                    last.then_inc(s.tok, 1)
                    wd = NORM[i][0].shape[-1]
                    pe.wait_ge(s.sq, i + 1)
                    if i:
                        pe.wait_ge(s.root, i)
                    nc.tensor.matmul(pn[:, 0:wd], g.blk, sq[:, i % 2, 0:wd], start=True, stop=True).then_inc(s.sum, 1)

            @block.scalar
            def _(act):
                act.sem_inc(s.ev, NL)
                with nc.scalar.Fori(0, NZ // 2) as i:
                    for u in range(2):
                        act.wait_ge(s_z[u], 16 * i)
                        for b in range(NL):
                            act.wait_ge(s.blk, NL * (2 * i + u) + b + 1)
                            nc.scalar.activation(zb[:, u, b * 512:(b + 1) * 512], ps[:, b], ACT.Silu).then_inc(s.ev, 1)
                ctxs = 0
                for n, (_, dst, ctx) in enumerate(REST, NZ):
                    if ctx:
                        ctxs += 1
                        act.wait_ge(s.blkc, ctxs)
                        nc.scalar.activation(dst[:, 0:CTX], ps[:, NL, 0:CTX], ACT.Copy).then_inc(s.evc, 1)
                    for b, (t0, wd) in enumerate(LB):
                        act.wait_ge(s.blk, NL * n + b + 1)
                        t0 -= 0 if ctx else CTX
                        nc.scalar.activation(dst[:, t0:t0 + wd], ps[:, b], ACT.Copy).then_inc(s.ev, 1)

                def root(i):
                    wd = NORM[i][0].shape[-1]
                    act.wait_ge(s.sum, i + 1)
                    if i >= 2:
                        act.wait_ge(s.nrm, i - 1)
                    nc.scalar.activation(rs[:, i % 2, 0:wd], pn[:, 0:wd], ACT.Sqrt, bias=g.eps[:, 0:1],
                                         scale=1.0 / DH).then_inc(s.root, 1)
                act.wait_ge(s.ev, NL * (NZ + len(REST) + 1))
                act.wait_ge(s.evc, 2)
                for i in range(NT):
                    view, _ = NORM[i]
                    wd = view.shape[-1]
                    if i >= 2:
                        act.wait_ge(s.sum, i - 1)
                    nc.scalar.activation(sq[:, i % 2, 0:wd], view, ACT.Square).then_inc(s.sq, 1)
                    act.wait_ge(s.tok, i + 1)
                    nc.scalar.activation(vb[:, i], pt[:, i % 2, 0:2 * P], ACT.Copy).then_inc(s.vcp, 1)
                    nc.scalar.activation(g.ab[:, i], pt[:, i % 2, 2 * P:2 * P + 16], ACT.Copy).then_inc(s.acp, 1)
                    if i:
                        root(i - 1)
                root(NT - 1)

            @block.vector
            def _(dve):
                dve.wait_ge(s.wt, 32)
                nc.vector.tensor_scalar(nw[:, 0:1], nw[:, 0:1], DH ** -0.5, None, ALU.mult).then_inc(s.rec, 1)

                def norm(i):
                    view, which = NORM[i]
                    wd = view.shape[-1]
                    dve.wait_ge(s.root, i + 1)
                    nc.vector.reciprocal(rs[:, i % 2, 0:wd], rs[:, i % 2, 0:wd]).then_inc(s.rec, 1)
                    dve.wait_ge(s.rec, i + 2)
                    nc.vector.scalar_tensor_tensor(view, view, nw[:, which:which + 1], rs[:, i % 2, 0:wd],
                                                   ALU.mult, ALU.mult).then_inc(s.nrm, 1)
                for i in range(NT):
                    norm(i)


def decays(nc, g):
    with ExitStack() as c:
        par = sbuf(nc, c, "par", [P, 2, 8])
        x, y, t, acc = (sbuf(nc, c, "dec" + n, [P, NT, 8]) for n in "xyta")
        ps = psum(nc, c, "dec_ps", (P, 4, POS * H))
        s = sems(nc, c, "de", "par ea ay beta own sum ex")
        with nc.Block() as block:
            @block.gpsimd
            def _(pool):
                pool.dma_start(par[:, 0], g.a_log.partition_broadcast(P)).then_inc(s.par, 16)
                pool.dma_start(par[:, 1], g.dt_bias.partition_broadcast(P)).then_inc(s.par, 16)

            @block.scalar
            def _(act):
                act.wait_ge(s.par, 32)
                nc.scalar.activation(par[:, 0], par[:, 0], ACT.Exp).then_inc(s.ea, 1)
                act.wait_ge(s.own, 2)
                nc.scalar.activation(y[:], y[:], ACT.Exp, scale=-1.0).then_inc(s.ay, 1)
                act.wait_ge(s.sum, 1)
                for d in range(2):
                    dst = g.begc[:, d], g.esfx[:, d]
                    for j in range(2):
                        nc.scalar.activation(dst[j], ps[:, 2 * d + j].rearrange("p (n h) -> p n h", h=H),
                                             ACT.Exp).then_inc(s.ex, 1)
                nc.scalar.activation(acc[:], g.ab[:, :, 8:16], ACT.Sigmoid).then_inc(s.beta, 1)

            @block.vector
            def _(dve):
                own = Steps(dve, s.own)
                v = nc.vector
                dve.wait_ge(s.par, 32)
                own.done(v.tensor_tensor(x[:], g.ab[:, :, 0:8], par[:, 1:2].broadcast_to([P, NT, 8]), ALU.add))
                own.settle()
                own.done(v.scalar_tensor_tensor(y[:], x[:], -1.0, x[:], ALU.mult, ALU.max))
                own.done(v.tensor_scalar(x[:], x[:], 0.0, None, ALU.max))
                dve.wait_ge(s.ay, 1)
                own.settle()
                own.done(v.tensor_scalar(t[:], y[:], 2.0, None, ALU.add))
                own.settle()
                own.done(v.reciprocal(t[:], t[:]))
                own.settle()
                own.done(v.tensor_tensor(y[:], y[:], t[:], ALU.mult))
                own.settle()
                own.done(v.tensor_tensor(t[:], y[:], y[:], ALU.mult))
                terms = 8
                own.settle()
                own.done(v.tensor_scalar(acc[:], t[:], 2.0 / (2 * terms + 1), 2.0 / (2 * terms - 1), ALU.mult, ALU.add))
                for m in range(terms - 2, -1, -1):
                    own.settle()
                    own.done(v.tensor_tensor(acc[:], acc[:], t[:], ALU.mult))
                    own.settle()
                    own.done(v.tensor_scalar(acc[:], acc[:], 2.0 / (2 * m + 1), None, ALU.add))
                own.settle()
                own.done(v.tensor_tensor(acc[:], acc[:], y[:], ALU.mult))
                own.settle()
                own.done(v.tensor_tensor(x[:], x[:], acc[:], ALU.add))
                own.settle()
                dve.wait_ge(s.ea, 1)
                for d in range(2):
                    own.done(v.scalar_tensor_tensor(g.gd[:, d, 0:NT], x[:, :, d * H:(d + 1) * H], -1.0,
                                                    par[:, 0:1, d * H:(d + 1) * H].broadcast_to([P, NT, H]), ALU.mult, ALU.mult))
                own.settle()
                own.done(v.tensor_copy(g.gd[:, :, NT:POS], g.gd[:, :, 0:CT]))
                dve.wait_ge(s.beta, 1)
                for d in range(2):
                    own.done(v.tensor_copy(g.beta[:, d, 0:NT], acc[:, :, d * H:(d + 1) * H]))
                own.settle()
                own.done(v.tensor_copy(g.beta[:, :, NT:POS], g.beta[:, :, 0:CT]))
                own.settle()
                own.done(v.tensor_tensor(g.begc[:], g.begc[:], g.beta[:], ALU.mult))
                own.settle()

            @block.tensor
            def _(pe):
                pe.wait_ge(s.own, 27)
                for d in range(2):
                    for j in range(2):
                        last = nc.tensor.matmul(ps[:, 2 * d + j], g.dirt(d, j), g.gd[:, d].rearrange("p n h -> p (n h)"),
                                                start=True, stop=True)
                last.then_inc(s.sum, 1)


def delta_rule(nc, g):
    STEPS = NT
    W = H * P
    with ExitStack() as c:
        def two(name):
            return [sbuf(nc, c, f"{name}{d}", [P, H, P]) for d in range(2)]
        lq, lk, lkt, lvt = ([[sbuf(nc, c, f"{n}{d}{u}", [P, H, P]) for u in range(2)] for d in range(2)]
                            for n in ("lq", "lk", "lkt", "lvt"))
        gt, dg, dec, eg, mt, tm, um, xm, qk, qg, kbg, vb, kg, ub, wb, vn, st = map(two, (
            "gt", "dg", "dec", "eg", "mt", "tm", "um", "xm", "qk", "qg", "kbg", "vbd", "kgd", "ub", "wb", "vn", "st"))
        ob = [[sbuf(nc, c, f"ob{d}{u}", [P, H, P]) for u in range(2)] for d in range(2)]
        bank = [[psum(nc, c, f"dr{d}{b}", (P, H, P)) for b in "abcd"] for d in range(2)]
        names = "ld0 ld1 gt dg mat exp kk qkp mt mt1 qkv qk px vx pb vt uw wt ws vn op su sup oe st0 st1 pool z gt2".split()
        s = [sems(nc, c, f"dr{d}", " ".join(names)) for d in range(2)]

        def heads(mask):
            return mask[:, None, :].broadcast_to([P, H, P])

        with nc.Block() as block:
            def pos(d, n):
                return n if d == 0 else n * -1 + (POS - 1)

            def col(t, d, at):
                return t[:, d, bass.ds(at[d], 1)].rearrange("p a h -> p (a h)")[:, :, None].broadcast_to([P, H, P])

            @block.sync
            def _(sp):
                def load(d, at, u):
                    for src, dst in ((g.q_d, lq), (g.k_d, lk), (g.kt_d, lkt), (g.vt_d, lvt)):
                        sp.dma_start(dst[d][u][:], src[at]).then_inc((s[d].ld0, s[d].ld1)[u], 16)

                def store(d, n, at, u):
                    sp.wait_ge(s[d].oe, n + 1)
                    sp.dma_start(g.o_d[d, at], ob[d][u][:]).then_inc((s[d].st0, s[d].st1)[u], 16)
                for u in range(2):
                    for d in range(2):
                        load(d, pos(d, u), u)
                with nc.sync.Fori(0, STEPS // 2 - 1) as i:
                    for u in range(2):
                        for d in range(2):
                            here, ahead = nc.sync.snap(pos(d, 2 * i + u)), nc.sync.snap(pos(d, 2 * i + u + 2))
                            sp.wait_ge(s[d].su, 2 * i + u + 1)
                            load(d, ahead, u)
                            store(d, 2 * i + u, here, u)
                for u in range(2):
                    for d in range(2):
                        store(d, STEPS - 2 + u, pos(d, STEPS - 2 + u), u)
                for d in range(2):
                    sp.wait_ge(s[d].st0, 16 * STEPS // 2)
                    sp.wait_ge(s[d].st1, 16 * STEPS // 2)

            @block.gpsimd
            def _(pool):
                tt = nc.gpsimd.tensor_tensor
                for d in range(2):
                    nc.gpsimd.memset(st[d][:], 0.0).then_inc(s[d].z, 1)

                with nc.gpsimd.Fori(0, STEPS // 2) as i:
                    for u in range(2):
                        n = 2 * i + u
                        at = [nc.gpsimd.snap(pos(d, n)) for d in range(2)]
                        for d in range(2):
                            q = s[d]
                            pool.wait_ge(q.mat, n)
                            tt(dg[d][:], heads(g.ident), col(g.beta, d, at), ALU.mult).then_inc(q.dg, 1)
                        for d in range(2):
                            q = s[d]
                            pool.wait_ge((q.ld0, q.ld1)[u], 64 * i + 64)
                            pool.wait_ge(q.uw, n)
                            tt(kbg[d][:], lkt[d][u][:], col(g.begc, d, at), ALU.mult).then_inc(q.pool, 1)
                            tt(vb[d][:], lvt[d][u][:], col(g.beta, d, at), ALU.mult).then_inc(q.pool, 1)
                            pool.wait_ge(q.su, n)
                            tt(kg[d][:], lkt[d][u][:], col(g.esfx, d, at), ALU.mult).then_inc(q.pool, 1)
                            pool.wait_ge(q.op, n)
                            pool.wait_ge(q.exp, 2 * n + 2)
                            tt(qg[d][:], lq[d][u][:], eg[d][:], ALU.mult).then_inc(q.pool, 1)
                            pool.wait_ge(q.qkv, n + 1)
                            tt(qk[d][:], qk[d][:], heads(g.dirt(d, 0)), ALU.mult).then_inc(q.qk, 1)

            @block.scalar
            def _(act):
                def step(i, u):
                    n = 2 * i + u
                    for d in range(2):
                        q, (A, B, C_, D_) = s[d], bank[d]
                        act.wait_ge(q.mat, n + 1)
                        act.wait_ge(q.qkv, n)
                        nc.scalar.activation(dec[d][:], A[:], ACT.Exp).then_inc(q.exp, 1)
                        act.wait_ge(q.sup, n)
                        act.wait_ge(q.pool, 4 * n)
                        nc.scalar.activation(eg[d][:], B[:], ACT.Exp).then_inc(q.exp, 1)
                    for d in range(2):
                        q, (A, B, C_, D_) = s[d], bank[d]
                        act.wait_ge(q.uw, n + 1)
                        act.wait_ge(q.vn, n)
                        nc.scalar.activation(ub[d][:], D_[:], ACT.Copy).then_inc(q.wt, 1)
                        act.wait_ge(q.ws, n)
                        nc.scalar.activation(wb[d][:], A[:], ACT.Copy).then_inc(q.wt, 1)
                    for d in range(2):
                        q, (A, B, C_, D_) = s[d], bank[d]
                        act.wait_ge(q.op, n + 1)
                        act.wait_ge((q.st0, q.st1)[u], 16 * i)
                        nc.scalar.activation(ob[d][u][:], C_[:], ACT.Copy).then_inc(q.oe, 1)

                with nc.scalar.Fori(0, STEPS // 2) as i:
                    for u in range(2):
                        step(i, u)

            @block.tensor
            def _(pe):
                def each(out, lhs, rhs):
                    for h in range(H):
                        last = nc.tensor.matmul(out[:, h], lhs[:, h], g.ident if rhs is None else rhs[:, h], start=True, stop=True)
                    return last

                with nc.tensor.Fori(0, STEPS // 2) as i:
                    for u in range(2):
                        n = 2 * i + u
                        for d in range(2):
                            q, (A, B, C_, D_) = s[d], bank[d]
                            flat = gt[d][:].rearrange("p h i -> p (h i)")
                            pe.wait_ge(q.gt, n + 1)
                            pe.wait_ge(q.dg, n + 1)
                            pe.wait_ge(q.wt, 2 * n)
                            pe.wait_ge(q.vn, n)
                            pe.wait_ge(q.oe, n)
                            nc.tensor.matmul(A[:].rearrange("p h i -> p (h i)"), g.dirt(d, 1), flat, start=True, stop=True)
                            nc.tensor.matmul(B[:].rearrange("p h i -> p (h i)"), g.ones, flat, start=True, stop=True)
                            nc.tensor.matmul(C_[:].rearrange("p h i -> p (h i)"), g.dirt(d, 1),
                                             dg[d][:].rearrange("p h i -> p (h i)"), start=True, stop=True).then_inc(q.mat, 1)
                            pe.wait_ge((q.ld0, q.ld1)[u], 64 * i + 64)
                            pe.wait_ge(q.sup, n)
                            each(D_, lk[d][u], lk[d][u]).then_inc(q.kk, 1)
                        for d in range(2):
                            q, (A, B, C_, D_) = s[d], bank[d]
                            pe.wait_ge(q.exp, 2 * n + 2)
                            each(A, lk[d][u], lq[d][u]).then_inc(q.qkp, 1)
                        for d in range(2):
                            q, (A, B, C_, D_) = s[d], bank[d]
                            pe.wait_ge(q.mt, n + 1)
                            each(B, mt[d], None).then_inc(q.px, 1)
                        for lev in range(1, N_LEV):
                            for d in range(2):
                                q, (A, B, C_, D_) = s[d], bank[d]
                                pe.wait_ge(q.vt, N_LEV * n + lev)
                                if lev == 1:
                                    pe.wait_ge(q.qkv, n + 1)
                                each(A, mt[d], tm[d]).then_inc(q.px, 1)
                            for d in range(2):
                                q, (A, B, C_, D_) = s[d], bank[d]
                                pe.wait_ge(q.vx, (N_LEV - 1) * n + lev)
                                if lev < N_LEV - 1:
                                    each(B, um[d], xm[d])
                                each(C_, xm[d], um[d]).then_inc(q.pb, 1)
                        for d in range(2):
                            q, (A, B, C_, D_) = s[d], bank[d]
                            pe.wait_ge(q.vt, N_LEV * n + N_LEV)
                            pe.wait_ge(q.pool, 4 * n + 2)
                            each(D_, um[d], vb[d])
                            each(A, kbg[d], um[d]).then_inc(q.uw, 1)
                        for d in range(2):
                            q, (A, B, C_, D_) = s[d], bank[d]
                            pe.wait_ge(q.wt, 2 * n + 2)
                            pe.wait_ge(q.sup, n)
                            pe.wait_ge(q.z, 1)
                            each(B, wb[d], st[d]).then_inc(q.ws, 1)
                        for d in range(2):
                            q, (A, B, C_, D_) = s[d], bank[d]
                            pe.wait_ge(q.vn, n + 1)
                            pe.wait_ge(q.pool, 4 * n + 4)
                            pe.wait_ge(q.qk, n + 1)
                            for h in range(H):
                                nc.tensor.matmul(C_[:, h], st[d][:, h], qg[d][:, h], start=True, stop=False)
                                last = nc.tensor.matmul(C_[:, h], vn[d][:, h], qk[d][:, h], start=False, stop=True)
                            last.then_inc(q.op, 1)
                            each(D_, kg[d], vn[d]).then_inc(q.su, 1)

            @block.vector
            def _(dve):
                v = nc.vector
                with nc.vector.Fori(0, STEPS // 2) as i:
                    for u in range(2):
                        n = 2 * i + u
                        at = [nc.vector.snap(pos(d, n)) for d in range(2)]
                        for d in range(2):
                            q = s[d]
                            dve.wait_ge(q.mat, n)
                            v.tensor_tensor(gt[d][:], heads(g.dirt(d, 0)), col(g.gd, d, at), ALU.mult).then_inc(q.gt, 1)
                        for d in range(2):
                            q, (A, B, C_, D_) = s[d], bank[d]
                            dve.wait_ge(q.exp, 2 * n + 2)
                            dve.wait_ge(q.px, N_LEV * n)
                            v.tensor_tensor(mt[d][:], dec[d][:], C_[:], ALU.mult).then_inc(q.mt1, 1)
                            dve.wait_ge(q.mt1, n + 1)
                            dve.wait_ge(q.kk, n + 1)
                            v.tensor_tensor(mt[d][:], mt[d][:], D_[:], ALU.mult).then_inc(q.mt, 1)
                        for d in range(2):
                            q, (A, B, C_, D_) = s[d], bank[d]
                            dve.wait_ge(q.qkp, n + 1)
                            dve.wait_ge(q.op, n)
                            v.tensor_tensor(qk[d][:], A[:], dec[d][:], ALU.mult).then_inc(q.qkv, 1)
                        for d in range(2):
                            q, (A, B, C_, D_) = s[d], bank[d]
                            dve.wait_ge(q.uw, n)
                            dve.wait_ge(q.mt, n + 1)
                            own = Steps(dve, q.gt2, 2 * n)
                            own.done(v.tensor_tensor(um[d][:], mt[d][:], heads(g.level(1 - d, 0)), ALU.mult))
                            dve.wait_ge(q.px, N_LEV * n + 1)
                            own.done(v.tensor_tensor(tm[d][:], B[:], heads(g.level(d, 0)), ALU.mult))
                            own.settle()
                            v.scalar_tensor_tensor(um[d][:], um[d][:], -1.0, heads(g.ident), ALU.mult, ALU.add)
                            v.scalar_tensor_tensor(tm[d][:], tm[d][:], -1.0, heads(g.ident), ALU.mult, ALU.add).then_inc(q.vt, 1)
                        for lev in range(1, N_LEV):
                            for d in range(2):
                                q, (A, B, C_, D_) = s[d], bank[d]
                                dve.wait_ge(q.px, N_LEV * n + lev + 1)
                                v.tensor_tensor(xm[d][:], A[:], heads(g.level(d, lev)), ALU.mult).then_inc(q.vx, 1)
                            for d in range(2):
                                q, (A, B, C_, D_) = s[d], bank[d]
                                dve.wait_ge(q.pb, (N_LEV - 1) * n + lev)
                                if lev < N_LEV - 1:
                                    v.tensor_tensor(tm[d][:], tm[d][:], B[:], ALU.subtract)
                                v.tensor_tensor(um[d][:], um[d][:], C_[:], ALU.subtract).then_inc(q.vt, 1)
                        for d in range(2):
                            q, (A, B, C_, D_) = s[d], bank[d]
                            dve.wait_ge(q.ws, n + 1)
                            dve.wait_ge(q.su, n)
                            v.tensor_tensor(vn[d][:], ub[d][:], B[:], ALU.subtract).then_inc(q.vn, 1)
                        for d in range(2):
                            q, (A, B, C_, D_) = s[d], bank[d]
                            last_tok = P - 1 if d == 0 else 0
                            dve.wait_ge(q.su, n + 1)
                            for h in range(H):
                                last = v.scalar_tensor_tensor(st[d][:, h], st[d][:, h], eg[d][:, h, last_tok:last_tok + 1],
                                                              D_[:, h], ALU.mult, ALU.add)
                            last.then_inc(q.sup, 1)


def wait(eng, sem, value):
    if not isinstance(value, int) or value > 0:
        eng.wait_ge(sem, value)


def attention(nc, g):
    UNITS = ROWS * HP
    LOC = WR * GRID
    KEYS = LOC + CTX
    KT = KEYS // P
    FREE = g.hT.rearrange("p k t -> p (k t)")
    v0 = FREE[:, 0:NT * 2 * P].rearrange("p (n c) -> p n c", c=2 * P)
    v1 = FREE[:, NT * 2 * P:(NT + LT - 1) * 2 * P].rearrange("p (n c) -> p n c", c=2 * P)
    first_in, last_in = WR // 4, (ROWS - WR // 2) // 2

    def place(i, k):
        odd, hp = k // 2, k % 2
        r = 2 * i + odd
        if isinstance(i, int):
            rs = min(max(r - WR // 2, 0), ROWS - WR)
            shift = r - rs
            vi = (rs - rs % 2) // 2
            return r, rs, vi, rs % 2, WR - 1 - shift
        return r, r - WR // 2, i - WR // 4, odd, WR - 1 - WR // 2

    def units(eng, body):
        for i in range(first_in + 1):
            for k in range(4):
                body(i, k)
        with eng.Fori(first_in + 1, last_in) as i:
            for k in range(4):
                body(i, k)
        for i in range(last_in, ROWS // 2):
            for k in range(4):
                body(i, k)

    def early(i, k, n):
        return isinstance(i, int) and 4 * i + k < n

    def back(i, k, n):
        return (i, k - n) if k >= n else (i - 1, k - n + 4)

    with ExitStack() as c:
        rpad = sbuf(nc, c, "rpad", [H * 15, 127])
        bt = sbuf(nc, c, "bt", [P, HP, 15, GRID])
        qb = sbuf(nc, c, "qb", [P, 2, 2 * GRID])
        sb = sbuf(nc, c, "scores", [P, 2, KEYS])
        pb = sbuf(nc, c, "probs", [P, 2, KEYS])
        pt = sbuf(nc, c, "probs_t", [P, 2, KT, P])
        mx = sbuf(nc, c, "mx", [P, 2, 4])
        ob = sbuf(nc, c, "ao", [P, 2, P])
        oc = sbuf(nc, c, "aoT", [P, 2, HP, GRID])
        loc = psum(nc, c, "loc_ps", (P, 2, 512))
        cx = psum(nc, c, "cx_ps", (P, 2, 512))
        tp = psum(nc, c, "tp_ps", (P, 2, 512))
        po = psum(nc, c, "po_ps")
        pot = psum(nc, c, "pot_ps")
        s = sems(nc, c, "at", "v pad z rp sk bt0 qb sc cx add mx nm ex rc tp ptd pta o oe ot ote st0 st1")
        s_st = [s.st0, s.st1]
        with nc.Block() as block:
            @block.sync
            def _(sp):
                sp.dma_start(v0, g.v_d.rearrange("(n p) c -> p n c", p=P)).then_inc(s.v, 16)
                sp.dma_start(v1, g.v_d[CTX + GRID:T - GRID].rearrange("(n p) c -> p n c", p=P)).then_inc(s.v, 16)
                sp.wait_ge(s.z, 1)
                sp.dma_start(rpad[:, 48:79], g.rpb).then_inc(s.rp, 16)
                sp.wait_ge(s.rp, 16)
                sp.dma_start(g.skew_d, rpad[:, None, :].broadcast_to([H * 15, GRID, 127])).then_inc(s.sk, 16)
                sp.wait_ge(s.sk, 16)
                for h in range(H):
                    src = g.skew_d[h * 15:(h + 1) * 15].rearrange("r j c -> r (j c)")
                    src = src[:, 63:63 + GRID * 126].rearrange("r (j c) -> j r c", c=126)[:, :, 0:GRID]
                    half = h % 2
                    sp.dma_start(bt[half * GRID:(half + 1) * GRID, h // 2], src).then_inc(s.bt0, 16)

                dst = g.oc_d.rearrange("(q p) (r t) -> p r q t", q=HP, t=GRID)

                def store(i, odd):
                    r = 2 * i + odd
                    sp.wait_ge(s.ote, 2 * (4 * i + 2 * odd + 2))
                    sp.dma_start(dst[:, bass.ds(r, 1)].rearrange("p r q t -> p (r q) t"), oc[:, odd]).then_inc(s_st[odd], 16)
                with nc.sync.Fori(0, ROWS // 2) as i:
                    for odd in range(2):
                        store(i, odd)
                for sem in s_st:
                    sp.wait_ge(sem, 8 * ROWS)

            @block.gpsimd
            def _(pool):
                nc.gpsimd.memset(rpad[:], 0.0).then_inc(s.z, 1)

                def body(i, k):
                    U = 4 * i + k
                    r = place(i, k)[0]
                    at = r * GRID if isinstance(i, int) else nc.gpsimd.snap(r * GRID)
                    wait(pool, s.sc, U - 1)
                    nc.gpsimd.tensor_tensor(qb[:, k % 2].rearrange("p (a t) -> p a t", a=2),
                                            g.qn[:, k % 2, bass.ds(at, GRID)][:, None, :].broadcast_to([P, 2, GRID]),
                                            g.blk.rearrange("p (a t) -> p a t", a=2), ALU.mult).then_inc(s.qb, 1)
                units(nc.gpsimd, body)

            @block.tensor
            def _(pe):
                def scores(i, k):
                    U, u = 4 * i + k, k % 2
                    _, rs, _, _, _ = place(i, k)
                    pe.wait_ge(s.qb, U + 1)
                    wait(pe, s.add, U - 1)
                    wait(pe, s.cx, U - 1)
                    nc.tensor.matmul(loc[:, u, 0:LOC], qb[:, u], g.kn[:, k % 2, bass.ds(CTX + rs * GRID, LOC)], start=True, stop=True)
                    nc.tensor.matmul(cx[:, u, 0:CTX], qb[:, u], g.kn[:, k % 2, 0:CTX], start=True, stop=True).then_inc(s.sc, 1)

                def turn(i, k):
                    U, u = 4 * i + k, k % 2
                    pe.wait_ge(s.ex, U + 1)
                    for b in range(2):
                        wait(pe, (s.ptd, s.pta)[b], U)
                        for j in range(KT // 2):
                            n = b * (KT // 2) + j
                            last = nc.tensor.transpose(tp[:, b, j * P:(j + 1) * P], pb[:, u, n * P:(n + 1) * P], g.ident)
                        last.then_inc(s.tp, 1)

                def values(i, k):
                    U, u, hp = 4 * i + k, k % 2, k % 2
                    _, _, vi, shifted, _ = place(i, k)
                    pe.wait_ge(s.ptd, U + 1)
                    pe.wait_ge(s.pta, U + 1)
                    wait(pe, s.oe, U)
                    cols = slice(hp * P, (hp + 1) * P)
                    for n in range(KT):
                        if n < KT - CT:
                            v = v1[:, bass.ds(vi + n, 1), cols] if shifted else v0[:, bass.ds(vi + n + CT, 1), cols]
                            v = v.rearrange("p a c -> p (a c)")
                        else:
                            v = v0[:, n - (KT - CT), cols]
                        last = nc.tensor.matmul(po[:, 0:P], pt[:, u, n], v, start=(n == 0), stop=(n == KT - 1))
                    last.then_inc(s.o, 1)

                def turn_out(i, k):
                    U, u = 4 * i + k, k % 2
                    pe.wait_ge(s.oe, U + 1)
                    wait(pe, s.ote, 2 * U)
                    nc.tensor.transpose(pot[:, 0:P], ob[:, u], g.ident).then_inc(s.ot, 1)

                def body(i, k):
                    scores(i, k)
                    if not early(i, k, 1):
                        turn(*back(i, k, 1))
                    if not early(i, k, 2):
                        turn_out(*back(i, k, 2))
                    if not early(i, k, 1):
                        values(*back(i, k, 1))
                pe.wait_ge(s.v, 32)
                units(nc.tensor, body)
                end = ROWS // 2 - 1
                turn(end, 3)
                turn_out(end, 2)
                values(end, 3)
                turn_out(end, 3)

            @block.scalar
            def _(act):
                def context(i, k):
                    U, u = 4 * i + k, k % 2
                    act.wait_ge(s.sc, U + 1)
                    wait(act, s.ex, U - 1)
                    nc.scalar.activation(sb[:, u, LOC:KEYS], cx[:, u, 0:CTX], ACT.Copy).then_inc(s.cx, 1)

                def exps(i, k):
                    U, u = 4 * i + k, k % 2
                    act.wait_ge(s.nm, U + 1)
                    wait(act, s.tp, 2 * (U - 1))
                    wait(act, s.rc, U - 1)
                    nc.scalar.activation(pb[:, u], sb[:, u], ACT.Exp, bias=mx[:, u, 1:2], accum_out=mx[:, u, 2:3]).then_inc(s.ex, 1)

                def copy_pt(i, k):
                    U, u = 4 * i + k, k % 2
                    act.wait_ge(s.tp, 2 * U + 2)
                    wait(act, s.o, U - 1)
                    nc.scalar.activation(pt[:, u, KT // 2:KT], tp[:, 1, 0:KT // 2 * P].rearrange("p (n c) -> p n c", c=P), ACT.Copy).then_inc(s.pta, 1)

                def out(i, k):
                    U, u = 4 * i + k, k % 2
                    act.wait_ge(s.o, U + 1)
                    act.wait_ge(s.rc, U + 1)
                    wait(act, s.ot, U - 1)
                    nc.scalar.activation(ob[:, u], po[:, 0:P], ACT.Copy, scale=mx[:, u, 3:4]).then_inc(s.oe, 1)

                def out_t(i, k):
                    U, odd, hp = 4 * i + k, k // 2, k % 2
                    act.wait_ge(s.ot, U + 1)
                    wait(act, s_st[odd], 16 * i)
                    for a in range(2):
                        half = slice(a * DH, (a + 1) * DH)
                        nc.scalar.activation(oc[half, odd, hp], pot[half, half], ACT.Copy).then_inc(s.ote, 1)

                def body(i, k):
                    context(i, k)
                    if not early(i, k, 1):
                        copy_pt(*back(i, k, 1))
                    if not early(i, k, 2):
                        out_t(*back(i, k, 2))
                    exps(i, k)
                    if not early(i, k, 1):
                        out(*back(i, k, 1))
                units(nc.scalar, body)
                end = ROWS // 2 - 1
                copy_pt(end, 3)
                out_t(end, 2)
                out(end, 3)
                out_t(end, 3)

            @block.vector
            def _(dve):
                v = nc.vector

                def softmax(i, k):
                    U, u = 4 * i + k, k % 2
                    dr = place(i, k)[4]
                    dve.wait_ge(s.sc, U + 1)
                    wait(dve, s.ex, U - 1)
                    v.tensor_tensor(sb[:, u, 0:LOC], loc[:, u, 0:LOC], bt[:, k % 2, dr:dr + WR].rearrange("p r c -> p (r c)"),
                                    ALU.add).then_inc(s.add, 1)
                    dve.wait_ge(s.add, U + 1)
                    dve.wait_ge(s.cx, U + 1)
                    v.reduce_max(mx[:, u, 0:1], sb[:, u], AX_X).then_inc(s.mx, 1)
                    dve.wait_ge(s.mx, U + 1)
                    v.tensor_scalar(mx[:, u, 1:2], mx[:, u, 0:1], -1.0, None, ALU.mult).then_inc(s.nm, 1)

                def rest(i, k):
                    U, u = 4 * i + k, k % 2
                    dve.wait_ge(s.ex, U + 1)
                    wait(dve, s.oe, U - 1)
                    v.reciprocal(mx[:, u, 3:4], mx[:, u, 2:3]).then_inc(s.rc, 1)
                    dve.wait_ge(s.tp, 2 * U + 1)
                    wait(dve, s.o, U - 1)
                    v.tensor_copy(pt[:, u, 0:KT // 2], tp[:, 0, 0:KT // 2 * P].rearrange("p (n c) -> p n c", c=P)).then_inc(s.ptd, 1)

                def body(i, k):
                    softmax(i, k)
                    if not early(i, k, 1):
                        rest(*back(i, k, 1))
                dve.wait_ge(s.bt0, 64)
                for hp in range(HP):
                    v.tensor_tensor(bt[:, hp], bt[:, hp], g.window[:, None, :].broadcast_to([P, 15, GRID]), ALU.add).then_inc(s.pad, 1)
                dve.wait_ge(s.pad, 2)
                units(nc.vector, body)
                rest(ROWS // 2 - 1, 3)


def fourier(nc, g):
    N1, N2 = P, SEQ // P
    LO = P // N2
    HI = N1 // LO
    FREE = g.hT.rearrange("p k t -> p (k t)")
    ab = FREE[:, 0:2 * N2 * FN].rearrange("p (s n c) -> p s n c", s=2, n=N2)
    zin = FREE[:, 2 * N2 * FN:4 * N2 * FN].rearrange("p (s h c) -> p s h c", s=2, h=HI)
    CH = N2 // 2
    with ExitStack() as c:
        ft = sbuf(nc, c, "ft", [P, F_W])
        zc = sbuf(nc, c, "zc", [P, 2, 4, 512])
        zs = sbuf(nc, c, "zs", [P, 2, 2, 512])
        y = sbuf(nc, c, "yf", [P, 2, 512])
        ybt = sbuf(nc, c, "ybt", [P, 2, SEQ])
        pa = psum(nc, c, "fa_ps", (P, 2, 512))
        pz = psum(nc, c, "fz_ps", (P, 2, 2, 512))
        pq = psum(nc, c, "fq_ps", (P, 2, 512))
        s = sems(nc, c, "fo", "ft pa ae pz m zz zst0 zst1 re py ye pq qe st")
        c4 = ft[:, F_C4:F_C4 + FN]
        dft = [ft[:, F_N1 + j * P:F_N1 + (j + 1) * P] for j in range(3)]
        twc, tws = (ft[:, F_TW + j * N2:F_TW + (j + 1) * N2] for j in range(2))
        k2c, k2s = (ft[:, F_K2 + j * P:F_K2 + (j + 1) * P] for j in range(2))
        with nc.Block() as block:
            @block.sync
            def _(sp):
                sp.dma_start(ft[:], g.ftab).then_inc(s.ft, 16)
                for q in range(CH):
                    sp.wait_ge(s.zz, 2 * q + 2)
                    sp.dma_start(g.z2_d[:, :, 2 * q:2 * q + 2].rearrange("s k n c -> k s (n c)"), zs[:, q % 2]).then_inc((s.zst0, s.zst1)[q % 2], 16)
                sp.wait_ge(s.zst0, 16 * CH // 2)
                sp.wait_ge(s.zst1, 16 * CH // 2)
                for n in range(N2):
                    for j in range(2):
                        sp.dma_start(zin[n * LO:(n + 1) * LO, j], g.z2_d[j, :, n].rearrange("(h l) c -> l h c", l=LO)).then_inc(s.re, 16)
                sp.wait_ge(s.qe, 2 * HI // 2)
                sp.dma_start(g.yb_d.rearrange("(a p) t -> p a t", p=P), ybt[:]).then_inc(s.st, 16)
                sp.wait_ge(s.st, 16)

            @block.tensor
            def _(pe):
                pe.wait_ge(s.ft, 16)
                for n in range(N2):
                    wait(pe, s.ae, n - 1)
                    for cc in range(2):
                        last = nc.tensor.matmul(pa[:, n % 2, cc * FN:(cc + 1) * FN], g.uT[:, cc, n:SEQ:N2], c4, start=True, stop=True)
                    last.then_inc(s.pa, 1)
                pe.wait_ge(s.ae, N2)
                for q in range(CH):
                    wait(pe, s.m, 4 * (q - 1))
                    a, b = (ab[:, j, 2 * q:2 * q + 2].rearrange("p n c -> p (n c)") for j in range(2))
                    re, im = pz[:, q % 2, 0], pz[:, q % 2, 1]
                    nc.tensor.matmul(re, dft[0], a, start=True, stop=False)
                    nc.tensor.matmul(re, dft[2], b, start=False, stop=True)
                    nc.tensor.matmul(im, dft[0], b, start=True, stop=False)
                    nc.tensor.matmul(im, dft[1], a, start=False, stop=True).then_inc(s.pz, 1)
                pe.wait_ge(s.re, 16 * 2 * N2)
                for q in range(HI // 2 + 1):
                    if q < HI // 2:
                        wait(pe, s.ye, q - 1)
                        for j in range(2):
                            last = nc.tensor.matmul(pa[:, q % 2], (k2c, k2s)[j], zin[:, j, 2 * q:2 * q + 2].rearrange("p h c -> p (h c)"),
                                                    start=(j == 0), stop=(j == 1))
                        last.then_inc(s.py, 1)
                    if q:
                        r = q - 1
                        pe.wait_ge(s.ye, r + 1)
                        wait(pe, s.qe, 2 * (r - 1))
                        for j in range(4):
                            last = nc.tensor.transpose(pq[:, r % 2, j * P:(j + 1) * P], y[:, r % 2, j * P:(j + 1) * P], g.ident)
                        last.then_inc(s.pq, 1)

            @block.scalar
            def _(act):
                for n in range(N2):
                    act.wait_ge(s.pa, n + 1)
                    nc.scalar.activation(ab[:, :, n].rearrange("p s (a x) -> p a s x", a=2),
                                         pa[:, n % 2].rearrange("p (a s x) -> p a s x", a=2, s=2), ACT.Copy).then_inc(s.ae, 1)
                for q in range(HI // 2):
                    act.wait_ge(s.py, q + 1)
                    wait(act, s.pq, q - 1)
                    nc.scalar.activation(y[:, q % 2], pa[:, q % 2], ACT.Copy).then_inc(s.ye, 1)

            @block.vector
            def _(dve):
                v = nc.vector
                for q in range(CH):
                    u = q % 2
                    dve.wait_ge(s.pz, q + 1)
                    wait(dve, s.zz, 2 * (q - 1))
                    tw = [t[:, 2 * q:2 * q + 2, None].broadcast_to([P, 2, FN]) for t in (twc, tws)]
                    for j, (part, t) in enumerate(((0, 0), (1, 1), (1, 0), (0, 1))):
                        v.tensor_tensor(zc[:, u, j].rearrange("p (n c) -> p n c", n=2), pz[:, u, part].rearrange("p (n c) -> p n c", n=2),
                                        tw[t], ALU.mult).then_inc(s.m, 1)
                for q in range(HI // 2):
                    dve.wait_ge(s.pq, q + 1)
                    for j in range(2):
                        k1 = (2 * q + j) * LO
                        out = ybt[:].rearrange("p a (k t) -> p a k t", t=N1)[:, :, :, k1:k1 + LO]
                        v.tensor_copy(out, pq[:, q % 2, j * FN:(j + 1) * FN].rearrange("p (a k t) -> p a k t", a=2, t=LO)).then_inc(s.qe, 1)

            @block.gpsimd
            def _(pool):
                for q in range(CH):
                    u = q % 2
                    pool.wait_ge(s.m, 4 * q + 4)
                    wait(pool, (s.zst0, s.zst1)[u], 16 * (q // 2))
                    nc.gpsimd.tensor_tensor(zs[:, u, 0], zc[:, u, 0], zc[:, u, 1], ALU.subtract).then_inc(s.zz, 1)
                    nc.gpsimd.tensor_tensor(zs[:, u, 1], zc[:, u, 2], zc[:, u, 3], ALU.add).then_inc(s.zz, 1)


def merge(nc, g):
    NBK = SEQ // 512
    BT = 512 // P
    NBR = 3
    BRANCH = [(0, H), (H, H + 2), (H + 2, KD)]
    with ExitStack() as c:
        hb = sbuf(nc, c, "hb", [P, KD, 512])
        of = sbuf(nc, c, "of", [P, 2, BT * H * P])
        zt = sbuf(nc, c, "zt", [P, H, 512])
        ob = sbuf(nc, c, "obr", [P, KD, 512])
        wg = sbuf(nc, c, "wg", [P, 2, NBR, KD, P])
        wb = sbuf(nc, c, "wbr", [P, 2, KD, P])
        wo = sbuf(nc, c, "wo", [P, KD, D])
        yT = sbuf(nc, c, "yT", [P, KD, 512])
        rows = sbuf(nc, c, "rowsm", [P, 3, D])
        gnw = sbuf(nc, c, "gnw", [P, 1])
        wr = sbuf(nc, c, "wr", [P, KD, E])
        sg = sbuf(nc, c, "sg", [P, NBR, 512])
        pr = sbuf(nc, c, "prm", [P, NBR, 512])
        xt = sbuf(nc, c, "xt", [P, 2, D])
        h2 = sbuf(nc, c, "h2", [P, 2, D])
        h2T = sbuf(nc, c, "h2T", [P, KD, P])
        st = sbuf(nc, c, "stat", [P, 2])
        pg = [psum(nc, c, f"pg{n}") for n in range(NBR)]
        pbr = [psum(nc, c, f"pbr{n}") for n in range(NBR)]
        po = [psum(nc, c, f"pom{n}") for n in range(2)]
        s = sems(nc, c, "me", "cst ldo ldh w0 w1 osum sq sum root rec oa gate sig br prod add y out x0 x1 half x1d ssq sr h2a h2 tr trc lg lgc st0 st1 held")
        s_w, s_x, s_st = [s.w0, s.w1], [s.x0, s.x1], [s.st0, s.st1]
        scans = [of[:, d].rearrange("p (b h i) -> p b h i", b=BT, h=H) for d in range(2)]
        squares, roots = (of[:, d].rearrange("p (h t) -> p h t", h=H) for d in (1, 0))
        SIG0, PROD0, BR0, HALF0 = NBR, NBR, 2 * NBR, 2

        with nc.Block() as block:
            @block.sync
            def _(sp):
                sp.dma_start(rows[:], g.rows_d[:, 0:3]).then_inc(s.cst, 16)
                sp.dma_start(gnw[:], g.gdn_norm).then_inc(s.cst, 16)
                sp.dma_start(wr[:], g.w_router).then_inc(s.cst, 16)
                sp.dma_start(wo[:], g.w_out).then_inc(s.cst, 16)
                with nc.sync.Fori(0, NBK) as b:
                    with nc.sync.Fori(0, KD // 2) as jj:
                        for u in range(2):
                            n = b * KD + jj * 2 + u
                            j = nc.sync.snap(jj * 2 + u)
                            sp.wait_ge(s.br, NBR * n + NBR)
                            sp.dma_start(wg[:, u], g.w_gates[j]).then_inc(s_w[u], 16)
                            sp.dma_start(wb[:, u], g.w_br[j]).then_inc(s_w[u], 16)

            @block.gpsimd
            def _(pool):
                def load_x(t, tt):
                    pool.dma_start(xt[:, tt % 2], g.x[bass.ds(t * P, P)]).then_inc(s_x[tt % 2], 16)

                with nc.gpsimd.Fori(0, NBK) as b:
                    t0 = nc.gpsimd.snap(b * 512)
                    pos = nc.gpsimd.snap(b * BT + CT)
                    pool.wait_ge(s.br, NBR * KD * b + BR0)
                    hold(pool, s.held)
                    for d in range(2):
                        pool.dma_start(scans[d], g.o_d[d, bass.ds(pos, BT)].rearrange("n p h c -> p n h c")).then_inc(s.ldo, 16)
                    pool.dma_start(zt[:], g.z_d[:, :, bass.ds(t0, 512)].rearrange("h p t -> p h t")).then_inc(s.ldo, 16)
                    pool.dma_start(ob[:, H:H + 2], g.yb_d[:, bass.ds(t0, 512)].rearrange("(a p) t -> p a t", p=P)).then_inc(s.ldh, 16)
                    pool.dma_start(ob[:, H + 2:KD], g.oc_d[:, bass.ds(t0, 512)].rearrange("(a p) t -> p a t", p=P)).then_inc(s.ldh, 16)
                    pool.dma_start(hb[:], g.h_d[:, :, bass.ds(t0 + CTX, 512)]).then_inc(s.ldh, 16)
                    for tt in range(2):
                        pool.wait_ge(s_st[tt], 2 * 32 * b)
                        hold(pool, s.held)
                        load_x(b * BT + tt, tt)
                    for tt in range(BT):
                        u = tt % 2
                        at = nc.gpsimd.snap((b * BT + tt) * P)
                        pool.wait_ge(s.h2, BT * b + tt + 1)
                        hold(pool, s.held)
                        pool.dma_start(g.out[bass.ds(at, P)], xt[:, u]).then_inc(s_st[u], 16)
                        pool.dma_start(g.h2_d[bass.ds(at, P)], h2[:, u]).then_inc(s_st[u], 16)
                        if tt < 2:
                            pool.wait_ge(s_st[u], 2 * 32 * b + 32)
                            hold(pool, s.held)
                            load_x(b * BT + tt + 2, tt)
                for u in range(2):
                    pool.wait_ge(s_st[u], 32 * BT // 2 * NBK)

            @block.tensor
            def _(pe):
                pe.sem_inc(s.br, BR0)

                def project_out(b, tt):
                    for half in range(2):
                        pe.wait_ge(s.half, 2 * (BT * b + tt) + half + 1)
                        for k in range(KD):
                            last = nc.tensor.matmul(po[half][:], yT[:, k, tt * P:(tt + 1) * P], wo[:, k, half * 512:(half + 1) * 512],
                                                    start=(k == 0), stop=(k == KD - 1))
                        last.then_inc(s.out, 1)

                def route(b, tt):
                    t = BT * b + tt
                    pe.wait_ge(s.h2, t + 1)
                    if tt == 0:
                        pe.wait_ge(s.sig, NBR * KD * (b + 1) + SIG0)
                    for q in range(2):
                        pe.wait_ge(s.trc, 2 * t)
                        for j in range(4):
                            last = nc.tensor.transpose(pg[q][:, j * P:(j + 1) * P], h2[:, tt % 2, (4 * q + j) * P:(4 * q + j + 1) * P], g.ident)
                        last.then_inc(s.tr, 1)
                    pe.wait_ge(s.trc, 2 * t + 2)
                    pe.wait_ge(s.lgc, t)
                    for k in range(KD):
                        last = nc.tensor.matmul(pg[2][:, 0:E], h2T[:, k], wr[:, k], start=(k == 0), stop=(k == KD - 1))
                    last.then_inc(s.lg, 1)

                pe.wait_ge(s.cst, 64)
                with nc.tensor.Fori(0, NBK) as b:
                    pe.wait_ge(s.trc, 2 * BT * b)
                    pe.wait_ge(s.lgc, BT * b)
                    pe.wait_ge(s.prod, NBR * KD * b + PROD0)
                    pe.wait_ge(s.sq, b + 1)
                    for h in range(H):
                        bank = (pg + pbr)[h]
                        nc.tensor.matmul(bank[:], g.ones, squares[:, h], start=True, stop=True).then_inc(s.sum, 1)
                    pe.wait_ge(s.root, H * (b + 1))
                    pe.wait_ge(s.oa, b + 1)
                    pe.wait_ge(s.ldh, 48 * b + 48)
                    hold(pe, s.held)
                    with nc.tensor.Fori(0, KD // 2) as jj:
                        for u in range(2):
                            n = b * KD + jj * 2 + u
                            pe.wait_ge(s_w[u], 32 * (b * (KD // 2) + jj) + 32)
                            for br in range(NBR):
                                pe.wait_ge(s.sig, NBR * n + br + 1)
                                for k in range(KD):
                                    last = nc.tensor.matmul(pg[br][:], wg[:, u, br, k], hb[:, k], start=(k == 0), stop=(k == KD - 1))
                                last.then_inc(s.gate, 1)
                                pe.wait_ge(s.prod, NBR * n + br + 1)
                                k0, k1 = BRANCH[br]
                                for k in range(k0, k1):
                                    last = nc.tensor.matmul(pbr[br][:], wb[:, u, k], ob[:, k], start=(k == k0), stop=(k == k1 - 1))
                                last.then_inc(s.br, 1)
                    pe.wait_ge(s.y, KD * (b + 1))
                    project_out(b, 0)
                    for tt in range(1, BT):
                        project_out(b, tt)
                        route(b, tt - 1)
                    route(b, BT - 1)

            @block.scalar
            def _(act):
                act.sem_inc(s.sig, SIG0)

                def spread(b, tt):
                    t = BT * b + tt
                    act.wait_ge(s.x1d, t + 1)
                    nc.scalar.activation(h2[:, tt % 2], xt[:, tt % 2], ACT.Square, accum_out=st[:, 0:1]).then_inc(s.ssq, 1)
                    act.wait_ge(s.ssq, t + 1)
                    act.wait_ge(s.h2, t)
                    nc.scalar.activation(st[:, 1:2], st[:, 0:1], ACT.Sqrt, bias=g.eps[:, 0:1], scale=1.0 / D).then_inc(s.sr, 1)

                def route(b, tt):
                    t = BT * b + tt
                    act.wait_ge(s.lg, t)
                    for q in range(2):
                        act.wait_ge(s.tr, 2 * t + q + 1)
                        nc.scalar.activation(h2T[:, 4 * q:4 * q + 4], pg[q][:].rearrange("p (k t) -> p k t", k=4), ACT.Copy).then_inc(s.trc, 1)
                    at = nc.scalar.snap(t + 0)
                    act.wait_ge(s.lg, t + 1)
                    nc.scalar.activation(g.logits[:, bass.ds(at, 1)].rearrange("p a e -> p (a e)"), pg[2][:, 0:E], ACT.Copy).then_inc(s.lgc, 1)

                with nc.scalar.Fori(0, NBK) as b:
                    act.wait_ge(s.osum, b + 1)
                    nc.scalar.activation(squares, ob[:, 0:H], ACT.Square).then_inc(s.sq, 1)
                    for h in range(H):
                        act.wait_ge(s.sum, H * b + h + 1)
                        nc.scalar.activation(roots[:, h], (pg + pbr)[h][:], ACT.Sqrt, bias=g.eps[:, 0:1], scale=1.0 / DK).then_inc(s.root, 1)
                    with nc.scalar.Fori(0, KD) as j:
                        n = b * KD + j
                        for br in range(NBR):
                            act.wait_ge(s.gate, NBR * n + br + 1)
                            act.wait_ge(s.prod, NBR * n + br + 1)
                            nc.scalar.activation(sg[:, br], pg[br][:], ACT.Sigmoid).then_inc(s.sig, 1)
                    spread(b, 0)
                    for tt in range(1, BT):
                        spread(b, tt)
                        route(b, tt - 1)
                    route(b, BT - 1)

            @block.vector
            def _(dve):
                v = nc.vector
                dve.sem_inc(s.prod, PROD0)
                dve.sem_inc(s.half, HALF0)
                dve.wait_ge(s.cst, 64)
                with nc.vector.Fori(0, NBK) as b:
                    dve.wait_ge(s.ldo, 48 * b + 48)
                    dve.wait_ge(s.br, NBR * KD * b + BR0)
                    da = ob[:, 0:H]
                    v.tensor_tensor(da.rearrange("p h (b i) -> p b h i", i=P), scans[0], scans[1], ALU.add).then_inc(s.osum, 1)
                    dve.wait_ge(s.root, H * (b + 1))
                    v.reciprocal(roots, roots).then_inc(s.rec, 1)
                    dve.wait_ge(s.rec, 2 * b + 1)
                    v.scalar_tensor_tensor(da, da, gnw[:, 0:1], roots, ALU.mult, ALU.mult).then_inc(s.rec, 1)
                    dve.wait_ge(s.rec, 2 * b + 2)
                    v.tensor_tensor(da, da, zt[:], ALU.mult).then_inc(s.oa, 1)
                    dve.wait_ge(s.out, 2 * BT * b)
                    hold(dve, s.held)
                    with nc.vector.Fori(0, KD) as j:
                        n = b * KD + j
                        at = nc.vector.snap(j + 0)
                        dve.wait_ge(s.y, n)
                        for br in range(NBR):
                            dve.wait_ge(s.sig, NBR * n + br + 1 + SIG0)
                            dve.wait_ge(s.br, NBR * n + br + 1 + BR0)
                            v.tensor_tensor(pr[:, br], sg[:, br], pbr[br][:], ALU.mult).then_inc(s.prod, 1)
                        dve.wait_ge(s.prod, NBR * n + NBR + PROD0)
                        v.tensor_tensor(pr[:, 0], pr[:, 0], pr[:, 1], ALU.add).then_inc(s.add, 1)
                        dve.wait_ge(s.add, n + 1)
                        v.tensor_tensor(yT[:, bass.ds(at, 1)].rearrange("p a t -> p (a t)"), pr[:, 0], pr[:, 2], ALU.add).then_inc(s.y, 1)
                    for tt in range(BT):
                        t, u = BT * b + tt, tt % 2
                        dve.wait_ge(s_x[u], 32 * b + 16 * (tt // 2) + 16)
                        if tt >= 2:
                            dve.wait_ge(s.tr, 2 * (t - 1))
                        else:
                            dve.wait_ge(s.tr, 2 * BT * b)
                        for half in range(2):
                            cols = slice(half * 512, (half + 1) * 512)
                            dve.wait_ge(s.out, 2 * t + half + 1)
                            v.tensor_tensor(h2[:, u, cols], po[half][:], rows[:, 0, cols], ALU.mult).then_inc(s.half, 1)
                        dve.wait_ge(s.half, 2 * t + 2 + HALF0)
                        v.tensor_tensor(xt[:, u], xt[:, u], h2[:, u], ALU.add).then_inc(s.x1d, 1)
                        dve.wait_ge(s.sr, t + 1)
                        v.reciprocal(st[:, 1:2], st[:, 1:2]).then_inc(s.h2a, 1)
                        dve.wait_ge(s.h2a, 2 * t + 1)
                        v.scalar_tensor_tensor(h2[:, u], xt[:, u], st[:, 1:2], rows[:, 2], ALU.mult, ALU.mult).then_inc(s.h2a, 1)
                        dve.wait_ge(s.h2a, 2 * t + 2)
                        v.tensor_tensor(h2[:, u], h2[:, u], rows[:, 1], ALU.add).then_inc(s.h2, 1)


def choose(nc, g):
    with ExitStack() as c:
        aff = sbuf(nc, c, "aff", [E, SEQ])
        red = sbuf(nc, c, "redc", [P, LT])
        val = sbuf(nc, c, "val", [E, CAP])
        idx = sbuf(nc, c, "idx", [E, CAP], U32)
        idf = sbuf(nc, c, "idf", [E, CAP])
        ps = psum(nc, c, "aff_ps", (P, 4, 512))
        pt = psum(nc, c, "ct_ps")
        s = sems(nc, c, "ch", "own ex aff tr trc top mi idf ct")
        with nc.Block() as block:
            @block.scalar
            def _(act):
                act.wait_ge(s.own, 2)
                nc.scalar.activation(g.logits, g.logits, ACT.Exp).then_inc(s.ex, 1)
                for q in range(4):
                    act.wait_ge(s.tr, q + 1)
                    nc.scalar.activation(aff[:, q * 512:(q + 1) * 512], ps[0:E, q], ACT.Copy).then_inc(s.trc, 1)

            @block.tensor
            def _(pe):
                pe.wait_ge(s.aff, 1)
                for q in range(4):
                    for j in range(4):
                        last = nc.tensor.transpose(ps[0:E, q, j * P:(j + 1) * P], g.logits[:, 4 * q + j], g.ident)
                    last.then_inc(s.tr, 1)
                pe.wait_ge(s.idf, 1)
                for half in range(CAP // P):
                    for j, rows in enumerate((val, idf)):
                        last = nc.tensor.transpose(pt[:, (2 * half + j) * E:(2 * half + j + 1) * E], rows[:, half * P:(half + 1) * P], g.ident[0:E, 0:E])
                last.then_inc(s.ct, 1)

            @block.vector
            def _(dve):
                v = nc.vector
                own = Steps(dve, s.own)
                lg = g.logits
                wide = red[:, :, None].broadcast_to([P, LT, E])
                own.done(v.tensor_reduce(red[:], lg, AX_X, ALU.max))
                own.settle()
                own.done(v.tensor_tensor(lg, lg, wide, ALU.subtract))
                dve.wait_ge(s.ex, 1)
                own.done(v.tensor_reduce(red[:], lg, AX_X, ALU.add))
                own.settle()
                own.done(v.reciprocal(red[:], red[:]))
                own.settle()
                v.tensor_tensor(lg, lg, wide, ALU.mult).then_inc(s.aff, 1)
                dve.wait_ge(s.trc, 4)
                own = Steps(dve, s.top)
                for r in range(CAP // 8):
                    at = slice(8 * r, 8 * r + 8)
                    own.done(v.max(val[:, at], aff[:]))
                    own.settle()
                    v.max_index(idx[:, at], val[:, at], aff[:]).then_inc(s.mi, 1)
                    own.done(v.match_replace(aff[:], val[:, at], aff[:], -1.0))
                    own.settle()
                dve.wait_ge(s.mi, CAP // 8)
                v.tensor_copy(idf[:], idx[:]).then_inc(s.idf, 1)
                dve.wait_ge(s.ct, 1)
                both = pt[:, 0:2 * CAP // P * E].rearrange("p (a j e) -> p a j e", j=2, e=E)
                own.done(v.tensor_copy(g.top_aff, both[:, :, 0]))
                own.done(v.tensor_copy(g.top_idx, both[:, :, 1]))
                own.settle()


def experts(nc, g):
    NF = FE // P
    NW = 3 * NF
    HALF = CAP // P
    TURN = 5
    with ExitStack() as c:
        w = sbuf(nc, c, "we", [P, NW, D])
        gt2 = sbuf(nc, c, "gt2", [P, D])
        ti = sbuf(nc, c, "ti", [P, 2, HALF], U32)
        ta = sbuf(nc, c, "ta", [P, 2, HALF])
        xe = sbuf(nc, c, "xe", [P, 2, HALF, D])
        xeT = sbuf(nc, c, "xeT", [P, 2, KD, CAP])
        hid = sbuf(nc, c, "hid", [P, NF, CAP])
        sg = sbuf(nc, c, "sge", [P, 2, CAP])
        yb = sbuf(nc, c, "ybe", [P, 2, HALF, D])
        pg = [psum(nc, c, f"eg{n}") for n in range(2)]
        pu = [psum(nc, c, f"eu{n}") for n in range(2)]
        py = [[psum(nc, c, f"ey{a}{n}") for n in range(2)] for a in range(HALF)]
        s = sems(nc, c, "ex", "cst pick ga0 ga1 tr xt used sig hid y yb sc0 sc1 held " + " ".join(f"w{n}" for n in range(NW)))
        s_w = list(s[-NW:])
        s_ga, s_sc = [s.ga0, s.ga1], [s.sc0, s.sc1]

        with nc.Block() as block:
            @block.sync
            def _(sp):
                sp.dma_start(gt2[:], g.rows_d[:, 3]).then_inc(s.cst, 16)
                for n in range(NW):
                    sp.dma_start(w[:, n], g.w_ex[0, n]).then_inc(s_w[n], 16)
                with nc.sync.Fori(1, E) as e:
                    for n in range(NW):
                        sp.wait_ge(s.used, NW * (e - 1) + n + 1)
                        sp.dma_start(w[:, n], g.w_ex[e, n]).then_inc(s_w[n], 16)

            @block.gpsimd
            def _(pool):
                def gather(e, u):
                    pool.wait_ge(s.pick, 2 * e + 2)
                    wait(pool, s.tr, 4 * (e - 1) if not isinstance(e, int) or e > 1 else 0)
                    hold(pool, s.held)
                    for a in range(HALF):
                        pool.indirect_dma_start(xe[:, u, a], None, g.h2_d,
                                                bass.IndirectOffsetOnAxis(ap=ti[:, u, a:a + 1], axis=0)).then_inc(s_ga[u], 16)

                def scatter(e, u, others):
                    pool.wait_ge(s.yb, 4 * e + 4)
                    pool.wait_ge(s_sc[1 - u], others)
                    hold(pool, s.held)
                    for a in range(HALF):
                        pool.indirect_dma_start(g.out, bass.IndirectOffsetOnAxis(ap=ti[:, u, a:a + 1], axis=0), yb[:, u, a], None,
                                                compute_op=ALU.add).then_inc(s_sc[u], 16)

                def pair(i, last):
                    scatter(2 * i, 0, 32 * i)
                    if not last:
                        gather(2 * i + 2, 0)
                    scatter(2 * i + 1, 1, 32 * i + 32)
                    if not last:
                        gather(2 * i + 3, 1)
                for u in range(2):
                    gather(u, u)
                with nc.gpsimd.Fori(0, E // 2 - 1) as i:
                    pair(i, False)
                pair(E // 2 - 1, True)
                for u in range(2):
                    pool.wait_ge(s_sc[u], 32 * E // 2)

            @block.tensor
            def _(pe):
                def turn(e, u):
                    pe.wait_ge(s_ga[u], 32 * ((e - u) // 2) + 32 if isinstance(e, int) else e * 16 + (2 - u) * 16)
                    pe.wait_ge(s.yb, 4 * (e - 1)) if not isinstance(e, int) or e > 1 else None
                    for a in range(HALF):
                        for q in range(2):
                            for j in range(4):
                                k = 4 * q + j
                                last = nc.tensor.transpose(py[a][q][:, j * P:(j + 1) * P], xe[:, u, a, k * P:(k + 1) * P], g.ident)
                            last.then_inc(s.tr, 1)

                def expert(e, u, last_one):
                    pe.wait_ge(s.xt, 4 * e + 4)
                    for f in range(NF):
                        for n, bank, free in ((2 * f, pg[f % 2], s.sig), (2 * f + 1, pu[f % 2], s.hid)):
                            pe.wait_ge(s_w[n], 16 * e + 16)
                            pe.wait_ge(free, NF * e + f + 1)
                            for k in range(KD):
                                last = nc.tensor.matmul(bank[:, 0:CAP], w[:, n, k * P:(k + 1) * P], xeT[:, u, k], start=(k == 0), stop=(k == KD - 1))
                            last.then_inc(s.used, 1)
                        if f == TURN and not last_one:
                            turn(e + 1, 1 - u)
                    if not last_one:
                        pe.wait_ge(s.xt, 4 * e + 8)
                    else:
                        pe.wait_ge(s.yb, 4 * e)
                    for f in range(NF):
                        n = 2 * NF + f
                        pe.wait_ge(s_w[n], 16 * e + 16)
                        pe.wait_ge(s.hid, NF * e + f + 1 + 2)
                        for a in range(HALF):
                            for q in range(2):
                                last = nc.tensor.matmul(py[a][q][:], hid[:, f, a * P:(a + 1) * P], w[:, n, q * 512:(q + 1) * 512],
                                                        start=(f == 0), stop=(f == NF - 1))
                        last.then_inc(s.used, 1)
                turn(0, 0)
                with nc.tensor.Fori(0, E // 2 - 1) as i:
                    for u in range(2):
                        expert(2 * i + u, u, False)
                expert(E - 2, 0, False)
                expert(E - 1, 1, True)

            @block.scalar
            def _(act):
                act.sem_inc(s.sig, 2)

                def copy_turned(e, u):
                    for a in range(HALF):
                        for q in range(2):
                            act.wait_ge(s.tr, 4 * e + 2 * a + q + 1)
                            nc.scalar.activation(xeT[:, u, 4 * q:4 * q + 4, a * P:(a + 1) * P],
                                                 py[a][q][:].rearrange("p (k t) -> p k t", k=4), ACT.Copy).then_inc(s.xt, 1)

                def expert(e, u, last_one):
                    for f in range(NF):
                        act.wait_ge(s.used, NW * e + 2 * f + 1)
                        act.wait_ge(s.hid, NF * e + f + 1)
                        nc.scalar.activation(sg[:, f % 2], pg[f % 2][:, 0:CAP], ACT.Silu).then_inc(s.sig, 1)
                        if f == TURN and not last_one:
                            copy_turned(e + 1, 1 - u)
                copy_turned(0, 0)
                with nc.scalar.Fori(0, E // 2 - 1) as i:
                    for u in range(2):
                        expert(2 * i + u, u, False)
                expert(E - 2, 0, False)
                expert(E - 1, 1, True)

            @block.vector
            def _(dve):
                v = nc.vector
                dve.sem_inc(s.hid, 2)
                dve.wait_ge(s.cst, 16)

                def pick(e, u, added):
                    at = e if isinstance(e, int) else nc.vector.snap(e)
                    wait(dve, s_sc[u], added)
                    v.tensor_copy(ti[:, u], g.top_idx[:, :, bass.ds(at, 1)].rearrange("p a e -> p (a e)")).then_inc(s.pick, 1)
                    v.tensor_copy(ta[:, u], g.top_aff[:, :, bass.ds(at, 1)].rearrange("p a e -> p (a e)")).then_inc(s.pick, 1)

                def expert(i, u, last_one):
                    e = 2 * i + u
                    for f in range(NF):
                        dve.wait_ge(s.used, NW * e + 2 * f + 2)
                        dve.wait_ge(s.sig, NF * e + f + 1 + 2)
                        v.tensor_tensor(hid[:, f], sg[:, f % 2], pu[f % 2][:, 0:CAP], ALU.mult).then_inc(s.hid, 1)
                        if f == 1 and not last_one and (u == 1 or not isinstance(i, int) or i > 0):
                            pick(e + 1, 1 - u, 32 * (i + u))
                    dve.wait_ge(s.used, NW * (e + 1))
                    dve.wait_ge(s.pick, 2 * e + 2)
                    for a in range(HALF):
                        for q in range(2):
                            cols = slice(q * 512, (q + 1) * 512)
                            v.scalar_tensor_tensor(yb[:, u, a, cols], py[a][q][:], ta[:, u, a:a + 1], gt2[:, cols],
                                                   ALU.mult, ALU.mult).then_inc(s.yb, 1)
                pick(0, 0, 0)
                pick(1, 1, 0)
                expert(0, 0, False)
                expert(0, 1, False)
                with nc.vector.Fori(1, E // 2 - 1) as i:
                    for u in range(2):
                        expert(i, u, False)
                expert(E // 2 - 1, 0, False)
                expert(E // 2 - 1, 1, True)


def shape_tables():
    i = np.arange(P)
    t = np.zeros((P, C_W), np.float32)
    t[:, C_ID:C_ID + P] = np.eye(P)
    t[:, C_ONE:C_ONE + P] = 1.0
    t[:, C_BLK:C_BLK + P] = (i[:, None] // DH) == (i[None, :] // DH)
    nf = DK // 4
    for half in range(2):
        for f in range(nf):
            a, b = half * 2 * nf + f, half * 2 * nf + nf + f
            t[b, C_ROT + a] = -1.0
            t[a, C_ROT + b] = 1.0
    l, m = i[:, None], i[None, :]
    for d in range(2):
        before, after = (l <= m, l > m) if d == 0 else (l >= m, l < m)
        at = C_DIR + d * N_DIRT * P
        t[:, at:at + P] = before
        t[:, at + P:at + 2 * P] = after
        for lev in range(N_LEV):
            size = 1 << lev
            pair = (l // (2 * size)) == (m // (2 * size))
            up, low = (l // size) % 2 == 1, (m // size) % 2 == 0
            mask = pair & up & low if d == 0 else pair & ~up & ~low
            at = C_LEV + (d * N_LEV + lev) * P
            t[:, at:at + P] = mask
    start = np.clip(np.arange(GRID) - WC // 2, 0, GRID - WC)
    j, col = i[:, None] % GRID, np.arange(GRID)[None, :]
    t[:, C_WIN:C_WIN + GRID] = np.where((col >= start[j]) & (col < start[j] + WC), 0.0, NEG)
    f = np.zeros((P, F_W), np.float64)
    same = (l // 64) == (m // 64)
    ang = 2 * np.pi * ((l % 64) * (m % 64) % 64) / 64
    f[:, F_C4:F_C4 + P] = same * np.cos(ang) / np.sqrt(SEQ * 64)
    f[:, F_C4 + P:F_C4 + 2 * P] = same * np.sin(ang) / np.sqrt(SEQ * 64)
    ang = 2 * np.pi * (l * m % P) / P
    for n, table in enumerate((np.cos(ang), np.sin(ang), -np.sin(ang))):
        f[:, F_N1 + n * P:F_N1 + (n + 1) * P] = table
    n2 = SEQ // P
    ang = 2 * np.pi * (i[:, None] * np.arange(n2)[None, :]) / SEQ
    f[:, F_TW:F_TW + n2], f[:, F_TW + n2:F_TW + 2 * n2] = np.cos(ang), np.sin(ang)
    lo = P // n2
    ang = 2 * np.pi * ((l // lo) * (m // lo) % n2) / n2
    same = (l % lo) == (m % lo)
    f[:, F_K2:F_K2 + P], f[:, F_K2 + P:F_K2 + 2 * P] = same * np.cos(ang), -1.0 * same * np.sin(ang)
    tok = np.arange(SEQ)
    inv = 10000.0 ** (-np.arange(nf) / nf)
    where = np.stack([tok // GRID, tok % GRID])
    ang = where[:, None, :] * inv[None, :, None]
    ang = np.repeat(ang[:, None], 2, axis=1).reshape(P, SEQ)
    rope = np.stack([np.cos(ang), np.sin(ang)], axis=1).astype(np.float32)
    return {"consts": t, "rope": rope, "ftab": f.astype(np.float32)}


def expert_chunks(i):
    gate, up = (i[n][0].reshape(E, KD, P, FE // P, P).transpose(0, 3, 2, 1, 4).reshape(E, FE // P, 1, P, D)
                for n in ("w_e_gate", "w_e_up"))
    down = i["w_e_down"][0].reshape(E, FE // P, P, D)
    first = np.concatenate([gate, up], axis=2).reshape(E, 2 * FE // P, P, D)
    return np.concatenate([first, down], axis=1)


def layouts(i):
    tokens = np.concatenate([i["ctx"][0], i["x"][0]], axis=0)

    def col(v):
        return v.reshape(-1, P).T

    def tiles(m):
        return m.reshape(KD, P, -1, P).transpose(2, 1, 0, 3)

    w_in = i["w_in"][0]
    cuts = np.cumsum([0, 512, 512, 512, 512, 8, 8, 256, 256, 256, 256, 3 * D])
    part = [w_in[:, a:b] for a, b in zip(cuts[:-1], cuts[1:])]
    q, k, v, z, a, b, u, qn, kn, vn, gr = part
    wm, bm = i["w_mod"][0], i["b_mod"][0]
    out = {
        "xT": tokens.T.reshape(KD, P, T).transpose(1, 0, 2),
        "x": i["x"][0],
        "cc": np.stack([col(i["c"][0]), col(i["c_ctx"])], axis=-1),
        "w_mod_col": wm[:, :2 * D].reshape(KD, P, 2 * D).transpose(1, 0, 2),
        "w_mod_row": wm[:, 2 * D:].reshape(KD, P, 2, 2 * D).transpose(2, 0, 1, 3).reshape(2 * KD, P, 2 * D),
        "b_mod_col": col(bm[:2 * D]),
        "b_mod_row": bm[2 * D:],
        "norm1": col(i["norm1_w"][0]),
        "norm2": i["norm2_w"][0],
        "w_ch": tiles(np.concatenate([q, k, v, z, qn, kn, u], axis=1)),
        "w_tok": np.concatenate([vn, a, b], axis=1).reshape(KD, P, -1).transpose(1, 0, 2),
        "conv_w": i["conv_w"][0].reshape(CONV, 3, H, P).transpose(3, 2, 1, 0),
        "na_norm": np.stack([np.tile(i["na_qn_w"][0], 2), np.tile(i["na_kn_w"][0], 2)], axis=-1),
        "gdn_norm": i["gdn_norm_w"][0].reshape(P, 1),
        "w_gates": tiles(gr).reshape(3, KD, P, KD, P).transpose(1, 2, 0, 3, 4),
        "w_br": tiles(np.concatenate([i["w_br_a"][0], i["w_br_b"][0], i["w_br_c"][0]], axis=0)),
        "w_out": i["w_out"][0].reshape(KD, P, D).transpose(1, 0, 2),
        "w_router": i["w_router"][0].reshape(KD, P, E).transpose(1, 0, 2),
        "w_ex": expert_chunks(i),
        "rpb": i["na_rpb"][0].reshape(H * 15, 31),
        "a_log": i["a_log"][0].reshape(-1),
        "dt_bias": i["dt_bias"][0].reshape(-1),
    }
    out.update(shape_tables())
    return {n: np.ascontiguousarray(a) for n, a in out.items()}


def shared(tensors):
    class Shared(namedtuple("Tensors", list(tensors))):
        pass
    return Shared(**tensors)


SCRATCH = {
    "rows_d": (P, 4, D),
    "h_d": (P, KD, T),
    "q_d": (POS, P, H, P), "k_d": (POS, P, H, P), "kt_d": (POS, P, H, P), "vt_d": (POS, P, H, P),
    "z_d": (H, P, SEQ),
    "v_d": (T, 2 * P),
    "h2_d": (SEQ, D),
    "skew_d": (H * 15, GRID, 127),
    "oc_d": (2 * P, SEQ),
    "z2_d": (2, P, SEQ // P, FN),
    "yb_d": (2 * P, SEQ),
    "o_d": (2, POS, P, H, P),
}


def program(nc, g, stages=99):
    with ExitStack() as c:
        consts = sbuf(nc, c, "consts_sb", [P, C_W])
        eps = sbuf(nc, c, "eps_sb", [P, 1])
        g.eps = eps[:]
        g.ident, g.ones, g.blk, g.rot = (consts[:, at:at + P] for at in (C_ID, C_ONE, C_BLK, C_ROT))
        g.window = consts[:, C_WIN:C_WIN + GRID]
        g.dirt = lambda d, j: consts[:, C_DIR + (d * N_DIRT + j) * P:C_DIR + (d * N_DIRT + j + 1) * P]
        g.level = lambda d, lev: consts[:, C_LEV + (d * N_LEV + lev) * P:C_LEV + (d * N_LEV + lev + 1) * P]
        g.gd, g.beta, g.begc, g.esfx = (sbuf(nc, c, n, [P, 2, POS, H])[:] for n in ("gd", "beta", "begc", "esfx"))
        g.ab = sbuf(nc, c, "ab", [P, NT, 16])[:]
        load_tables(nc, g, consts, eps)
        with ExitStack() as c1:
            g.mod1 = sbuf(nc, c1, "mod1", [P, 2, KD, 2])[:]
            modulation(nc, g)
            g.hT = sbuf(nc, c1, "hT", [P, KD, T])[:]
            first_norm(nc, g)
            if stages < 2:
                return
            delta_inputs(nc, g)
            g.qn = sbuf(nc, c1, "qn", [P, HP, SEQ])[:]
            g.kn = sbuf(nc, c1, "kn", [P, HP, T])[:]
            g.uT = sbuf(nc, c1, "uT", [P, 2, SEQ])[:]
            mixer_inputs(nc, g)
            if stages >= 2.5:
                attention(nc, g)
                fourier(nc, g)
        if stages < 3:
            return
        decays(nc, g)
        delta_rule(nc, g)
        if stages < 4:
            return
        g.logits = sbuf(nc, c, "logits", [P, LT, E])[:]
        g.top_aff = sbuf(nc, c, "top_aff", [P, CAP // P, E])[:]
        g.top_idx = sbuf(nc, c, "top_idx", [P, CAP // P, E], U32)[:]
        merge(nc, g)
        choose(nc, g)
        experts(nc, g)


def load_tables(nc, g, consts, eps):
    with ExitStack() as c:
        s = sems(nc, c, "tab", "ld eps")
        with nc.Block() as block:
            @block.sync
            def _(sp):
                sp.dma_start(consts[:], g.consts).then_inc(s.ld, 16)
                sp.wait_ge(s.ld, 16)

            @block.vector
            def _(dve):
                nc.vector.memset(eps[:], EPS).then_inc(s.eps, 1)
                dve.wait_ge(s.eps, 1)


def kernel(**inputs):
    import concourse.bacc as bacc
    from concourse.bass_utils import run_bass_kernel_spmd

    nc = bacc.Bacc("TRN2", target_bir_lowering=False, num_devices=1)
    arrays = {"in_" + n: a for n, a in layouts({n: np.asarray(a) for n, a in inputs.items()}).items()}
    tensors = {n[3:]: nc.dram_tensor(n, a.shape, mybir.dt.from_np(a.dtype), kind="ExternalInput").ap() for n, a in arrays.items()}
    tensors.update({n: nc.dram_tensor(n, list(shape), F32).ap() for n, shape in SCRATCH.items()})
    tensors["out"] = nc.dram_tensor("out", (SEQ, D), F32, kind="ExternalOutput").ap()
    g = shared(tensors)
    program(nc, g)
    r = run_bass_kernel_spmd(nc, [arrays], core_ids=[0])
    return r.results[0]["out"].reshape(1, SEQ, D)
```

```python
from collections import namedtuple
from contextlib import ExitStack

import numpy as np

import concourse.bass as bass
from concourse import mybir

F32 = mybir.dt.float32
U32 = mybir.dt.uint32
F32R = mybir.dt.float32r
ACT = mybir.ActivationFunctionType
ALU = mybir.AluOpType
AX_X = mybir.AxisListType.X

P = 128
D = 1024
KD = D // P
CTX = 256
SEQ = 2048
T = CTX + SEQ
NT = T // P
CT = CTX // P
LT = SEQ // P
POS = NT + CT
EPS = 1e-6
H = 4
DK = 128
CONV = 5
PAD = CONV // 2
CONVW = T + 3 * PAD
CONVO = CONVW - 2 * PAD
GRID = 64
WR, WC = 8, 16
ROWS = SEQ // GRID
DH = 64
HP = 2
FN = 256
E = 16
CAP = 2 * SEQ // E
FE = 1024
BLOCKS = [(0, CTX)] + [(CTX + 512 * b, 512) for b in range(4)]
NEG = -1e30

C_ID, C_ONE, C_BLK, C_ROT = 0, P, 2 * P, 3 * P
C_DIR = 4 * P
N_DIRT = 2
C_LEV = C_DIR + 2 * N_DIRT * P
N_LEV = 7
C_WIN = C_LEV + 2 * N_LEV * P
C_W = C_WIN + GRID

F_C4 = 0
F_N1 = F_C4 + FN
F_TW = F_N1 + 3 * P
F_K2 = F_TW + 2 * (SEQ // P)
F_W = F_K2 + 2 * P


class Steps:

    def __init__(self, eng, sem, start=0):
        self.eng, self.sem, self.start, self.n = eng, sem, start, 0

    def done(self, ins):
        self.n += 1
        return ins.then_inc(self.sem, 1)

    def settle(self):
        self.eng.wait_ge(self.sem, self.start + self.n)


def hold(eng, sem):
    eng.sem_inc(sem, 1)


def sbuf(nc, c, name, shape, dt=F32):
    return c.enter_context(nc.sbuf_tensor("sb_" + name, shape, dt))


def psum(nc, c, name, shape=(P, 512), dt=F32):
    return c.enter_context(nc.psum_tensor(name, list(shape), dt))


def sems(nc, c, prefix, names):
    made = {n: nc.alloc_semaphore(prefix + "_" + n) for n in names.split()}


    def clear():
        nc.clear_and_free_semaphores(list(made.values()))
        nc.all_engine_barrier()
    c.callback(clear)
    return namedtuple("Semaphores", list(made))(**made)


def modulation(nc, g):
    with ExitStack() as c:
        cc = sbuf(nc, c, "cc", [P, KD, 2])
        cs = sbuf(nc, c, "cs", [P, KD, 2])
        csb = sbuf(nc, c, "csb", [P, KD, P])
        wcol = sbuf(nc, c, "wcol", [P, KD, 2 * D])
        bcol = sbuf(nc, c, "bcol", [P, 2 * KD])
        n1 = sbuf(nc, c, "n1", [P, KD])
        wrow = sbuf(nc, c, "wrow", [P, 2, 2 * D])
        rows = sbuf(nc, c, "rows", [P, 4, D])
        brow = sbuf(nc, c, "brow", [P, 4 * D])
        n2 = sbuf(nc, c, "n2", [P, D])
        ps = psum(nc, c, "mod_ps", (P, 8, 512))
        s = sems(nc, c, "mod", "small srow wcol w0 w1 silu bc col row fin rowfin st used")
        s_w = [s.w0, s.w1]
        pcol = ps[:, 0, 0:4 * KD].rearrange("p (m s) -> p m s", s=2)
        with nc.Block() as block:
            @block.sync
            def _(sp):
                sp.dma_start(cc[:], g.cc).then_inc(s.small, 16)
                sp.dma_start(bcol[:], g.b_mod_col).then_inc(s.small, 16)
                sp.dma_start(n1[:], g.norm1).then_inc(s.small, 16)
                sp.dma_start(wcol[:], g.w_mod_col).then_inc(s.wcol, 16)
                for k in range(2 * KD):
                    if k >= 2:
                        sp.wait_ge(s.used, k - 1)
                    sp.dma_start(wrow[:, k % 2], g.w_mod_row[k]).then_inc(s_w[k % 2], 16)
                sp.wait_ge(s.rowfin, 9)
                sp.dma_start(g.rows_d, rows[:]).then_inc(s.st, 16)
                sp.wait_ge(s.st, 16)

            @block.gpsimd
            def _(pool):
                pool.dma_start(brow[:], g.b_mod_row.partition_broadcast(P)).then_inc(s.srow, 16)
                pool.dma_start(n2[:], g.norm2.partition_broadcast(P)).then_inc(s.srow, 16)

            @block.scalar
            def _(act):
                act.wait_ge(s.small, 48)
                nc.scalar.activation(cs[:], cc[:], ACT.Silu).then_inc(s.silu, 1)

            @block.tensor
            def _(pe):
                pe.wait_ge(s.silu, 1)
                pe.wait_ge(s.wcol, 16)
                for m in range(2 * KD):
                    for k in range(KD):
                        last = nc.tensor.matmul(pcol[:, m], wcol[:, k, m * P:(m + 1) * P], cs[:, k],
                                                start=(k == 0), stop=(k == KD - 1))
                last.then_inc(s.col, 1)
                pe.wait_ge(s.bc, 1)
                pe.wait_ge(s.fin, 3)
                for half in range(2):
                    for k in range(KD):
                        n = half * KD + k
                        pe.wait_ge(s_w[n % 2], 16 * (n // 2 + 1))
                        for j in range(4):
                            last = nc.tensor.matmul(ps[:, half * 4 + j], csb[:, k], wrow[:, n % 2, j * 512:(j + 1) * 512],
                                                    start=(k == 0), stop=(k == KD - 1))
                        last.then_inc(s.used, 1)
                    last = None

            @block.vector
            def _(dve):
                own = Steps(dve, s.fin)
                dve.wait_ge(s.silu, 1)
                nc.vector.tensor_copy(csb[:], cs[:, :, 0:1].broadcast_to([P, KD, P])).then_inc(s.bc, 1)
                dve.wait_ge(s.small, 48)
                dve.wait_ge(s.srow, 32)
                dve.wait_ge(s.col, 1)
                own.done(nc.vector.tensor_tensor(g.mod1[:, 0], pcol[:, 0:KD], bcol[:, 0:KD, None].broadcast_to([P, KD, 2]), ALU.add))
                own.done(nc.vector.tensor_tensor(g.mod1[:, 1], pcol[:, KD:], bcol[:, KD:, None].broadcast_to([P, KD, 2]), ALU.add))
                own.settle()
                own.done(nc.vector.scalar_tensor_tensor(g.mod1[:, 1], g.mod1[:, 1], 1.0, n1[:, :, None].broadcast_to([P, KD, 2]),
                                                        ALU.add, ALU.mult))
                own = Steps(dve, s.rowfin)
                for half in range(2):
                    dve.wait_ge(s.used, (half + 1) * KD)
                    for j in range(half * 4, half * 4 + 4):
                        own.done(nc.vector.tensor_tensor(rows[:, j // 2, (j % 2) * 512:(j % 2 + 1) * 512], ps[:, j],
                                                         brow[:, j * 512:(j + 1) * 512], ALU.add))
                own.settle()
                own.done(nc.vector.scalar_tensor_tensor(rows[:, 2], rows[:, 2], 1.0, n2[:], ALU.add, ALU.mult))


def first_norm(nc, g):
    with ExitStack() as c:
        sq = sbuf(nc, c, "sq", [P, KD, 512])
        rs = sbuf(nc, c, "rs", [P, 512])
        ps = psum(nc, c, "n_ps")
        s = sems(nc, c, "n1", "ld0 ld1 ld2 ld3 ld4 sq sum root dve h st")
        ld = [s.ld0, s.ld1, s.ld2, s.ld3, s.ld4]
        with nc.Block() as block:
            @block.sync
            def _(sp):
                for b, (t0, w) in enumerate(BLOCKS):
                    sp.dma_start(g.hT[:, :, t0:t0 + w], g.xT[:, :, t0:t0 + w]).then_inc(ld[b], 16)
                for b, (t0, w) in enumerate(BLOCKS):
                    sp.wait_ge(s.h, KD * (b + 1))
                    sp.dma_start(g.h_d[:, :, t0:t0 + w], g.hT[:, :, t0:t0 + w]).then_inc(s.st, 16)
                sp.wait_ge(s.st, 16 * len(BLOCKS))

            @block.scalar
            def _(act):
                for b, (t0, w) in enumerate(BLOCKS):
                    act.wait_ge(ld[b], 16)
                    if b:
                        act.wait_ge(s.sum, b)
                    nc.scalar.activation(sq[:, :, 0:w], g.hT[:, :, t0:t0 + w], ACT.Square).then_inc(s.sq, 1)
                    act.wait_ge(s.sum, b + 1)
                    if b:
                        act.wait_ge(s.dve, 2 * b)
                    nc.scalar.activation(rs[:, 0:w], ps[:, 0:w], ACT.Sqrt, bias=g.eps[:, 0:1], scale=1.0 / D).then_inc(s.root, 1)
                    act.wait_ge(s.dve, 2 * b + 2)
                    which = 1 if b == 0 else 0
                    for k in range(KD):
                        nc.scalar.activation(g.hT[:, k, t0:t0 + w], g.hT[:, k, t0:t0 + w], ACT.Identity,
                                             bias=g.mod1[:, 0, k, which:which + 1],
                                             scale=g.mod1[:, 1, k, which:which + 1]).then_inc(s.h, 1)

            @block.tensor
            def _(pe):
                for b, (t0, w) in enumerate(BLOCKS):
                    pe.wait_ge(s.sq, b + 1)
                    if b:
                        pe.wait_ge(s.root, b)
                    for k in range(KD):
                        last = nc.tensor.matmul(ps[:, 0:w], g.ones, sq[:, k, 0:w], start=(k == 0), stop=(k == KD - 1))
                    last.then_inc(s.sum, 1)

            @block.vector
            def _(dve):
                own = Steps(dve, s.dve)
                for b, (t0, w) in enumerate(BLOCKS):
                    dve.wait_ge(s.root, b + 1)
                    own.done(nc.vector.reciprocal(rs[:, 0:w], rs[:, 0:w]))
                    own.settle()
                    own.done(nc.vector.tensor_tensor(g.hT[:, :, t0:t0 + w], g.hT[:, :, t0:t0 + w],
                                                     rs[:, None, 0:w].broadcast_to([P, KD, w]), ALU.mult))


BANKS = 3
NB = len(BLOCKS)
TG = [(j, min(4, NT - j)) for j in range(0, NT, 4)]
NG = len(TG)
NROT = NB - 1


def before(b):
    if b >= BANKS:
        return b - BANKS, 0
    return max(x for x in range(NB) if x % BANKS == b), 1


def staggered(eng, first, second):
    first(0, 0)
    with eng.Fori(0, H - 1) as h:
        for kind in range(3):
            first(h + (kind == 2), (kind + 1) % 3)
            second(h, kind)
    for kind in range(3):
        if kind < 2:
            first(H - 1, kind + 1)
        second(H - 1, kind)


def delta_inputs(nc, g):
    with ExitStack() as c:
        w = sbuf(nc, c, "wq", [P, 3, KD, P])
        raw = sbuf(nc, c, "raw", [P, CONVW])
        cv = sbuf(nc, c, "cv", [P, CONVO])
        sl = sbuf(nc, c, "sl", [P, 3, T])
        tt = sbuf(nc, c, "turned", [P, NT, P])
        rs = sbuf(nc, c, "rsb", [P, 2, 512])
        rope = sbuf(nc, c, "ropeb", [P, 2, SEQ])
        tmp = sbuf(nc, c, "tmp", [P, 512])
        cw = sbuf(nc, c, "cw", [P, H, 3, CONV])
        ps = psum(nc, c, "p_ps", (P, BANKS, 512))
        pn = psum(nc, c, "pn_ps", (P, 2, 512))
        pr = psum(nc, c, "pr_ps")
        pt = psum(nc, c, "pt_ps", (P, 2, 512))
        s = sems(nc, c, "di", "w0 w1 w2 tab zero conv proj rawp cdone silu sq sum root rec nrm perm mul rot tr trc stq stk stv stt")
        s_w = [s.w0, s.w1, s.w2]
        s_st = [s.stq, s.stk]
        dst = (g.q_d, g.k_d, g.kt_d, g.vt_d)

        with nc.Block() as block:
            @block.sync
            def _(sp):
                sp.dma_start(cw[:], g.conv_w).then_inc(s.tab, 16)
                sp.dma_start(rope[:], g.rope).then_inc(s.tab, 16)

                def store(h, tensor, src, sem):
                    sp.dma_start(tensor[0:NT, :, h].rearrange("n p c -> p n c"), src).then_inc(sem, 16)
                    sp.dma_start(tensor[NT:POS, :, h].rearrange("n p c -> p n c"), src[:, 0:CT]).then_inc(sem, 16)

                def stores(h):
                    for kind in range(2):
                        sp.wait_ge(s.rot, NROT * (2 * h + kind + 1))
                        store(h, dst[kind], sl[:, kind].rearrange("p (n c) -> p n c", c=P), s_st[kind])
                    for kind in range(2):
                        sp.wait_ge(s.trc, NG * (2 * h + kind + 1))
                        store(h, dst[2 + kind], tt[:], s.stt)
                with nc.sync.Fori(0, H) as h:
                    stores(h)
                for sem, n in ((s.stq, 32 * H), (s.stk, 32 * H), (s.stt, 64 * H)):
                    sp.wait_ge(sem, n)

            @block.gpsimd
            def _(pool):
                for kind in range(3):
                    pool.dma_start(w[:, kind], g.w_ch[kind * H]).then_inc(s_w[kind], 16)
                with nc.gpsimd.Fori(0, H - 1) as h:
                    for kind in range(3):
                        pool.wait_ge(s.proj, NB * (3 * h + kind + 1))
                        pool.dma_start(w[:, kind], g.w_ch[kind * H + h + 1]).then_inc(s_w[kind], 16)

            @block.tensor
            def _(pe):
                def project(h, kind):
                    t = 3 * h + kind
                    pe.wait_ge(s_w[kind], 16 * h + 16)
                    for b, (t0, wd) in enumerate(BLOCKS):
                        bb, back = before(b)
                        pe.wait_ge(s.rawp, NB * (t + 1 - back) + bb + 1)
                        for k in range(KD):
                            last = nc.tensor.matmul(ps[:, b % BANKS, 0:wd], w[:, kind, k], g.hT[:, k, t0:t0 + wd],
                                                    start=(k == 0), stop=(k == KD - 1))
                        last.then_inc(s.proj, 1)

                def finish(h, kind):
                    if kind < 2:
                        r = 2 * h + kind
                        pe.wait_ge(s.sq, r + 1)
                        for b, (t0, wd) in enumerate(BLOCKS):
                            pe.wait_ge(s.root, NB * r + max(b - 1, 0))
                            nc.tensor.matmul(pn[:, b % 2, 0:wd], g.ones, cv[:, t0:t0 + wd],
                                             start=True, stop=True).then_inc(s.sum, 1)
                        for b in range(NROT):
                            t0, wd = BLOCKS[b + 1]
                            pe.wait_ge(s.nrm, NB * r + b + 2)
                            pe.wait_ge(s.rot, NROT * r + b)
                            nc.tensor.matmul(pr[:, 0:wd], g.rot, sl[:, kind, t0:t0 + wd],
                                             start=True, stop=True).then_inc(s.perm, 1)
                    if kind > 0:
                        m = 2 * h + kind - 1
                        if kind == 1:
                            pe.wait_ge(s.rot, NROT * (2 * h + 2))
                        else:
                            pe.wait_ge(s.silu, 2 * (3 * h + 3))
                        for j, (n0, cnt) in enumerate(TG):
                            pe.wait_ge(s.trc, NG * m + max(j - 1, 0))
                            for i in range(cnt):
                                last = nc.tensor.transpose(pt[:, j % 2, i * P:(i + 1) * P],
                                                           sl[:, kind, (n0 + i) * P:(n0 + i + 1) * P], g.ident)
                            last.then_inc(s.tr, 1)
                staggered(nc.tensor, project, finish)

            @block.scalar
            def _(act):
                act.sem_inc(s.rawp, NB)
                act.wait_ge(s.zero, 1)

                def copy_raw(h, kind):
                    t = 3 * h + kind
                    act.wait_ge(s.cdone, t)
                    for b, (t0, wd) in enumerate(BLOCKS):
                        act.wait_ge(s.proj, NB * t + b + 1)
                        at = t0 + PAD * (1 if b == 0 else 2)
                        nc.scalar.activation(raw[:, at:at + wd], ps[:, b % BANKS, 0:wd], ACT.Copy).then_inc(s.rawp, 1)

                def activate(h, kind):
                    t = 3 * h + kind
                    act.wait_ge(s.cdone, t + 1)
                    if kind < 2:
                        act.wait_ge(s_st[kind], 32 * h)
                    if kind > 0:
                        act.wait_ge(s.tr, NG * (2 * h + kind - 1))
                    own = Steps(act, s.silu, 2 * t)
                    own.done(nc.scalar.activation(sl[:, kind, 0:CTX], cv[:, 0:CTX], ACT.Silu))
                    own.done(nc.scalar.activation(sl[:, kind, CTX:T], cv[:, CTX + PAD:CONVO], ACT.Silu))
                    if kind < 2:
                        own.settle()
                        nc.scalar.activation(cv[:, 0:T], sl[:, kind], ACT.Square).then_inc(s.sq, 1)

                def finish(h, kind):
                    if kind < 2:
                        r = 2 * h + kind
                        for b, (t0, wd) in enumerate(BLOCKS):
                            act.wait_ge(s.sum, NB * r + b + 1)
                            act.wait_ge(s.nrm, NB * r + max(b - 1, 0))
                            nc.scalar.activation(rs[:, b % 2, 0:wd], pn[:, b % 2, 0:wd], ACT.Sqrt,
                                                 bias=g.eps[:, 0:1]).then_inc(s.root, 1)
                    if kind > 0:
                        m = 2 * h + kind - 1
                        act.wait_ge(s.stt, 32 * m)
                        for j, (n0, cnt) in enumerate(TG):
                            act.wait_ge(s.tr, NG * m + j + 1)
                            nc.scalar.activation(tt[:, n0:n0 + cnt], pt[:, j % 2, 0:cnt * P], ACT.Copy).then_inc(s.trc, 1)

                copy_raw(0, 0)
                activate(0, 0)

                def step(h, kind, last):
                    if not last:
                        copy_raw(h + (kind == 2), (kind + 1) % 3)
                    finish(h, kind)
                    if not last:
                        activate(h + (kind == 2), (kind + 1) % 3)
                with nc.scalar.Fori(0, H - 1) as h:
                    for kind in range(3):
                        step(h, kind, False)
                for kind in range(3):
                    step(H - 1, kind, kind == 2)

            @block.vector
            def _(dve):
                nc.vector.memset(raw[:], 0.0).then_inc(s.zero, 1)
                dve.wait_ge(s.tab, 32)

                def convolve(h, kind):
                    t = 3 * h + kind
                    dve.wait_ge(s.rawp, NB * (t + 2))
                    dve.wait_ge(s.silu, 2 * t)
                    if kind == 1:
                        dve.wait_ge(s.sum, NB * (2 * h + 1))
                    if kind == 2:
                        dve.wait_ge(s.sum, NB * (2 * h + 2))
                    own = Steps(dve, s.conv, (CONV - 1) * t)
                    own.done(nc.vector.tensor_scalar(cv[:], raw[:, 0:CONVO], cw[:, h, kind, 0:1], None, ALU.mult))
                    for i in range(1, CONV):
                        own.settle()
                        ins = nc.vector.scalar_tensor_tensor(cv[:], raw[:, i:i + CONVO], cw[:, h, kind, i:i + 1], cv[:],
                                                             ALU.mult, ALU.add)
                        if i < CONV - 1:
                            own.done(ins)
                        else:
                            ins.then_inc(s.cdone, 1)

                def finish(h, kind):
                    if kind == 2:
                        return
                    r = 2 * h + kind
                    scale = DK ** -0.5 if kind == 0 else 1.0
                    for b, (t0, wd) in enumerate(BLOCKS):
                        dve.wait_ge(s.root, NB * r + b + 1)
                        nc.vector.reciprocal(rs[:, b % 2, 0:wd], rs[:, b % 2, 0:wd]).then_inc(s.rec, 1)
                        dve.wait_ge(s.rec, NB * r + b + 1)
                        nc.vector.scalar_tensor_tensor(sl[:, kind, t0:t0 + wd], rs[:, b % 2, 0:wd], scale,
                                                       sl[:, kind, t0:t0 + wd], ALU.mult, ALU.mult).then_inc(s.nrm, 1)
                    for b in range(NROT):
                        t0, wd = BLOCKS[b + 1]
                        n = NROT * r + b
                        dve.wait_ge(s.perm, n + 1)
                        own = Steps(dve, s.mul, 2 * n)
                        dve.wait_ge(s.rot, n)
                        own.done(nc.vector.tensor_tensor(tmp[:], pr[:], rope[:, 1, b * 512:(b + 1) * 512], ALU.mult))
                        own.done(nc.vector.tensor_tensor(sl[:, kind, t0:t0 + wd], sl[:, kind, t0:t0 + wd],
                                                         rope[:, 0, b * 512:(b + 1) * 512], ALU.mult))
                        own.settle()
                        nc.vector.tensor_tensor(sl[:, kind, t0:t0 + wd], sl[:, kind, t0:t0 + wd], tmp[:],
                                                ALU.add).then_inc(s.rot, 1)

                convolve(0, 0)

                def step(h, kind, last):
                    finish(h, kind)
                    if not last:
                        convolve(h + (kind == 2), (kind + 1) % 3)
                with nc.vector.Fori(0, H - 1) as h:
                    for kind in range(3):
                        step(h, kind, False)
                for kind in range(3):
                    step(H - 1, kind, kind == 2)


def mixer_inputs(nc, g):
    LB = BLOCKS[1:]
    NL = len(LB)
    REST = [(16, g.qn[:, 0], False), (17, g.qn[:, 1], False), (20, g.uT[:, 0], False), (21, g.uT[:, 1], False),
            (18, g.kn[:, 0], True), (19, g.kn[:, 1], True)]
    NORM = [(g.qn[:, j, 512 * b:512 * (b + 1)], 0) for j in range(HP) for b in range(NL)]
    NORM += [(g.kn[:, j, t0:t0 + wd], 1) for j in range(HP) for t0, wd in BLOCKS]
    assert len(NORM) == NT
    with ExitStack() as c:
        w = sbuf(nc, c, "wz", [P, 2, KD, P])
        wt = sbuf(nc, c, "wt", [P, KD, 2 * P + 16])
        zb = sbuf(nc, c, "zb", [P, 2, SEQ])
        vb = sbuf(nc, c, "vb", [P, NT, 2 * P])
        sq = sbuf(nc, c, "sqn", [P, 2, 512])
        rs = sbuf(nc, c, "rsn", [P, 2, 512])
        nw = sbuf(nc, c, "nw", [P, 2])
        ps = psum(nc, c, "z_ps", (P, 5, 512))
        pn = psum(nc, c, "zn_ps")
        pt = psum(nc, c, "zt_ps", (P, 2, 512))
        s = sems(nc, c, "mi", "w0 w1 wt blk blkc ev evc z0 z1 tok vcp acp sq sum root rec nrm st")
        s_w, s_z = [s.w0, s.w1], [s.z0, s.z1]
        NZ = H
        with nc.Block() as block:
            @block.sync
            def _(sp):
                sp.dma_start(nw[:], g.na_norm).then_inc(s.wt, 16)
                sp.dma_start(wt[:], g.w_tok).then_inc(s.wt, 16)
                with nc.sync.Fori(0, NZ // 2) as i:
                    for u in range(2):
                        sp.wait_ge(s.ev, NL * (2 * i + u + 2))
                        sp.dma_start(g.z_d[2 * i + u], zb[:, u]).then_inc(s_z[u], 16)
                sp.wait_ge(s.vcp, NT)
                sp.dma_start(g.v_d.rearrange("(n p) c -> p n c", p=P), vb[:]).then_inc(s.st, 16)
                sp.wait_ge(s.z0, 16 * NZ // 2)
                sp.wait_ge(s.z1, 16 * NZ // 2)
                sp.wait_ge(s.st, 16)

            @block.gpsimd
            def _(pool):
                for n in range(NZ + len(REST)):
                    if n >= 2:
                        pool.wait_ge(s.blk, NL * (n - 1))
                    pool.dma_start(w[:, n % 2], g.w_ch[12 + n if n < NZ else REST[n - NZ][0]]).then_inc(s_w[n % 2], 16)

            @block.tensor
            def _(pe):
                def project(u, b, t0, wd):
                    for k in range(KD):
                        last = nc.tensor.matmul(ps[:, b, 0:wd], w[:, u, k], g.hT[:, k, t0:t0 + wd],
                                                start=(k == 0), stop=(k == KD - 1))
                    return last

                with nc.tensor.Fori(0, NZ // 2) as i:
                    for u in range(2):
                        pe.wait_ge(s_w[u], 16 * i + 16)
                        for b, (t0, wd) in enumerate(LB):
                            pe.wait_ge(s.ev, NL * (2 * i + u) + b + 1)
                            project(u, b, t0, wd).then_inc(s.blk, 1)
                ctxs = 0
                for n, (_, _, ctx) in enumerate(REST, NZ):
                    pe.wait_ge(s_w[n % 2], 16 * (n // 2 + 1))
                    if ctx:
                        if ctxs:
                            pe.wait_ge(s.evc, ctxs)
                        project(n % 2, NL, *BLOCKS[0]).then_inc(s.blkc, 1)
                        ctxs += 1
                    for b, (t0, wd) in enumerate(LB):
                        pe.wait_ge(s.ev, NL * n + b + 1)
                        project(n % 2, b, t0, wd).then_inc(s.blk, 1)
                pe.wait_ge(s.wt, 32)
                for i in range(NT):
                    if i >= 2:
                        pe.wait_ge(s.vcp, i - 1)
                        pe.wait_ge(s.acp, i - 1)
                    for k in range(KD):
                        last = nc.tensor.matmul(pt[:, i % 2, 0:2 * P + 16], g.hT[:, k, i * P:(i + 1) * P], wt[:, k],
                                                start=(k == 0), stop=(k == KD - 1))
                    last.then_inc(s.tok, 1)
                    wd = NORM[i][0].shape[-1]
                    pe.wait_ge(s.sq, i + 1)
                    if i:
                        pe.wait_ge(s.root, i)
                    nc.tensor.matmul(pn[:, 0:wd], g.blk, sq[:, i % 2, 0:wd], start=True, stop=True).then_inc(s.sum, 1)

            @block.scalar
            def _(act):
                act.sem_inc(s.ev, NL)
                with nc.scalar.Fori(0, NZ // 2) as i:
                    for u in range(2):
                        act.wait_ge(s_z[u], 16 * i)
                        for b in range(NL):
                            act.wait_ge(s.blk, NL * (2 * i + u) + b + 1)
                            nc.scalar.activation(zb[:, u, b * 512:(b + 1) * 512], ps[:, b], ACT.Silu).then_inc(s.ev, 1)
                ctxs = 0
                for n, (_, dst, ctx) in enumerate(REST, NZ):
                    if ctx:
                        ctxs += 1
                        act.wait_ge(s.blkc, ctxs)
                        nc.scalar.activation(dst[:, 0:CTX], ps[:, NL, 0:CTX], ACT.Copy).then_inc(s.evc, 1)
                    for b, (t0, wd) in enumerate(LB):
                        act.wait_ge(s.blk, NL * n + b + 1)
                        t0 -= 0 if ctx else CTX
                        nc.scalar.activation(dst[:, t0:t0 + wd], ps[:, b], ACT.Copy).then_inc(s.ev, 1)

                def root(i):
                    wd = NORM[i][0].shape[-1]
                    act.wait_ge(s.sum, i + 1)
                    if i >= 2:
                        act.wait_ge(s.nrm, i - 1)
                    nc.scalar.activation(rs[:, i % 2, 0:wd], pn[:, 0:wd], ACT.Sqrt, bias=g.eps[:, 0:1],
                                         scale=1.0 / DH).then_inc(s.root, 1)
                act.wait_ge(s.ev, NL * (NZ + len(REST) + 1))
                act.wait_ge(s.evc, 2)
                for i in range(NT):
                    view, _ = NORM[i]
                    wd = view.shape[-1]
                    if i >= 2:
                        act.wait_ge(s.sum, i - 1)
                    nc.scalar.activation(sq[:, i % 2, 0:wd], view, ACT.Square).then_inc(s.sq, 1)
                    act.wait_ge(s.tok, i + 1)
                    nc.scalar.activation(vb[:, i], pt[:, i % 2, 0:2 * P], ACT.Copy).then_inc(s.vcp, 1)
                    nc.scalar.activation(g.ab[:, i], pt[:, i % 2, 2 * P:2 * P + 16], ACT.Copy).then_inc(s.acp, 1)
                    if i:
                        root(i - 1)
                root(NT - 1)

            @block.vector
            def _(dve):
                dve.wait_ge(s.wt, 32)
                nc.vector.tensor_scalar(nw[:, 0:1], nw[:, 0:1], DH ** -0.5, None, ALU.mult).then_inc(s.rec, 1)

                def norm(i):
                    view, which = NORM[i]
                    wd = view.shape[-1]
                    dve.wait_ge(s.root, i + 1)
                    nc.vector.reciprocal(rs[:, i % 2, 0:wd], rs[:, i % 2, 0:wd]).then_inc(s.rec, 1)
                    dve.wait_ge(s.rec, i + 2)
                    nc.vector.scalar_tensor_tensor(view, view, nw[:, which:which + 1], rs[:, i % 2, 0:wd],
                                                   ALU.mult, ALU.mult).then_inc(s.nrm, 1)
                for i in range(NT):
                    norm(i)


def decays(nc, g):
    with ExitStack() as c:
        par = sbuf(nc, c, "par", [P, 2, 8])
        x, y, t, acc = (sbuf(nc, c, "dec" + n, [P, NT, 8]) for n in "xyta")
        ps = psum(nc, c, "dec_ps", (P, 4, POS * H))
        s = sems(nc, c, "de", "par ea ay beta own sum ex")
        with nc.Block() as block:
            @block.gpsimd
            def _(pool):
                pool.dma_start(par[:, 0], g.a_log.partition_broadcast(P)).then_inc(s.par, 16)
                pool.dma_start(par[:, 1], g.dt_bias.partition_broadcast(P)).then_inc(s.par, 16)

            @block.scalar
            def _(act):
                act.wait_ge(s.par, 32)
                nc.scalar.activation(par[:, 0], par[:, 0], ACT.Exp).then_inc(s.ea, 1)
                act.wait_ge(s.own, 2)
                nc.scalar.activation(y[:], y[:], ACT.Exp, scale=-1.0).then_inc(s.ay, 1)
                act.wait_ge(s.sum, 1)
                for d in range(2):
                    dst = g.begc[:, d], g.esfx[:, d]
                    for j in range(2):
                        nc.scalar.activation(dst[j], ps[:, 2 * d + j].rearrange("p (n h) -> p n h", h=H),
                                             ACT.Exp).then_inc(s.ex, 1)
                nc.scalar.activation(acc[:], g.ab[:, :, 8:16], ACT.Sigmoid).then_inc(s.beta, 1)

            @block.vector
            def _(dve):
                own = Steps(dve, s.own)
                v = nc.vector
                dve.wait_ge(s.par, 32)
                own.done(v.tensor_tensor(x[:], g.ab[:, :, 0:8], par[:, 1:2].broadcast_to([P, NT, 8]), ALU.add))
                own.settle()
                own.done(v.scalar_tensor_tensor(y[:], x[:], -1.0, x[:], ALU.mult, ALU.max))
                own.done(v.tensor_scalar(x[:], x[:], 0.0, None, ALU.max))
                dve.wait_ge(s.ay, 1)
                own.settle()
                own.done(v.tensor_scalar(t[:], y[:], 2.0, None, ALU.add))
                own.settle()
                own.done(v.reciprocal(t[:], t[:]))
                own.settle()
                own.done(v.tensor_tensor(y[:], y[:], t[:], ALU.mult))
                own.settle()
                own.done(v.tensor_tensor(t[:], y[:], y[:], ALU.mult))
                terms = 8
                own.settle()
                own.done(v.tensor_scalar(acc[:], t[:], 2.0 / (2 * terms + 1), 2.0 / (2 * terms - 1), ALU.mult, ALU.add))
                for m in range(terms - 2, -1, -1):
                    own.settle()
                    own.done(v.tensor_tensor(acc[:], acc[:], t[:], ALU.mult))
                    own.settle()
                    own.done(v.tensor_scalar(acc[:], acc[:], 2.0 / (2 * m + 1), None, ALU.add))
                own.settle()
                own.done(v.tensor_tensor(acc[:], acc[:], y[:], ALU.mult))
                own.settle()
                own.done(v.tensor_tensor(x[:], x[:], acc[:], ALU.add))
                own.settle()
                dve.wait_ge(s.ea, 1)
                for d in range(2):
                    own.done(v.scalar_tensor_tensor(g.gd[:, d, 0:NT], x[:, :, d * H:(d + 1) * H], -1.0,
                                                    par[:, 0:1, d * H:(d + 1) * H].broadcast_to([P, NT, H]), ALU.mult, ALU.mult))
                own.settle()
                own.done(v.tensor_copy(g.gd[:, :, NT:POS], g.gd[:, :, 0:CT]))
                dve.wait_ge(s.beta, 1)
                for d in range(2):
                    own.done(v.tensor_copy(g.beta[:, d, 0:NT], acc[:, :, d * H:(d + 1) * H]))
                own.settle()
                own.done(v.tensor_copy(g.beta[:, :, NT:POS], g.beta[:, :, 0:CT]))
                own.settle()
                own.done(v.tensor_tensor(g.begc[:], g.begc[:], g.beta[:], ALU.mult))
                own.settle()

            @block.tensor
            def _(pe):
                pe.wait_ge(s.own, 27)
                for d in range(2):
                    for j in range(2):
                        last = nc.tensor.matmul(ps[:, 2 * d + j], g.dirt(d, j), g.gd[:, d].rearrange("p n h -> p (n h)"),
                                                start=True, stop=True)
                last.then_inc(s.sum, 1)


def delta_rule(nc, g):
    STEPS = NT
    W = H * P
    with ExitStack() as c:
        def two(name):
            return [sbuf(nc, c, f"{name}{d}", [P, H, P]) for d in range(2)]
        lq, lk, lkt, lvt = ([[sbuf(nc, c, f"{n}{d}{u}", [P, H, P]) for u in range(2)] for d in range(2)]
                            for n in ("lq", "lk", "lkt", "lvt"))
        gt, dg, dec, eg, mt, tm, um, xm, qk, qg, kbg, vb, kg, ub, wb, vn, st = map(two, (
            "gt", "dg", "dec", "eg", "mt", "tm", "um", "xm", "qk", "qg", "kbg", "vbd", "kgd", "ub", "wb", "vn", "st"))
        ob = [[sbuf(nc, c, f"ob{d}{u}", [P, H, P]) for u in range(2)] for d in range(2)]
        bank = [[psum(nc, c, f"dr{d}{b}", (P, H, P)) for b in "abcd"] for d in range(2)]
        names = "ld0 ld1 gt dg mat exp kk qkp mt mt1 qkv qk px vx pb vt uw wt ws vn op su sup oe st0 st1 pool z gt2".split()
        s = [sems(nc, c, f"dr{d}", " ".join(names)) for d in range(2)]

        def heads(mask):
            return mask[:, None, :].broadcast_to([P, H, P])

        with nc.Block() as block:
            def pos(d, n):
                return n if d == 0 else n * -1 + (POS - 1)

            def col(t, d, at):
                return t[:, d, bass.ds(at[d], 1)].rearrange("p a h -> p (a h)")[:, :, None].broadcast_to([P, H, P])

            @block.sync
            def _(sp):
                def load(d, at, u):
                    for src, dst in ((g.q_d, lq), (g.k_d, lk), (g.kt_d, lkt), (g.vt_d, lvt)):
                        sp.dma_start(dst[d][u][:], src[at]).then_inc((s[d].ld0, s[d].ld1)[u], 16)

                def store(d, n, at, u):
                    sp.wait_ge(s[d].oe, n + 1)
                    sp.dma_start(g.o_d[d, at], ob[d][u][:]).then_inc((s[d].st0, s[d].st1)[u], 16)
                for u in range(2):
                    for d in range(2):
                        load(d, pos(d, u), u)
                with nc.sync.Fori(0, STEPS // 2 - 1) as i:
                    for u in range(2):
                        for d in range(2):
                            here, ahead = nc.sync.snap(pos(d, 2 * i + u)), nc.sync.snap(pos(d, 2 * i + u + 2))
                            sp.wait_ge(s[d].su, 2 * i + u + 1)
                            load(d, ahead, u)
                            store(d, 2 * i + u, here, u)
                for u in range(2):
                    for d in range(2):
                        store(d, STEPS - 2 + u, pos(d, STEPS - 2 + u), u)
                for d in range(2):
                    sp.wait_ge(s[d].st0, 16 * STEPS // 2)
                    sp.wait_ge(s[d].st1, 16 * STEPS // 2)

            @block.gpsimd
            def _(pool):
                tt = nc.gpsimd.tensor_tensor
                for d in range(2):
                    nc.gpsimd.memset(st[d][:], 0.0).then_inc(s[d].z, 1)

                with nc.gpsimd.Fori(0, STEPS // 2) as i:
                    for u in range(2):
                        n = 2 * i + u
                        at = [nc.gpsimd.snap(pos(d, n)) for d in range(2)]
                        for d in range(2):
                            q = s[d]
                            pool.wait_ge(q.mat, n)
                            tt(dg[d][:], heads(g.ident), col(g.beta, d, at), ALU.mult).then_inc(q.dg, 1)
                        for d in range(2):
                            q = s[d]
                            pool.wait_ge((q.ld0, q.ld1)[u], 64 * i + 64)
                            pool.wait_ge(q.uw, n)
                            tt(kbg[d][:], lkt[d][u][:], col(g.begc, d, at), ALU.mult).then_inc(q.pool, 1)
                            tt(vb[d][:], lvt[d][u][:], col(g.beta, d, at), ALU.mult).then_inc(q.pool, 1)
                            pool.wait_ge(q.su, n)
                            tt(kg[d][:], lkt[d][u][:], col(g.esfx, d, at), ALU.mult).then_inc(q.pool, 1)
                            pool.wait_ge(q.op, n)
                            pool.wait_ge(q.exp, 2 * n + 2)
                            tt(qg[d][:], lq[d][u][:], eg[d][:], ALU.mult).then_inc(q.pool, 1)
                            pool.wait_ge(q.qkv, n + 1)
                            tt(qk[d][:], qk[d][:], heads(g.dirt(d, 0)), ALU.mult).then_inc(q.qk, 1)

            @block.scalar
            def _(act):
                def step(i, u):
                    n = 2 * i + u
                    for d in range(2):
                        q, (A, B, C_, D_) = s[d], bank[d]
                        act.wait_ge(q.mat, n + 1)
                        act.wait_ge(q.qkv, n)
                        nc.scalar.activation(dec[d][:], A[:], ACT.Exp).then_inc(q.exp, 1)
                        act.wait_ge(q.sup, n)
                        act.wait_ge(q.pool, 4 * n)
                        nc.scalar.activation(eg[d][:], B[:], ACT.Exp).then_inc(q.exp, 1)
                    for d in range(2):
                        q, (A, B, C_, D_) = s[d], bank[d]
                        act.wait_ge(q.uw, n + 1)
                        act.wait_ge(q.vn, n)
                        nc.scalar.activation(ub[d][:], D_[:], ACT.Copy).then_inc(q.wt, 1)
                        act.wait_ge(q.ws, n)
                        nc.scalar.activation(wb[d][:], A[:], ACT.Copy).then_inc(q.wt, 1)
                    for d in range(2):
                        q, (A, B, C_, D_) = s[d], bank[d]
                        act.wait_ge(q.op, n + 1)
                        act.wait_ge((q.st0, q.st1)[u], 16 * i)
                        nc.scalar.activation(ob[d][u][:], C_[:], ACT.Copy).then_inc(q.oe, 1)

                with nc.scalar.Fori(0, STEPS // 2) as i:
                    for u in range(2):
                        step(i, u)

            @block.tensor
            def _(pe):
                def each(out, lhs, rhs):
                    for h in range(H):
                        last = nc.tensor.matmul(out[:, h], lhs[:, h], g.ident if rhs is None else rhs[:, h], start=True, stop=True)
                    return last

                with nc.tensor.Fori(0, STEPS // 2) as i:
                    for u in range(2):
                        n = 2 * i + u
                        for d in range(2):
                            q, (A, B, C_, D_) = s[d], bank[d]
                            flat = gt[d][:].rearrange("p h i -> p (h i)")
                            pe.wait_ge(q.gt, n + 1)
                            pe.wait_ge(q.dg, n + 1)
                            pe.wait_ge(q.wt, 2 * n)
                            pe.wait_ge(q.vn, n)
                            pe.wait_ge(q.oe, n)
                            nc.tensor.matmul(A[:].rearrange("p h i -> p (h i)"), g.dirt(d, 1), flat, start=True, stop=True)
                            nc.tensor.matmul(B[:].rearrange("p h i -> p (h i)"), g.ones, flat, start=True, stop=True)
                            nc.tensor.matmul(C_[:].rearrange("p h i -> p (h i)"), g.dirt(d, 1),
                                             dg[d][:].rearrange("p h i -> p (h i)"), start=True, stop=True).then_inc(q.mat, 1)
                            pe.wait_ge((q.ld0, q.ld1)[u], 64 * i + 64)
                            pe.wait_ge(q.sup, n)
                            each(D_, lk[d][u], lk[d][u]).then_inc(q.kk, 1)
                        for d in range(2):
                            q, (A, B, C_, D_) = s[d], bank[d]
                            pe.wait_ge(q.exp, 2 * n + 2)
                            each(A, lk[d][u], lq[d][u]).then_inc(q.qkp, 1)
                        for d in range(2):
                            q, (A, B, C_, D_) = s[d], bank[d]
                            pe.wait_ge(q.mt, n + 1)
                            each(B, mt[d], None).then_inc(q.px, 1)
                        for lev in range(1, N_LEV):
                            for d in range(2):
                                q, (A, B, C_, D_) = s[d], bank[d]
                                pe.wait_ge(q.vt, N_LEV * n + lev)
                                if lev == 1:
                                    pe.wait_ge(q.qkv, n + 1)
                                each(A, mt[d], tm[d]).then_inc(q.px, 1)
                            for d in range(2):
                                q, (A, B, C_, D_) = s[d], bank[d]
                                pe.wait_ge(q.vx, (N_LEV - 1) * n + lev)
                                if lev < N_LEV - 1:
                                    each(B, um[d], xm[d])
                                each(C_, xm[d], um[d]).then_inc(q.pb, 1)
                        for d in range(2):
                            q, (A, B, C_, D_) = s[d], bank[d]
                            pe.wait_ge(q.vt, N_LEV * n + N_LEV)
                            pe.wait_ge(q.pool, 4 * n + 2)
                            each(D_, um[d], vb[d])
                            each(A, kbg[d], um[d]).then_inc(q.uw, 1)
                        for d in range(2):
                            q, (A, B, C_, D_) = s[d], bank[d]
                            pe.wait_ge(q.wt, 2 * n + 2)
                            pe.wait_ge(q.sup, n)
                            pe.wait_ge(q.z, 1)
                            each(B, wb[d], st[d]).then_inc(q.ws, 1)
                        for d in range(2):
                            q, (A, B, C_, D_) = s[d], bank[d]
                            pe.wait_ge(q.vn, n + 1)
                            pe.wait_ge(q.pool, 4 * n + 4)
                            pe.wait_ge(q.qk, n + 1)
                            for h in range(H):
                                nc.tensor.matmul(C_[:, h], st[d][:, h], qg[d][:, h], start=True, stop=False)
                                last = nc.tensor.matmul(C_[:, h], vn[d][:, h], qk[d][:, h], start=False, stop=True)
                            last.then_inc(q.op, 1)
                            each(D_, kg[d], vn[d]).then_inc(q.su, 1)

            @block.vector
            def _(dve):
                v = nc.vector
                with nc.vector.Fori(0, STEPS // 2) as i:
                    for u in range(2):
                        n = 2 * i + u
                        at = [nc.vector.snap(pos(d, n)) for d in range(2)]
                        for d in range(2):
                            q = s[d]
                            dve.wait_ge(q.mat, n)
                            v.tensor_tensor(gt[d][:], heads(g.dirt(d, 0)), col(g.gd, d, at), ALU.mult).then_inc(q.gt, 1)
                        for d in range(2):
                            q, (A, B, C_, D_) = s[d], bank[d]
                            dve.wait_ge(q.exp, 2 * n + 2)
                            dve.wait_ge(q.px, N_LEV * n)
                            v.tensor_tensor(mt[d][:], dec[d][:], C_[:], ALU.mult).then_inc(q.mt1, 1)
                            dve.wait_ge(q.mt1, n + 1)
                            dve.wait_ge(q.kk, n + 1)
                            v.tensor_tensor(mt[d][:], mt[d][:], D_[:], ALU.mult).then_inc(q.mt, 1)
                        for d in range(2):
                            q, (A, B, C_, D_) = s[d], bank[d]
                            dve.wait_ge(q.qkp, n + 1)
                            dve.wait_ge(q.op, n)
                            v.tensor_tensor(qk[d][:], A[:], dec[d][:], ALU.mult).then_inc(q.qkv, 1)
                        for d in range(2):
                            q, (A, B, C_, D_) = s[d], bank[d]
                            dve.wait_ge(q.uw, n)
                            dve.wait_ge(q.mt, n + 1)
                            own = Steps(dve, q.gt2, 2 * n)
                            own.done(v.tensor_tensor(um[d][:], mt[d][:], heads(g.level(1 - d, 0)), ALU.mult))
                            dve.wait_ge(q.px, N_LEV * n + 1)
                            own.done(v.tensor_tensor(tm[d][:], B[:], heads(g.level(d, 0)), ALU.mult))
                            own.settle()
                            v.scalar_tensor_tensor(um[d][:], um[d][:], -1.0, heads(g.ident), ALU.mult, ALU.add)
                            v.scalar_tensor_tensor(tm[d][:], tm[d][:], -1.0, heads(g.ident), ALU.mult, ALU.add).then_inc(q.vt, 1)
                        for lev in range(1, N_LEV):
                            for d in range(2):
                                q, (A, B, C_, D_) = s[d], bank[d]
                                dve.wait_ge(q.px, N_LEV * n + lev + 1)
                                v.tensor_tensor(xm[d][:], A[:], heads(g.level(d, lev)), ALU.mult).then_inc(q.vx, 1)
                            for d in range(2):
                                q, (A, B, C_, D_) = s[d], bank[d]
                                dve.wait_ge(q.pb, (N_LEV - 1) * n + lev)
                                if lev < N_LEV - 1:
                                    v.tensor_tensor(tm[d][:], tm[d][:], B[:], ALU.subtract)
                                v.tensor_tensor(um[d][:], um[d][:], C_[:], ALU.subtract).then_inc(q.vt, 1)
                        for d in range(2):
                            q, (A, B, C_, D_) = s[d], bank[d]
                            dve.wait_ge(q.ws, n + 1)
                            dve.wait_ge(q.su, n)
                            v.tensor_tensor(vn[d][:], ub[d][:], B[:], ALU.subtract).then_inc(q.vn, 1)
                        for d in range(2):
                            q, (A, B, C_, D_) = s[d], bank[d]
                            last_tok = P - 1 if d == 0 else 0
                            dve.wait_ge(q.su, n + 1)
                            for h in range(H):
                                last = v.scalar_tensor_tensor(st[d][:, h], st[d][:, h], eg[d][:, h, last_tok:last_tok + 1],
                                                              D_[:, h], ALU.mult, ALU.add)
                            last.then_inc(q.sup, 1)


def wait(eng, sem, value):
    if not isinstance(value, int) or value > 0:
        eng.wait_ge(sem, value)


def attention(nc, g):
    UNITS = ROWS * HP
    LOC = WR * GRID
    KEYS = LOC + CTX
    KT = KEYS // P
    FREE = g.hT.rearrange("p k t -> p (k t)")
    v0 = FREE[:, 0:NT * 2 * P].rearrange("p (n c) -> p n c", c=2 * P)
    v1 = FREE[:, NT * 2 * P:(NT + LT - 1) * 2 * P].rearrange("p (n c) -> p n c", c=2 * P)
    first_in, last_in = WR // 4, (ROWS - WR // 2) // 2

    def place(i, k):
        odd, hp = k // 2, k % 2
        r = 2 * i + odd
        if isinstance(i, int):
            rs = min(max(r - WR // 2, 0), ROWS - WR)
            shift = r - rs
            vi = (rs - rs % 2) // 2
            return r, rs, vi, rs % 2, WR - 1 - shift
        return r, r - WR // 2, i - WR // 4, odd, WR - 1 - WR // 2

    def units(eng, body):
        for i in range(first_in + 1):
            for k in range(4):
                body(i, k)
        with eng.Fori(first_in + 1, last_in) as i:
            for k in range(4):
                body(i, k)
        for i in range(last_in, ROWS // 2):
            for k in range(4):
                body(i, k)

    def early(i, k, n):
        return isinstance(i, int) and 4 * i + k < n

    def back(i, k, n):
        return (i, k - n) if k >= n else (i - 1, k - n + 4)

    with ExitStack() as c:
        rpad = sbuf(nc, c, "rpad", [H * 15, 127])
        bt = sbuf(nc, c, "bt", [P, HP, 15, GRID])
        qb = sbuf(nc, c, "qb", [P, 2, 2 * GRID])
        sb = sbuf(nc, c, "scores", [P, 2, KEYS])
        pb = sbuf(nc, c, "probs", [P, 2, KEYS])
        pt = sbuf(nc, c, "probs_t", [P, 2, KT, P])
        mx = sbuf(nc, c, "mx", [P, 2, 4])
        ob = sbuf(nc, c, "ao", [P, 2, P])
        oc = sbuf(nc, c, "aoT", [P, 2, HP, GRID])
        loc = psum(nc, c, "loc_ps", (P, 2, 512))
        cx = psum(nc, c, "cx_ps", (P, 2, 512))
        tp = psum(nc, c, "tp_ps", (P, 2, 512))
        po = psum(nc, c, "po_ps")
        pot = psum(nc, c, "pot_ps")
        s = sems(nc, c, "at", "v pad z rp sk bt0 qb sc cx add mx nm ex rc tp ptd pta o oe ot ote st0 st1")
        s_st = [s.st0, s.st1]
        with nc.Block() as block:
            @block.sync
            def _(sp):
                sp.dma_start(v0, g.v_d.rearrange("(n p) c -> p n c", p=P)).then_inc(s.v, 16)
                sp.dma_start(v1, g.v_d[CTX + GRID:T - GRID].rearrange("(n p) c -> p n c", p=P)).then_inc(s.v, 16)
                sp.wait_ge(s.z, 1)
                sp.dma_start(rpad[:, 48:79], g.rpb).then_inc(s.rp, 16)
                sp.wait_ge(s.rp, 16)
                sp.dma_start(g.skew_d, rpad[:, None, :].broadcast_to([H * 15, GRID, 127])).then_inc(s.sk, 16)
                sp.wait_ge(s.sk, 16)
                for h in range(H):
                    src = g.skew_d[h * 15:(h + 1) * 15].rearrange("r j c -> r (j c)")
                    src = src[:, 63:63 + GRID * 126].rearrange("r (j c) -> j r c", c=126)[:, :, 0:GRID]
                    half = h % 2
                    sp.dma_start(bt[half * GRID:(half + 1) * GRID, h // 2], src).then_inc(s.bt0, 16)

                dst = g.oc_d.rearrange("(q p) (r t) -> p r q t", q=HP, t=GRID)

                def store(i, odd):
                    r = 2 * i + odd
                    sp.wait_ge(s.ote, 2 * (4 * i + 2 * odd + 2))
                    sp.dma_start(dst[:, bass.ds(r, 1)].rearrange("p r q t -> p (r q) t"), oc[:, odd]).then_inc(s_st[odd], 16)
                with nc.sync.Fori(0, ROWS // 2) as i:
                    for odd in range(2):
                        store(i, odd)
                for sem in s_st:
                    sp.wait_ge(sem, 8 * ROWS)

            @block.gpsimd
            def _(pool):
                nc.gpsimd.memset(rpad[:], 0.0).then_inc(s.z, 1)

                def body(i, k):
                    U = 4 * i + k
                    r = place(i, k)[0]
                    at = r * GRID if isinstance(i, int) else nc.gpsimd.snap(r * GRID)
                    wait(pool, s.sc, U - 1)
                    nc.gpsimd.tensor_tensor(qb[:, k % 2].rearrange("p (a t) -> p a t", a=2),
                                            g.qn[:, k % 2, bass.ds(at, GRID)][:, None, :].broadcast_to([P, 2, GRID]),
                                            g.blk.rearrange("p (a t) -> p a t", a=2), ALU.mult).then_inc(s.qb, 1)
                units(nc.gpsimd, body)

            @block.tensor
            def _(pe):
                def scores(i, k):
                    U, u = 4 * i + k, k % 2
                    _, rs, _, _, _ = place(i, k)
                    pe.wait_ge(s.qb, U + 1)
                    wait(pe, s.add, U - 1)
                    wait(pe, s.cx, U - 1)
                    nc.tensor.matmul(loc[:, u, 0:LOC], qb[:, u], g.kn[:, k % 2, bass.ds(CTX + rs * GRID, LOC)], start=True, stop=True)
                    nc.tensor.matmul(cx[:, u, 0:CTX], qb[:, u], g.kn[:, k % 2, 0:CTX], start=True, stop=True).then_inc(s.sc, 1)

                def turn(i, k):
                    U, u = 4 * i + k, k % 2
                    pe.wait_ge(s.ex, U + 1)
                    for b in range(2):
                        wait(pe, (s.ptd, s.pta)[b], U)
                        for j in range(KT // 2):
                            n = b * (KT // 2) + j
                            last = nc.tensor.transpose(tp[:, b, j * P:(j + 1) * P], pb[:, u, n * P:(n + 1) * P], g.ident)
                        last.then_inc(s.tp, 1)

                def values(i, k):
                    U, u, hp = 4 * i + k, k % 2, k % 2
                    _, _, vi, shifted, _ = place(i, k)
                    pe.wait_ge(s.ptd, U + 1)
                    pe.wait_ge(s.pta, U + 1)
                    wait(pe, s.oe, U)
                    cols = slice(hp * P, (hp + 1) * P)
                    for n in range(KT):
                        if n < KT - CT:
                            v = v1[:, bass.ds(vi + n, 1), cols] if shifted else v0[:, bass.ds(vi + n + CT, 1), cols]
                            v = v.rearrange("p a c -> p (a c)")
                        else:
                            v = v0[:, n - (KT - CT), cols]
                        last = nc.tensor.matmul(po[:, 0:P], pt[:, u, n], v, start=(n == 0), stop=(n == KT - 1))
                    last.then_inc(s.o, 1)

                def turn_out(i, k):
                    U, u = 4 * i + k, k % 2
                    pe.wait_ge(s.oe, U + 1)
                    wait(pe, s.ote, 2 * U)
                    nc.tensor.transpose(pot[:, 0:P], ob[:, u], g.ident).then_inc(s.ot, 1)

                def body(i, k):
                    scores(i, k)
                    if not early(i, k, 1):
                        turn(*back(i, k, 1))
                    if not early(i, k, 2):
                        turn_out(*back(i, k, 2))
                    if not early(i, k, 1):
                        values(*back(i, k, 1))
                pe.wait_ge(s.v, 32)
                units(nc.tensor, body)
                end = ROWS // 2 - 1
                turn(end, 3)
                turn_out(end, 2)
                values(end, 3)
                turn_out(end, 3)

            @block.scalar
            def _(act):
                def context(i, k):
                    U, u = 4 * i + k, k % 2
                    act.wait_ge(s.sc, U + 1)
                    wait(act, s.ex, U - 1)
                    nc.scalar.activation(sb[:, u, LOC:KEYS], cx[:, u, 0:CTX], ACT.Copy).then_inc(s.cx, 1)

                def exps(i, k):
                    U, u = 4 * i + k, k % 2
                    act.wait_ge(s.nm, U + 1)
                    wait(act, s.tp, 2 * (U - 1))
                    wait(act, s.rc, U - 1)
                    nc.scalar.activation(pb[:, u], sb[:, u], ACT.Exp, bias=mx[:, u, 1:2], accum_out=mx[:, u, 2:3]).then_inc(s.ex, 1)

                def copy_pt(i, k):
                    U, u = 4 * i + k, k % 2
                    act.wait_ge(s.tp, 2 * U + 2)
                    wait(act, s.o, U - 1)
                    nc.scalar.activation(pt[:, u, KT // 2:KT], tp[:, 1, 0:KT // 2 * P].rearrange("p (n c) -> p n c", c=P), ACT.Copy).then_inc(s.pta, 1)

                def out(i, k):
                    U, u = 4 * i + k, k % 2
                    act.wait_ge(s.o, U + 1)
                    act.wait_ge(s.rc, U + 1)
                    wait(act, s.ot, U - 1)
                    nc.scalar.activation(ob[:, u], po[:, 0:P], ACT.Copy, scale=mx[:, u, 3:4]).then_inc(s.oe, 1)

                def out_t(i, k):
                    U, odd, hp = 4 * i + k, k // 2, k % 2
                    act.wait_ge(s.ot, U + 1)
                    wait(act, s_st[odd], 16 * i)
                    for a in range(2):
                        half = slice(a * DH, (a + 1) * DH)
                        nc.scalar.activation(oc[half, odd, hp], pot[half, half], ACT.Copy).then_inc(s.ote, 1)

                def body(i, k):
                    context(i, k)
                    if not early(i, k, 1):
                        copy_pt(*back(i, k, 1))
                    if not early(i, k, 2):
                        out_t(*back(i, k, 2))
                    exps(i, k)
                    if not early(i, k, 1):
                        out(*back(i, k, 1))
                units(nc.scalar, body)
                end = ROWS // 2 - 1
                copy_pt(end, 3)
                out_t(end, 2)
                out(end, 3)
                out_t(end, 3)

            @block.vector
            def _(dve):
                v = nc.vector

                def softmax(i, k):
                    U, u = 4 * i + k, k % 2
                    dr = place(i, k)[4]
                    dve.wait_ge(s.sc, U + 1)
                    wait(dve, s.ex, U - 1)
                    v.tensor_tensor(sb[:, u, 0:LOC], loc[:, u, 0:LOC], bt[:, k % 2, dr:dr + WR].rearrange("p r c -> p (r c)"),
                                    ALU.add).then_inc(s.add, 1)
                    dve.wait_ge(s.add, U + 1)
                    dve.wait_ge(s.cx, U + 1)
                    v.reduce_max(mx[:, u, 0:1], sb[:, u], AX_X).then_inc(s.mx, 1)
                    dve.wait_ge(s.mx, U + 1)
                    v.tensor_scalar(mx[:, u, 1:2], mx[:, u, 0:1], -1.0, None, ALU.mult).then_inc(s.nm, 1)

                def rest(i, k):
                    U, u = 4 * i + k, k % 2
                    dve.wait_ge(s.ex, U + 1)
                    wait(dve, s.oe, U - 1)
                    v.reciprocal(mx[:, u, 3:4], mx[:, u, 2:3]).then_inc(s.rc, 1)
                    dve.wait_ge(s.tp, 2 * U + 1)
                    wait(dve, s.o, U - 1)
                    v.tensor_copy(pt[:, u, 0:KT // 2], tp[:, 0, 0:KT // 2 * P].rearrange("p (n c) -> p n c", c=P)).then_inc(s.ptd, 1)

                def body(i, k):
                    softmax(i, k)
                    if not early(i, k, 1):
                        rest(*back(i, k, 1))
                dve.wait_ge(s.bt0, 64)
                for hp in range(HP):
                    v.tensor_tensor(bt[:, hp], bt[:, hp], g.window[:, None, :].broadcast_to([P, 15, GRID]), ALU.add).then_inc(s.pad, 1)
                dve.wait_ge(s.pad, 2)
                units(nc.vector, body)
                rest(ROWS // 2 - 1, 3)


def fourier(nc, g):
    N1, N2 = P, SEQ // P
    LO = P // N2
    HI = N1 // LO
    FREE = g.hT.rearrange("p k t -> p (k t)")
    ab = FREE[:, 0:2 * N2 * FN].rearrange("p (s n c) -> p s n c", s=2, n=N2)
    zin = FREE[:, 2 * N2 * FN:4 * N2 * FN].rearrange("p (s h c) -> p s h c", s=2, h=HI)
    CH = N2 // 2
    with ExitStack() as c:
        ft = sbuf(nc, c, "ft", [P, F_W])
        zc = sbuf(nc, c, "zc", [P, 2, 4, 512])
        zs = sbuf(nc, c, "zs", [P, 2, 2, 512])
        y = sbuf(nc, c, "yf", [P, 2, 512])
        ybt = sbuf(nc, c, "ybt", [P, 2, SEQ])
        pa = psum(nc, c, "fa_ps", (P, 2, 512))
        pz = psum(nc, c, "fz_ps", (P, 2, 2, 512))
        pq = psum(nc, c, "fq_ps", (P, 2, 512))
        s = sems(nc, c, "fo", "ft pa ae pz m zz zst0 zst1 re py ye pq qe st")
        c4 = ft[:, F_C4:F_C4 + FN]
        dft = [ft[:, F_N1 + j * P:F_N1 + (j + 1) * P] for j in range(3)]
        twc, tws = (ft[:, F_TW + j * N2:F_TW + (j + 1) * N2] for j in range(2))
        k2c, k2s = (ft[:, F_K2 + j * P:F_K2 + (j + 1) * P] for j in range(2))
        with nc.Block() as block:
            @block.sync
            def _(sp):
                sp.dma_start(ft[:], g.ftab).then_inc(s.ft, 16)
                for q in range(CH):
                    sp.wait_ge(s.zz, 2 * q + 2)
                    sp.dma_start(g.z2_d[:, :, 2 * q:2 * q + 2].rearrange("s k n c -> k s (n c)"), zs[:, q % 2]).then_inc((s.zst0, s.zst1)[q % 2], 16)
                sp.wait_ge(s.zst0, 16 * CH // 2)
                sp.wait_ge(s.zst1, 16 * CH // 2)
                for n in range(N2):
                    for j in range(2):
                        sp.dma_start(zin[n * LO:(n + 1) * LO, j], g.z2_d[j, :, n].rearrange("(h l) c -> l h c", l=LO)).then_inc(s.re, 16)
                sp.wait_ge(s.qe, 2 * HI // 2)
                sp.dma_start(g.yb_d.rearrange("(a p) t -> p a t", p=P), ybt[:]).then_inc(s.st, 16)
                sp.wait_ge(s.st, 16)

            @block.tensor
            def _(pe):
                pe.wait_ge(s.ft, 16)
                for n in range(N2):
                    wait(pe, s.ae, n - 1)
                    for cc in range(2):
                        last = nc.tensor.matmul(pa[:, n % 2, cc * FN:(cc + 1) * FN], g.uT[:, cc, n:SEQ:N2], c4, start=True, stop=True)
                    last.then_inc(s.pa, 1)
                pe.wait_ge(s.ae, N2)
                for q in range(CH):
                    wait(pe, s.m, 4 * (q - 1))
                    a, b = (ab[:, j, 2 * q:2 * q + 2].rearrange("p n c -> p (n c)") for j in range(2))
                    re, im = pz[:, q % 2, 0], pz[:, q % 2, 1]
                    nc.tensor.matmul(re, dft[0], a, start=True, stop=False)
                    nc.tensor.matmul(re, dft[2], b, start=False, stop=True)
                    nc.tensor.matmul(im, dft[0], b, start=True, stop=False)
                    nc.tensor.matmul(im, dft[1], a, start=False, stop=True).then_inc(s.pz, 1)
                pe.wait_ge(s.re, 16 * 2 * N2)
                for q in range(HI // 2 + 1):
                    if q < HI // 2:
                        wait(pe, s.ye, q - 1)
                        for j in range(2):
                            last = nc.tensor.matmul(pa[:, q % 2], (k2c, k2s)[j], zin[:, j, 2 * q:2 * q + 2].rearrange("p h c -> p (h c)"),
                                                    start=(j == 0), stop=(j == 1))
                        last.then_inc(s.py, 1)
                    if q:
                        r = q - 1
                        pe.wait_ge(s.ye, r + 1)
                        wait(pe, s.qe, 2 * (r - 1))
                        for j in range(4):
                            last = nc.tensor.transpose(pq[:, r % 2, j * P:(j + 1) * P], y[:, r % 2, j * P:(j + 1) * P], g.ident)
                        last.then_inc(s.pq, 1)

            @block.scalar
            def _(act):
                for n in range(N2):
                    act.wait_ge(s.pa, n + 1)
                    nc.scalar.activation(ab[:, :, n].rearrange("p s (a x) -> p a s x", a=2),
                                         pa[:, n % 2].rearrange("p (a s x) -> p a s x", a=2, s=2), ACT.Copy).then_inc(s.ae, 1)
                for q in range(HI // 2):
                    act.wait_ge(s.py, q + 1)
                    wait(act, s.pq, q - 1)
                    nc.scalar.activation(y[:, q % 2], pa[:, q % 2], ACT.Copy).then_inc(s.ye, 1)

            @block.vector
            def _(dve):
                v = nc.vector
                for q in range(CH):
                    u = q % 2
                    dve.wait_ge(s.pz, q + 1)
                    wait(dve, s.zz, 2 * (q - 1))
                    tw = [t[:, 2 * q:2 * q + 2, None].broadcast_to([P, 2, FN]) for t in (twc, tws)]
                    for j, (part, t) in enumerate(((0, 0), (1, 1), (1, 0), (0, 1))):
                        v.tensor_tensor(zc[:, u, j].rearrange("p (n c) -> p n c", n=2), pz[:, u, part].rearrange("p (n c) -> p n c", n=2),
                                        tw[t], ALU.mult).then_inc(s.m, 1)
                for q in range(HI // 2):
                    dve.wait_ge(s.pq, q + 1)
                    for j in range(2):
                        k1 = (2 * q + j) * LO
                        out = ybt[:].rearrange("p a (k t) -> p a k t", t=N1)[:, :, :, k1:k1 + LO]
                        v.tensor_copy(out, pq[:, q % 2, j * FN:(j + 1) * FN].rearrange("p (a k t) -> p a k t", a=2, t=LO)).then_inc(s.qe, 1)

            @block.gpsimd
            def _(pool):
                for q in range(CH):
                    u = q % 2
                    pool.wait_ge(s.m, 4 * q + 4)
                    wait(pool, (s.zst0, s.zst1)[u], 16 * (q // 2))
                    nc.gpsimd.tensor_tensor(zs[:, u, 0], zc[:, u, 0], zc[:, u, 1], ALU.subtract).then_inc(s.zz, 1)
                    nc.gpsimd.tensor_tensor(zs[:, u, 1], zc[:, u, 2], zc[:, u, 3], ALU.add).then_inc(s.zz, 1)


def merge(nc, g):
    NBK = SEQ // 512
    BT = 512 // P
    NBR = 3
    NC = NBR + 1
    WB = NBR
    BRANCH = [(0, H), (H, H + 2), (H + 2, KD)]
    with ExitStack() as c:
        hb = sbuf(nc, c, "hb", [P, KD, 512])
        of = sbuf(nc, c, "of", [P, 2, BT * H * P])
        zt = sbuf(nc, c, "zt", [P, H, 512])
        ob = sbuf(nc, c, "obr", [P, KD, 512])
        hh, hl, oh, ol = (sbuf(nc, c, n, [P, KD, 512], F32R) for n in ("hb_high", "hb_low", "obr_high", "obr_low"))
        w = sbuf(nc, c, "wm", [P, NC, KD * P])
        wh, wl = (sbuf(nc, c, n, [P, NC, KD * P], F32R) for n in ("wm_high", "wm_low"))
        gnw = sbuf(nc, c, "gnw", [P, 1])
        sg = sbuf(nc, c, "sg", [P, NBR, 512])
        pr = sbuf(nc, c, "prm", [P, NBR, 512])
        yb = sbuf(nc, c, "yTb", [P, 2, 512])
        pg = [psum(nc, c, f"pg{n}") for n in range(NBR)]
        pbr = [psum(nc, c, f"pbr{n}") for n in range(NBR)]
        pn = [psum(nc, c, f"pnm{n}") for n in range(2)]
        s = sems(nc, c, "me", "cst ldo ldh w0 w1 w2 w3 wh wl hh hl oh ol osum sq sum root rec oa gate sig br prod add y y0 y1 held")
        s_w, s_y = [s.w0, s.w1, s.w2, s.w3], [s.y0, s.y1]
        scans = [of[:, d].rearrange("p (b h i) -> p b h i", b=BT, h=H) for d in range(2)]
        roots, squares = (of[:, d].rearrange("p (h t) -> p h t", h=H) for d in range(2))
        SIG0, PROD0, WL0 = NBR, NBR, NC

        def blocks(eng, block):
            with eng.Fori(0, NBK - 1) as b:
                block(b, True)
            block(NBK - 1, False)

        def tiles(eng, b, more, tile):
            for u in range(2):
                tile(b * KD + u, u, u == 0, None, False)
            with eng.Fori(1, KD // 2 - 1) as jj:
                for u in range(2):
                    tile(b * KD + jj * 2 + u, u, False, None, False)
            for u in range(2):
                tile(b * KD + KD - 2 + u, u, False, u if more else None, not more and u == 1)

        with nc.Block() as block:
            @block.sync
            def _(sp):
                sp.dma_start(gnw[:], g.gdn_norm).then_inc(s.cst, 16)
                with nc.sync.Fori(0, NBK) as b:
                    with nc.sync.Fori(0, KD) as j:
                        m = b * KD + j
                        at = nc.sync.snap(j + 0)
                        for n in range(NC):
                            sp.wait_ge(s.wl, NC * m + n + 1)
                            sp.dma_start(w[:, n], g.w_br[at] if n == WB else g.w_gates[at, :, n]).then_inc(s_w[n], 16)

            @block.gpsimd
            def _(pool):
                def load_delta(b):
                    pos, t0 = b * BT + CT, b * 512
                    for d in range(2):
                        pool.dma_start(scans[d], g.o_d[d, bass.ds(pos, BT)].rearrange("n p h c -> p n h c")).then_inc(s.ldo, 16)
                    pool.dma_start(zt[:], g.z_d[:, :, bass.ds(t0, 512)].rearrange("h p t -> p h t")).then_inc(s.ldo, 16)

                def load_rest(b):
                    t0 = b * 512
                    pool.dma_start(hb[:], g.h_d[:, :, bass.ds(t0 + CTX, 512)]).then_inc(s.ldh, 16)
                    pool.dma_start(ob[:, H:H + 2], g.yb_d[:, bass.ds(t0, 512)].rearrange("(a p) t -> p a t", p=P)).then_inc(s.ldh, 16)
                    pool.dma_start(ob[:, H + 2:KD], g.oc_d[:, bass.ds(t0, 512)].rearrange("(a p) t -> p a t", p=P)).then_inc(s.ldh, 16)

                def stores(b):
                    t0 = b * 512 if isinstance(b, int) else nc.gpsimd.snap(b * 512)
                    with nc.gpsimd.Fori(0, KD // 2) as jj:
                        for u in range(2):
                            j = nc.gpsimd.snap(jj * 2 + u)
                            pool.wait_ge(s.y, b * KD + jj * 2 + u + 1)
                            hold(pool, s.held)
                            pool.dma_start(g.y_d[:, bass.ds(j, 1), bass.ds(t0, 512)].rearrange("p a t -> p (a t)"), yb[:, u]).then_inc(s_y[u], 16)
                load_delta(0)
                load_rest(0)
                with nc.gpsimd.Fori(0, NBK - 1) as b:
                    ahead = nc.gpsimd.snap(b + 1)
                    pool.wait_ge(s.oa, b + 1)
                    hold(pool, s.held)
                    load_delta(ahead)
                    pool.wait_ge(s.ol, KD * (b + 1))
                    hold(pool, s.held)
                    load_rest(ahead)
                    stores(b)
                stores(NBK - 1)
                for u in range(2):
                    pool.wait_ge(s_y[u], 16 * NBK * KD // 2)

            @block.tensor
            def _(pe):
                def sums(b, heads):
                    pe.wait_ge(s.sq, b + 1)
                    for h in heads:
                        wait(pe, s.root, H * b + h - 1)
                        nc.tensor.matmul(pn[h % 2][:], g.ones, squares[:, h], start=True, stop=True).then_inc(s.sum, 1)

                def product(bank, n, rights, ks, split, b):
                    rh, rl = rights
                    for k in ks:
                        if split is not None:
                            pe.wait_ge(split, KD * b + k + 1)
                        high, low = (x[:, n, k * P:(k + 1) * P] for x in (wh, wl))
                        nc.tensor.matmul(bank[:], high, rh[:, k], start=(k == ks[0]), stop=False)
                        nc.tensor.matmul(bank[:], high, rl[:, k], start=False, stop=False)
                        last = nc.tensor.matmul(bank[:], low, rh[:, k], start=False, stop=(k == ks[-1]))
                    return last

                def block(b, more):
                    def tile(m, u, first, near, last):
                        for br in range(NBR):
                            pe.wait_ge(s.wl, NC * m + br + 1 + WL0)
                            pe.wait_ge(s.sig, NBR * m + br + 1)
                            product(pg[br], br, (hh, hl), range(KD), s.hl if first and br == 0 else None, b).then_inc(s.gate, 1)
                            if br == 0:
                                pe.wait_ge(s.wl, NC * m + WB + 1 + WL0)
                            pe.wait_ge(s.prod, NBR * m + br + 1)
                            product(pbr[br], WB, (oh, ol), range(*BRANCH[br]), s.ol if first else None, b).then_inc(s.br, 1)
                            if near == 0 and br < 2:
                                sums(b + 1, (2 * br, 2 * br + 1))
                    tiles(nc.tensor, b, more, tile)
                sums(0, range(H))
                blocks(nc.tensor, block)

            @block.scalar
            def _(act):
                act.sem_inc(s.sig, SIG0)
                a = nc.scalar.activation

                def square(b):
                    act.wait_ge(s.osum, b + 1)
                    a(squares, ob[:, 0:H], ACT.Square).then_inc(s.sq, 1)

                def root(b, heads):
                    for h in heads:
                        act.wait_ge(s.sum, H * b + h + 1)
                        a(roots[:, h], pn[h % 2][:], ACT.Sqrt, bias=g.eps[:, 0:1], scale=1.0 / DK).then_inc(s.root, 1)

                def high_chunk(m, n):
                    act.wait_ge(s_w[n], 16 * m + 16)
                    a(wh[:, n], w[:, n], ACT.Copy).then_inc(s.wh, 1)

                def high_h(b):
                    act.wait_ge(s.ldh, 48 * b + 48)
                    for k in range(KD):
                        a(hh[:, k], hb[:, k], ACT.Copy).then_inc(s.hh, 1)

                def high_o(b):
                    act.wait_ge(s.oa, b + 1)
                    for k in range(KD):
                        a(oh[:, k], ob[:, k], ACT.Copy).then_inc(s.oh, 1)

                def block(b, more):
                    def tile(m, u, first, near, last):
                        if near == 0:
                            square(b + 1)
                        for br in range(NBR):
                            act.wait_ge(s.gate, NBR * m + br + 1)
                            act.wait_ge(s.prod, NBR * m + br + 1)
                            a(sg[:, br], pg[br][:], ACT.Sigmoid).then_inc(s.sig, 1)
                            if not last:
                                high_chunk(m + 1, br)
                            if near == 0 and br > 0:
                                root(b + 1, (2 * br - 2, 2 * br - 1))
                        if near == 1:
                            high_h(b + 1)
                        if not last:
                            act.wait_ge(s.br, NBR * m + NBR)
                            high_chunk(m + 1, WB)
                        if near == 1:
                            high_o(b + 1)
                    tiles(nc.scalar, b, more, tile)
                square(0)
                high_chunk(0, 0)
                high_h(0)
                root(0, range(H))
                for n in range(1, NC):
                    high_chunk(0, n)
                high_o(0)
                blocks(nc.scalar, block)

            @block.vector
            def _(dve):
                v = nc.vector
                dve.sem_inc(s.prod, PROD0)
                dve.sem_inc(s.wl, WL0)
                dve.wait_ge(s.cst, 16)
                da = ob[:, 0:H]

                def add_scans(b):
                    dve.wait_ge(s.ldo, 48 * b + 48)
                    v.tensor_tensor(da.rearrange("p h (b i) -> p b h i", i=P), scans[0], scans[1], ALU.add).then_inc(s.osum, 1)

                def invert(b, h):
                    dve.wait_ge(s.root, H * b + h + 1)
                    v.reciprocal(roots[:, h], roots[:, h]).then_inc(s.rec, 1)

                def norm(b):
                    dve.wait_ge(s.rec, (H + 1) * b + H)
                    v.scalar_tensor_tensor(da, da, gnw[:, 0:1], roots, ALU.mult, ALU.mult).then_inc(s.rec, 1)
                    dve.wait_ge(s.rec, (H + 1) * b + H + 1)
                    v.tensor_tensor(da, da, zt[:], ALU.mult).then_inc(s.oa, 1)

                def low_chunk(m, n):
                    dve.wait_ge(s.wh, NC * m + n + 1)
                    v.tensor_tensor(wl[:, n], w[:, n], wh[:, n], ALU.subtract).then_inc(s.wl, 1)

                def low_h(b):
                    for k in range(KD):
                        dve.wait_ge(s.hh, KD * b + k + 1)
                        v.tensor_tensor(hl[:, k], hb[:, k], hh[:, k], ALU.subtract).then_inc(s.hl, 1)

                def low_o(b):
                    for k in range(KD):
                        dve.wait_ge(s.oh, KD * b + k + 1)
                        v.tensor_tensor(ol[:, k], ob[:, k], oh[:, k], ALU.subtract).then_inc(s.ol, 1)

                def block(b, more):
                    def tile(m, u, first, near, last):
                        if near == 0:
                            add_scans(b + 1)
                        for br in range(NBR):
                            if not last:
                                low_chunk(m + 1, br)
                            if br == 0:
                                wait(dve, s.y, m)
                            dve.wait_ge(s.sig, NBR * m + br + 1 + SIG0)
                            dve.wait_ge(s.br, NBR * m + br + 1)
                            v.tensor_tensor(pr[:, br], sg[:, br], pbr[br][:], ALU.mult).then_inc(s.prod, 1)
                            if near == 0 and br > 0:
                                invert(b + 1, br - 1)
                            if near == 1 and br < 2:
                                invert(b + 1, 2 + br)
                            if near == 1 and br == 1:
                                norm(b + 1)
                        if near == 1:
                            low_h(b + 1)
                        if not last:
                            low_chunk(m + 1, WB)
                        dve.wait_ge(s.prod, NBR * m + NBR + PROD0)
                        v.tensor_tensor(pr[:, 0], pr[:, 0], pr[:, 1], ALU.add).then_inc(s.add, 1)
                        dve.wait_ge(s.add, m + 1)
                        dve.wait_ge(s_y[u], (m - u) * 8)
                        v.tensor_tensor(yb[:, u], pr[:, 0], pr[:, 2], ALU.add).then_inc(s.y, 1)
                        if near == 1:
                            low_o(b + 1)
                    tiles(nc.vector, b, more, tile)
                add_scans(0)
                low_chunk(0, 0)
                low_h(0)
                for h in range(H):
                    invert(0, h)
                norm(0)
                for n in range(1, NC):
                    low_chunk(0, n)
                low_o(0)
                blocks(nc.vector, block)


def project_out(nc, g):
    with ExitStack() as c:
        wo = sbuf(nc, c, "wo", [P, KD, D])
        wh, wl = (sbuf(nc, c, n, [P, KD, D], F32R) for n in ("wo_high", "wo_low"))
        y = sbuf(nc, c, "yp", [P, 2, KD, P])
        yh, yl = (sbuf(nc, c, n, [P, 2, KD, P], F32R) for n in ("yp_high", "yp_low"))
        rows = sbuf(nc, c, "rowsm", [P, 3, D])
        wr = sbuf(nc, c, "wr", [P, KD, E])
        xt = sbuf(nc, c, "xt", [P, 2, D])
        h2 = sbuf(nc, c, "h2", [P, 2, D])
        h2T = sbuf(nc, c, "h2T", [P, KD, P])
        st = sbuf(nc, c, "stat", [P, 2])
        po = [[psum(nc, c, f"po{u}{n}") for n in range(2)] for u in range(2)]
        pt = [psum(nc, c, f"ptp{n}") for n in range(2)]
        pl = psum(nc, c, "plp")
        s = sems(nc, c, "po", "cst rt " + " ".join(f"wo{k}" for k in range(KD)) + " wh wl y0 y1 yh yl x0 x1 out half x1d ssq sr h2a h2 tr trc lg lgc st0 st1 held")
        s_wo = list(s[2:2 + KD])
        s_ld, s_x, s_st = [s.y0, s.y1], [s.x0, s.x1], [s.st0, s.st1]

        def steps(eng, step):
            for u in range(2):
                step(u, u, True)
            with eng.Fori(1, LT // 2 - 1) as i:
                for u in range(2):
                    step(2 * i + u, u, True)
            for u in range(2):
                step(LT - 2 + u, u, u == 0)

        def first(t):
            return isinstance(t, int) and t == 0

        with nc.Block() as block:
            @block.sync
            def _(sp):
                def load(t, u):
                    at = bass.ds(t * P, P)
                    wait(sp, s.yl, t - 1)
                    sp.dma_start(y[:, u], g.y_d[:, :, at]).then_inc(s_ld[u], 16)
                    wait(sp, s_st[u], 16 * (t - u))
                    sp.dma_start(xt[:, u], g.x[at]).then_inc(s_x[u], 16)
                for u in range(2):
                    load(u, u)
                for k in range(KD):
                    sp.dma_start(wo[:, k], g.w_out[:, k]).then_inc(s_wo[k], 16)
                sp.dma_start(rows[:], g.rows_d[:, 0:3]).then_inc(s.cst, 16)
                sp.dma_start(wr[:], g.w_router).then_inc(s.rt, 16)
                with nc.sync.Fori(1, LT // 2) as i:
                    for u in range(2):
                        t = nc.sync.snap(2 * i + u)
                        load(t, u)

            @block.gpsimd
            def _(pool):
                with nc.gpsimd.Fori(0, LT // 2) as i:
                    for u in range(2):
                        at = nc.gpsimd.snap(i * 2 * P + u * P)
                        pool.wait_ge(s.h2, 2 * i + u + 1)
                        hold(pool, s.held)
                        pool.dma_start(g.out[bass.ds(at, P)], xt[:, u]).then_inc(s_st[u], 16)
                        pool.dma_start(g.h2_d[bass.ds(at, P)], h2[:, u]).then_inc(s_st[u], 16)
                for u in range(2):
                    pool.wait_ge(s_st[u], 16 * LT)

            @block.tensor
            def _(pe):
                def project(t, u, half, load):
                    wait(pe, s.half, 2 * t + half - 3)
                    pe.wait_ge(s.yl, t + 1)
                    for k in range(KD):
                        if load:
                            pe.wait_ge(s.wl, k + 1)
                        high, low = yh[:, u, k], yl[:, u, k]
                        rh, rl = (x[:, k, half * 512:(half + 1) * 512] for x in (wh, wl))
                        nc.tensor.matmul(po[u][half][:], high, rh, start=(k == 0), stop=False)
                        nc.tensor.matmul(po[u][half][:], high, rl, start=False, stop=False)
                        last = nc.tensor.matmul(po[u][half][:], low, rh, start=False, stop=(k == KD - 1))
                    last.then_inc(s.out, 1)

                def turn(t, u):
                    pe.wait_ge(s.h2, t + 1)
                    wait(pe, s.trc, 2 * t)
                    for q in range(2):
                        for j in range(4):
                            k = 4 * q + j
                            last = nc.tensor.transpose(pt[q][:, j * P:(j + 1) * P], h2[:, u, k * P:(k + 1) * P], g.ident)
                        last.then_inc(s.tr, 1)

                def route(t):
                    if first(t):
                        pe.wait_ge(s.rt, 16)
                    pe.wait_ge(s.trc, 2 * t + 2)
                    wait(pe, s.lgc, t)
                    for k in range(KD):
                        last = nc.tensor.matmul(pl[:, 0:E], h2T[:, k], wr[:, k], start=(k == 0), stop=(k == KD - 1))
                    last.then_inc(s.lg, 1)

                def step(t, u, more):
                    project(t, u, 0, first(t))
                    if not isinstance(t, int) or t > 1:
                        route(t - 2)
                    project(t, u, 1, False)
                    if not first(t):
                        turn(t - 1, 1 - u)
                steps(nc.tensor, step)
                route(LT - 2)
                turn(LT - 1, (LT - 1) % 2)
                route(LT - 1)

            @block.scalar
            def _(act):
                a = nc.scalar.activation

                def high(t, u):
                    act.wait_ge(s_ld[u], 8 * (t - u) + 16)
                    wait(act, s.out, 2 * t - 2)
                    a(yh[:, u], y[:, u], ACT.Copy).then_inc(s.yh, 1)

                def spread(t, u):
                    act.wait_ge(s.x1d, t + 1)
                    a(h2[:, u], xt[:, u], ACT.Square, accum_out=st[:, 0:1]).then_inc(s.ssq, 1)
                    act.wait_ge(s.ssq, t + 1)
                    wait(act, s.h2, t)
                    a(st[:, 1:2], st[:, 0:1], ACT.Sqrt, bias=g.eps[:, 0:1], scale=1.0 / D).then_inc(s.sr, 1)

                def logits(t):
                    at = t if isinstance(t, int) else nc.scalar.snap(t)
                    act.wait_ge(s.lg, t + 1)
                    a(g.logits[:, bass.ds(at, 1)].rearrange("p a e -> p (a e)"), pl[:, 0:E], ACT.Copy).then_inc(s.lgc, 1)

                def turned(t):
                    wait(act, s.lg, t)
                    for q in range(2):
                        act.wait_ge(s.tr, 2 * t + q + 1)
                        a(h2T[:, 4 * q:4 * q + 4], pt[q][:].rearrange("p (k t) -> p k t", k=4), ACT.Copy).then_inc(s.trc, 1)

                def step(t, u, more):
                    if more:
                        high(t + 1, 1 - u)
                    if first(t):
                        for k in range(KD):
                            act.wait_ge(s_wo[k], 16)
                            a(wh[:, k], wo[:, k], ACT.Copy).then_inc(s.wh, 1)
                        return
                    spread(t - 1, 1 - u)
                    if not isinstance(t, int) or t > 1:
                        logits(t - 2)
                    turned(t - 1)
                high(0, 0)
                steps(nc.scalar, step)
                spread(LT - 1, (LT - 1) % 2)
                logits(LT - 2)
                turned(LT - 1)
                logits(LT - 1)

            @block.vector
            def _(dve):
                v = nc.vector
                dve.wait_ge(s.cst, 16)

                def low(t, u):
                    dve.wait_ge(s.yh, t + 1)
                    v.tensor_tensor(yl[:, u], y[:, u], yh[:, u], ALU.subtract).then_inc(s.yl, 1)

                def residual(t, u):
                    dve.wait_ge(s_x[u], 8 * (t - u) + 16)
                    wait(dve, s.tr, 2 * t - 2)
                    for half in range(2):
                        cols = slice(half * 512, (half + 1) * 512)
                        dve.wait_ge(s.out, 2 * t + half + 1)
                        v.tensor_tensor(h2[:, u, cols], po[u][half][:], rows[:, 0, cols], ALU.mult).then_inc(s.half, 1)
                    dve.wait_ge(s.half, 2 * t + 2)
                    v.tensor_tensor(xt[:, u], xt[:, u], h2[:, u], ALU.add).then_inc(s.x1d, 1)

                def norm(t, u):
                    dve.wait_ge(s.sr, t + 1)
                    v.reciprocal(st[:, 1:2], st[:, 1:2]).then_inc(s.h2a, 1)
                    dve.wait_ge(s.h2a, 2 * t + 1)
                    v.scalar_tensor_tensor(h2[:, u], xt[:, u], st[:, 1:2], rows[:, 2], ALU.mult, ALU.mult).then_inc(s.h2a, 1)
                    dve.wait_ge(s.h2a, 2 * t + 2)
                    v.tensor_tensor(h2[:, u], h2[:, u], rows[:, 1], ALU.add).then_inc(s.h2, 1)

                def step(t, u, more):
                    if not first(t):
                        residual(t - 1, 1 - u)
                    if more:
                        low(t + 1, 1 - u)
                    if first(t):
                        for k in range(KD):
                            dve.wait_ge(s.wh, k + 1)
                            v.tensor_tensor(wl[:, k], wo[:, k], wh[:, k], ALU.subtract).then_inc(s.wl, 1)
                    else:
                        norm(t - 1, 1 - u)
                low(0, 0)
                steps(nc.vector, step)
                residual(LT - 1, (LT - 1) % 2)
                norm(LT - 1, (LT - 1) % 2)


def choose(nc, g):
    with ExitStack() as c:
        aff = sbuf(nc, c, "aff", [E, SEQ])
        red = sbuf(nc, c, "redc", [P, LT])
        val = sbuf(nc, c, "val", [E, CAP])
        idx = sbuf(nc, c, "idx", [E, CAP], U32)
        idf = sbuf(nc, c, "idf", [E, CAP])
        ps = psum(nc, c, "aff_ps", (P, 4, 512))
        pt = psum(nc, c, "ct_ps")
        s = sems(nc, c, "ch", "own ex aff tr trc top mi idf ct")
        with nc.Block() as block:
            @block.scalar
            def _(act):
                act.wait_ge(s.own, 2)
                nc.scalar.activation(g.logits, g.logits, ACT.Exp).then_inc(s.ex, 1)
                for q in range(4):
                    act.wait_ge(s.tr, q + 1)
                    nc.scalar.activation(aff[:, q * 512:(q + 1) * 512], ps[0:E, q], ACT.Copy).then_inc(s.trc, 1)

            @block.tensor
            def _(pe):
                pe.wait_ge(s.aff, 1)
                for q in range(4):
                    for j in range(4):
                        last = nc.tensor.transpose(ps[0:E, q, j * P:(j + 1) * P], g.logits[:, 4 * q + j], g.ident)
                    last.then_inc(s.tr, 1)
                pe.wait_ge(s.idf, 1)
                for half in range(CAP // P):
                    for j, rows in enumerate((val, idf)):
                        last = nc.tensor.transpose(pt[:, (2 * half + j) * E:(2 * half + j + 1) * E], rows[:, half * P:(half + 1) * P], g.ident[0:E, 0:E])
                last.then_inc(s.ct, 1)

            @block.vector
            def _(dve):
                v = nc.vector
                own = Steps(dve, s.own)
                lg = g.logits
                wide = red[:, :, None].broadcast_to([P, LT, E])
                own.done(v.tensor_reduce(red[:], lg, AX_X, ALU.max))
                own.settle()
                own.done(v.tensor_tensor(lg, lg, wide, ALU.subtract))
                dve.wait_ge(s.ex, 1)
                own.done(v.tensor_reduce(red[:], lg, AX_X, ALU.add))
                own.settle()
                own.done(v.reciprocal(red[:], red[:]))
                own.settle()
                v.tensor_tensor(lg, lg, wide, ALU.mult).then_inc(s.aff, 1)
                dve.wait_ge(s.trc, 4)
                own = Steps(dve, s.top)
                for r in range(CAP // 8):
                    at = slice(8 * r, 8 * r + 8)
                    own.done(v.max(val[:, at], aff[:]))
                    own.settle()
                    v.max_index(idx[:, at], val[:, at], aff[:]).then_inc(s.mi, 1)
                    own.done(v.match_replace(aff[:], val[:, at], aff[:], -1.0))
                    own.settle()
                dve.wait_ge(s.mi, CAP // 8)
                v.tensor_copy(idf[:], idx[:]).then_inc(s.idf, 1)
                dve.wait_ge(s.ct, 1)
                both = pt[:, 0:2 * CAP // P * E].rearrange("p (a j e) -> p a j e", j=2, e=E)
                own.done(v.tensor_copy(g.top_aff, both[:, :, 0]))
                own.done(v.tensor_copy(g.top_idx, both[:, :, 1]))
                own.settle()


def experts(nc, g):
    NF = FE // P
    NW = 3 * NF
    HALF = CAP // P
    RAW, CUT = NW // 2, NF
    LEAD = CUT - 1
    TURN = 5
    with ExitStack() as c:
        w = sbuf(nc, c, "we", [P, RAW, D])
        wh, wl = (sbuf(nc, c, n, [P, CUT, D], F32R) for n in ("we_high", "we_low"))
        gt2 = sbuf(nc, c, "gt2", [P, D])
        ti = sbuf(nc, c, "ti", [P, 2, HALF], U32)
        ta = sbuf(nc, c, "ta", [P, 2, HALF])
        xe = sbuf(nc, c, "xe", [P, HALF, D])
        xh, xl = (sbuf(nc, c, n, [P, 2, KD, CAP], F32R) for n in ("xe_high", "xe_low"))
        hid = sbuf(nc, c, "hid", [P, 2, CAP])
        hh, hl = (sbuf(nc, c, n, [P, NF, CAP], F32R) for n in ("hid_high", "hid_low"))
        sg = sbuf(nc, c, "sge", [P, 2, CAP])
        yb = sbuf(nc, c, "ybe", [P, HALF, D])
        pg = [psum(nc, c, f"eg{n}") for n in range(2)]
        pu = [psum(nc, c, f"eu{n}") for n in range(2)]
        py = [[psum(nc, c, f"ey{a}{n}") for n in range(2)] for a in range(HALF)]
        s = sems(nc, c, "ex", "cst pick ga0 ga1 tr xh xl used wh wl sig hid hh hl yb sc0 sc1 held " + " ".join(f"w{n}" for n in range(RAW)))
        s_w = list(s[-RAW:])
        s_ga, s_sc = [s.ga0, s.ga1], [s.sc0, s.sc1]

        with nc.Block() as block:
            @block.sync
            def _(sp):
                sp.dma_start(gt2[:], g.rows_d[:, 3]).then_inc(s.cst, 16)
                for n in range(RAW):
                    sp.dma_start(w[:, n], g.w_ex[0, n]).then_inc(s_w[n], 16)

                def load(e, n):
                    sp.wait_ge(s.wl, NW * e + n - RAW + 1)
                    sp.dma_start(w[:, n % RAW], g.w_ex[e, n]).then_inc(s_w[n % RAW], 16)
                for n in range(RAW, NW):
                    load(0, n)
                with nc.sync.Fori(1, E) as e:
                    for n in range(NW):
                        load(e, n)

            @block.gpsimd
            def _(pool):
                def gather(e, u):
                    pool.wait_ge(s.pick, 2 * e + 2)
                    wait(pool, s.tr, 4 * e)
                    hold(pool, s.held)
                    for a in range(HALF):
                        pool.indirect_dma_start(xe[:, a], None, g.h2_d,
                                                bass.IndirectOffsetOnAxis(ap=ti[:, u, a:a + 1], axis=0)).then_inc(s_ga[u], 16)

                def scatter(e, u, others):
                    pool.wait_ge(s.yb, 4 * e + 4)
                    pool.wait_ge(s_sc[1 - u], others)
                    hold(pool, s.held)
                    for a in range(HALF):
                        pool.indirect_dma_start(g.out, bass.IndirectOffsetOnAxis(ap=ti[:, u, a:a + 1], axis=0), yb[:, a], None,
                                                compute_op=ALU.add).then_inc(s_sc[u], 16)

                def pair(i, last):
                    scatter(2 * i, 0, 32 * i)
                    if not last:
                        gather(2 * i + 2, 0)
                    scatter(2 * i + 1, 1, 32 * i + 32)
                    if not last:
                        gather(2 * i + 3, 1)
                for u in range(2):
                    gather(u, u)
                with nc.gpsimd.Fori(0, E // 2 - 1) as i:
                    pair(i, False)
                pair(E // 2 - 1, True)
                for u in range(2):
                    pool.wait_ge(s_sc[u], 32 * E // 2)

            @block.tensor
            def _(pe):
                def turn(e, u):
                    pe.wait_ge(s_ga[u], 32 * ((e - u) // 2) + 32 if isinstance(e, int) else e * 16 + (2 - u) * 16)
                    wait(pe, s.yb, 4 * (e - 1) if not isinstance(e, int) or e > 1 else 0)
                    for a in range(HALF):
                        for q in range(2):
                            for j in range(4):
                                k = 4 * q + j
                                last = nc.tensor.transpose(py[a][q][:, j * P:(j + 1) * P], xe[:, a, k * P:(k + 1) * P], g.ident)
                            last.then_inc(s.tr, 1)

                def expert(e, u, last_one):
                    pe.wait_ge(s.xl, 4 * e + 4)
                    for f in range(NF):
                        for n, bank, free in ((2 * f, pg[f % 2], s.sig), (2 * f + 1, pu[f % 2], s.hid)):
                            pe.wait_ge(s.wl, NW * e + n + 1)
                            pe.wait_ge(free, NF * e + f + 1)
                            for k in range(KD):
                                high, low = (x[:, n % CUT, k * P:(k + 1) * P] for x in (wh, wl))
                                nc.tensor.matmul(bank[:, 0:CAP], high, xh[:, u, k], start=(k == 0), stop=False)
                                nc.tensor.matmul(bank[:, 0:CAP], high, xl[:, u, k], start=False, stop=False)
                                last = nc.tensor.matmul(bank[:, 0:CAP], low, xh[:, u, k], start=False, stop=(k == KD - 1))
                            last.then_inc(s.used, 1)
                        if f == TURN and not last_one:
                            turn(e + 1, 1 - u)
                    if not last_one:
                        pe.wait_ge(s.xl, 4 * e + 8)
                    else:
                        pe.wait_ge(s.yb, 4 * e)
                    for f in range(NF):
                        n = 2 * NF + f
                        pe.wait_ge(s.wl, NW * e + n + 1)
                        pe.wait_ge(s.hl, NF * e + f + 1)
                        for a in range(HALF):
                            high, low = (x[:, f, a * P:(a + 1) * P] for x in (hh, hl))
                            for lhs, rhs in ((high, wh), (high, wl), (low, wh)):
                                for q in range(2):
                                    last = nc.tensor.matmul(py[a][q][:], lhs, rhs[:, n % CUT, q * 512:(q + 1) * 512],
                                                            start=(f == 0 and lhs is high and rhs is wh),
                                                            stop=(f == NF - 1 and lhs is low))
                        last.then_inc(s.used, 1)
                turn(0, 0)
                with nc.tensor.Fori(0, E // 2 - 1) as i:
                    for u in range(2):
                        expert(2 * i + u, u, False)
                expert(E - 2, 0, False)
                expert(E - 1, 1, True)

            @block.scalar
            def _(act):
                act.sem_inc(s.sig, 2)

                def high_rows(e, u):
                    for a in range(HALF):
                        for q in range(2):
                            act.wait_ge(s.tr, 4 * e + 2 * a + q + 1)
                            nc.scalar.activation(xh[:, u, 4 * q:4 * q + 4, a * P:(a + 1) * P],
                                                 py[a][q][:].rearrange("p (k t) -> p k t", k=4), ACT.Copy).then_inc(s.xh, 1)

                def high_chunk(e, n):
                    act.wait_ge(s_w[n % RAW], 32 * e + 16 * (n // RAW + 1))
                    if not isinstance(e, int) or NW * e + n >= CUT:
                        act.wait_ge(s.used, NW * e + n - CUT + 1)
                    nc.scalar.activation(wh[:, n % CUT], w[:, n % RAW], ACT.Copy).then_inc(s.wh, 1)

                def expert(e, u, last_one):
                    for f in range(NF):
                        act.wait_ge(s.used, NW * e + 2 * f + 1)
                        act.wait_ge(s.hid, NF * e + f + 1)
                        nc.scalar.activation(sg[:, f % 2], pg[f % 2][:, 0:CAP], ACT.Silu).then_inc(s.sig, 1)
                        high_chunk(e, 2 * f + LEAD)
                        act.wait_ge(s.hid, NF * e + f + 1 + 2)
                        nc.scalar.activation(hh[:, f], hid[:, f % 2], ACT.Copy).then_inc(s.hh, 1)
                        high_chunk(e, 2 * f + 1 + LEAD)
                        if f == TURN and not last_one:
                            high_rows(e + 1, 1 - u)
                    for n in range(2 * NF + LEAD, NW + LEAD):
                        if n < NW or not last_one:
                            high_chunk(e, n)
                for n in range(LEAD):
                    high_chunk(0, n)
                high_rows(0, 0)
                with nc.scalar.Fori(0, E // 2 - 1) as i:
                    for u in range(2):
                        expert(2 * i + u, u, False)
                expert(E - 2, 0, False)
                expert(E - 1, 1, True)

            @block.vector
            def _(dve):
                v = nc.vector
                dve.sem_inc(s.hid, 2)
                dve.wait_ge(s.cst, 16)

                def pick(e, u, added):
                    at = e if isinstance(e, int) else nc.vector.snap(e)
                    wait(dve, s_sc[u], added)
                    v.tensor_copy(ti[:, u], g.top_idx[:, :, bass.ds(at, 1)].rearrange("p a e -> p (a e)")).then_inc(s.pick, 1)
                    v.tensor_copy(ta[:, u], g.top_aff[:, :, bass.ds(at, 1)].rearrange("p a e -> p (a e)")).then_inc(s.pick, 1)

                def low_rows(e, u):
                    for a in range(HALF):
                        for q in range(2):
                            dve.wait_ge(s.xh, 4 * e + 2 * a + q + 1)
                            at = (slice(None), u, slice(4 * q, 4 * q + 4), slice(a * P, (a + 1) * P))
                            v.tensor_tensor(xl[at], py[a][q][:].rearrange("p (k t) -> p k t", k=4), xh[at], ALU.subtract).then_inc(s.xl, 1)

                def low_chunk(e, n):
                    dve.wait_ge(s.wh, NW * e + n + 1)
                    v.tensor_tensor(wl[:, n % CUT], w[:, n % RAW], wh[:, n % CUT], ALU.subtract).then_inc(s.wl, 1)

                def expert(i, u, last_one):
                    e = 2 * i + u
                    for f in range(NF):
                        dve.wait_ge(s.used, NW * e + 2 * f + 2)
                        dve.wait_ge(s.sig, NF * e + f + 1 + 2)
                        v.tensor_tensor(hid[:, f % 2], sg[:, f % 2], pu[f % 2][:, 0:CAP], ALU.mult).then_inc(s.hid, 1)
                        low_chunk(e, 2 * f + LEAD)
                        dve.wait_ge(s.hh, NF * e + f + 1)
                        v.tensor_tensor(hl[:, f], hid[:, f % 2], hh[:, f], ALU.subtract).then_inc(s.hl, 1)
                        low_chunk(e, 2 * f + 1 + LEAD)
                        if f == TURN and not last_one:
                            low_rows(e + 1, 1 - u)
                        if f == 1 and not last_one and (u == 1 or not isinstance(i, int) or i > 0):
                            pick(e + 1, 1 - u, 32 * (i + u))
                    for n in range(2 * NF + LEAD, NW + LEAD):
                        if n < NW or not last_one:
                            low_chunk(e, n)
                    dve.wait_ge(s.used, NW * (e + 1))
                    dve.wait_ge(s.pick, 2 * e + 2)
                    wait(dve, s_sc[1 - u], 32 * (i + u))
                    for a in range(HALF):
                        for q in range(2):
                            cols = slice(q * 512, (q + 1) * 512)
                            v.scalar_tensor_tensor(yb[:, a, cols], py[a][q][:], ta[:, u, a:a + 1], gt2[:, cols],
                                                   ALU.mult, ALU.mult).then_inc(s.yb, 1)
                pick(0, 0, 0)
                pick(1, 1, 0)
                for n in range(LEAD):
                    low_chunk(0, n)
                low_rows(0, 0)
                expert(0, 0, False)
                expert(0, 1, False)
                with nc.vector.Fori(1, E // 2 - 1) as i:
                    for u in range(2):
                        expert(i, u, False)
                expert(E // 2 - 1, 0, False)
                expert(E // 2 - 1, 1, True)


def shape_tables():
    i = np.arange(P)
    t = np.zeros((P, C_W), np.float32)
    t[:, C_ID:C_ID + P] = np.eye(P)
    t[:, C_ONE:C_ONE + P] = 1.0
    t[:, C_BLK:C_BLK + P] = (i[:, None] // DH) == (i[None, :] // DH)
    nf = DK // 4
    for half in range(2):
        for f in range(nf):
            a, b = half * 2 * nf + f, half * 2 * nf + nf + f
            t[b, C_ROT + a] = -1.0
            t[a, C_ROT + b] = 1.0
    l, m = i[:, None], i[None, :]
    for d in range(2):
        before, after = (l <= m, l > m) if d == 0 else (l >= m, l < m)
        at = C_DIR + d * N_DIRT * P
        t[:, at:at + P] = before
        t[:, at + P:at + 2 * P] = after
        for lev in range(N_LEV):
            size = 1 << lev
            pair = (l // (2 * size)) == (m // (2 * size))
            up, low = (l // size) % 2 == 1, (m // size) % 2 == 0
            mask = pair & up & low if d == 0 else pair & ~up & ~low
            at = C_LEV + (d * N_LEV + lev) * P
            t[:, at:at + P] = mask
    start = np.clip(np.arange(GRID) - WC // 2, 0, GRID - WC)
    j, col = i[:, None] % GRID, np.arange(GRID)[None, :]
    t[:, C_WIN:C_WIN + GRID] = np.where((col >= start[j]) & (col < start[j] + WC), 0.0, NEG)
    f = np.zeros((P, F_W), np.float64)
    same = (l // 64) == (m // 64)
    ang = 2 * np.pi * ((l % 64) * (m % 64) % 64) / 64
    f[:, F_C4:F_C4 + P] = same * np.cos(ang) / np.sqrt(SEQ * 64)
    f[:, F_C4 + P:F_C4 + 2 * P] = same * np.sin(ang) / np.sqrt(SEQ * 64)
    ang = 2 * np.pi * (l * m % P) / P
    for n, table in enumerate((np.cos(ang), np.sin(ang), -np.sin(ang))):
        f[:, F_N1 + n * P:F_N1 + (n + 1) * P] = table
    n2 = SEQ // P
    ang = 2 * np.pi * (i[:, None] * np.arange(n2)[None, :]) / SEQ
    f[:, F_TW:F_TW + n2], f[:, F_TW + n2:F_TW + 2 * n2] = np.cos(ang), np.sin(ang)
    lo = P // n2
    ang = 2 * np.pi * ((l // lo) * (m // lo) % n2) / n2
    same = (l % lo) == (m % lo)
    f[:, F_K2:F_K2 + P], f[:, F_K2 + P:F_K2 + 2 * P] = same * np.cos(ang), -1.0 * same * np.sin(ang)
    tok = np.arange(SEQ)
    inv = 10000.0 ** (-np.arange(nf) / nf)
    where = np.stack([tok // GRID, tok % GRID])
    ang = where[:, None, :] * inv[None, :, None]
    ang = np.repeat(ang[:, None], 2, axis=1).reshape(P, SEQ)
    rope = np.stack([np.cos(ang), np.sin(ang)], axis=1).astype(np.float32)
    return {"consts": t, "rope": rope, "ftab": f.astype(np.float32)}


def expert_chunks(i):
    gate, up = (i[n][0].reshape(E, KD, P, FE // P, P).transpose(0, 3, 2, 1, 4).reshape(E, FE // P, 1, P, D)
                for n in ("w_e_gate", "w_e_up"))
    down = i["w_e_down"][0].reshape(E, FE // P, P, D)
    first = np.concatenate([gate, up], axis=2).reshape(E, 2 * FE // P, P, D)
    return np.concatenate([first, down], axis=1)


def layouts(i):
    tokens = np.concatenate([i["ctx"][0], i["x"][0]], axis=0)

    def col(v):
        return v.reshape(-1, P).T

    def tiles(m):
        return m.reshape(KD, P, -1, P).transpose(2, 1, 0, 3)

    w_in = i["w_in"][0]
    cuts = np.cumsum([0, 512, 512, 512, 512, 8, 8, 256, 256, 256, 256, 3 * D])
    part = [w_in[:, a:b] for a, b in zip(cuts[:-1], cuts[1:])]
    q, k, v, z, a, b, u, qn, kn, vn, gr = part
    wm, bm = i["w_mod"][0], i["b_mod"][0]
    out = {
        "xT": tokens.T.reshape(KD, P, T).transpose(1, 0, 2),
        "x": i["x"][0],
        "cc": np.stack([col(i["c"][0]), col(i["c_ctx"])], axis=-1),
        "w_mod_col": wm[:, :2 * D].reshape(KD, P, 2 * D).transpose(1, 0, 2),
        "w_mod_row": wm[:, 2 * D:].reshape(KD, P, 2, 2 * D).transpose(2, 0, 1, 3).reshape(2 * KD, P, 2 * D),
        "b_mod_col": col(bm[:2 * D]),
        "b_mod_row": bm[2 * D:],
        "norm1": col(i["norm1_w"][0]),
        "norm2": i["norm2_w"][0],
        "w_ch": tiles(np.concatenate([q, k, v, z, qn, kn, u], axis=1)),
        "w_tok": np.concatenate([vn, a, b], axis=1).reshape(KD, P, -1).transpose(1, 0, 2),
        "conv_w": i["conv_w"][0].reshape(CONV, 3, H, P).transpose(3, 2, 1, 0),
        "na_norm": np.stack([np.tile(i["na_qn_w"][0], 2), np.tile(i["na_kn_w"][0], 2)], axis=-1),
        "gdn_norm": i["gdn_norm_w"][0].reshape(P, 1),
        "w_gates": tiles(gr).reshape(3, KD, P, KD, P).transpose(1, 2, 0, 3, 4),
        "w_br": tiles(np.concatenate([i["w_br_a"][0], i["w_br_b"][0], i["w_br_c"][0]], axis=0)),
        "w_out": i["w_out"][0].reshape(KD, P, D).transpose(1, 0, 2),
        "w_router": i["w_router"][0].reshape(KD, P, E).transpose(1, 0, 2),
        "w_ex": expert_chunks(i),
        "rpb": i["na_rpb"][0].reshape(H * 15, 31),
        "a_log": i["a_log"][0].reshape(-1),
        "dt_bias": i["dt_bias"][0].reshape(-1),
    }
    out.update(shape_tables())
    return {n: np.ascontiguousarray(a) for n, a in out.items()}


def shared(tensors):
    class Shared(namedtuple("Tensors", list(tensors))):
        pass
    return Shared(**tensors)


SCRATCH = {
    "rows_d": (P, 4, D),
    "h_d": (P, KD, T),
    "q_d": (POS, P, H, P), "k_d": (POS, P, H, P), "kt_d": (POS, P, H, P), "vt_d": (POS, P, H, P),
    "z_d": (H, P, SEQ),
    "v_d": (T, 2 * P),
    "h2_d": (SEQ, D),
    "skew_d": (H * 15, GRID, 127),
    "oc_d": (2 * P, SEQ),
    "z2_d": (2, P, SEQ // P, FN),
    "yb_d": (2 * P, SEQ),
    "y_d": (P, KD, SEQ),
    "o_d": (2, POS, P, H, P),
}


def program(nc, g, stages=99):
    with ExitStack() as c:
        consts = sbuf(nc, c, "consts_sb", [P, C_W])
        eps = sbuf(nc, c, "eps_sb", [P, 1])
        g.eps = eps[:]
        g.ident, g.ones, g.blk, g.rot = (consts[:, at:at + P] for at in (C_ID, C_ONE, C_BLK, C_ROT))
        g.window = consts[:, C_WIN:C_WIN + GRID]
        g.dirt = lambda d, j: consts[:, C_DIR + (d * N_DIRT + j) * P:C_DIR + (d * N_DIRT + j + 1) * P]
        g.level = lambda d, lev: consts[:, C_LEV + (d * N_LEV + lev) * P:C_LEV + (d * N_LEV + lev + 1) * P]
        g.gd, g.beta, g.begc, g.esfx = (sbuf(nc, c, n, [P, 2, POS, H])[:] for n in ("gd", "beta", "begc", "esfx"))
        g.ab = sbuf(nc, c, "ab", [P, NT, 16])[:]
        load_tables(nc, g, consts, eps)
        with ExitStack() as c1:
            g.mod1 = sbuf(nc, c1, "mod1", [P, 2, KD, 2])[:]
            modulation(nc, g)
            g.hT = sbuf(nc, c1, "hT", [P, KD, T])[:]
            first_norm(nc, g)
            if stages < 2:
                return
            delta_inputs(nc, g)
            g.qn = sbuf(nc, c1, "qn", [P, HP, SEQ])[:]
            g.kn = sbuf(nc, c1, "kn", [P, HP, T])[:]
            g.uT = sbuf(nc, c1, "uT", [P, 2, SEQ])[:]
            mixer_inputs(nc, g)
            if stages >= 2.5:
                attention(nc, g)
                fourier(nc, g)
        if stages < 3:
            return
        decays(nc, g)
        delta_rule(nc, g)
        if stages < 4:
            return
        g.logits = sbuf(nc, c, "logits", [P, LT, E])[:]
        g.top_aff = sbuf(nc, c, "top_aff", [P, CAP // P, E])[:]
        g.top_idx = sbuf(nc, c, "top_idx", [P, CAP // P, E], U32)[:]
        merge(nc, g)
        project_out(nc, g)
        choose(nc, g)
        experts(nc, g)


def load_tables(nc, g, consts, eps):
    with ExitStack() as c:
        s = sems(nc, c, "tab", "ld eps")
        with nc.Block() as block:
            @block.sync
            def _(sp):
                sp.dma_start(consts[:], g.consts).then_inc(s.ld, 16)
                sp.wait_ge(s.ld, 16)

            @block.vector
            def _(dve):
                nc.vector.memset(eps[:], EPS).then_inc(s.eps, 1)
                dve.wait_ge(s.eps, 1)


def kernel(**inputs):
    import concourse.bacc as bacc
    from concourse.bass_utils import run_bass_kernel_spmd

    nc = bacc.Bacc("TRN2", target_bir_lowering=False, num_devices=1)
    arrays = {"in_" + n: a for n, a in layouts({n: np.asarray(a) for n, a in inputs.items()}).items()}
    tensors = {n[3:]: nc.dram_tensor(n, a.shape, mybir.dt.from_np(a.dtype), kind="ExternalInput").ap() for n, a in arrays.items()}
    tensors.update({n: nc.dram_tensor(n, list(shape), F32).ap() for n, shape in SCRATCH.items()})
    tensors["out"] = nc.dram_tensor("out", (SEQ, D), F32, kind="ExternalOutput").ap()
    g = shared(tensors)
    program(nc, g)
    r = run_bass_kernel_spmd(nc, [arrays], core_ids=[0])
    return r.results[0]["out"].reshape(1, SEQ, D)
```

```python
from collections import namedtuple
from contextlib import ExitStack

import numpy as np

import concourse.bass as bass
from concourse import mybir

F32 = mybir.dt.float32
U32 = mybir.dt.uint32
F32R = mybir.dt.float32r
ACT = mybir.ActivationFunctionType
ALU = mybir.AluOpType
AX_X = mybir.AxisListType.X

P = 128
D = 1024
KD = D // P
CTX = 256
SEQ = 2048
T = CTX + SEQ
NT = T // P
CT = CTX // P
LT = SEQ // P
POS = NT + CT
EPS = 1e-6
H = 4
DK = 128
CONV = 5
PAD = CONV // 2
CONVW = T + 3 * PAD
CONVO = CONVW - 2 * PAD
GRID = 64
WR, WC = 8, 16
ROWS = SEQ // GRID
DH = 64
HP = 2
FN = 256
E = 16
CAP = 2 * SEQ // E
FE = 1024
BLOCKS = [(0, CTX)] + [(CTX + 512 * b, 512) for b in range(4)]
NEG = -1e30

C_ID, C_ONE, C_BLK, C_ROT = 0, P, 2 * P, 3 * P
C_DIR = 4 * P
N_DIRT = 2
C_LEV = C_DIR + 2 * N_DIRT * P
N_LEV = 7
C_WIN = C_LEV + 2 * N_LEV * P
C_FLIP = C_WIN + GRID
C_W = C_FLIP + P

F_C4 = 0
F_N1 = F_C4 + FN
F_TW = F_N1 + 3 * P
F_K2 = F_TW + 2 * (SEQ // P)
F_W = F_K2 + 2 * P


class Steps:

    def __init__(self, eng, sem, start=0):
        self.eng, self.sem, self.start, self.n = eng, sem, start, 0

    def done(self, ins):
        self.n += 1
        return ins.then_inc(self.sem, 1)

    def settle(self):
        self.eng.wait_ge(self.sem, self.start + self.n)


def hold(eng, sem):
    eng.sem_inc(sem, 1)


def sbuf(nc, c, name, shape, dt=F32):
    return c.enter_context(nc.sbuf_tensor("sb_" + name, shape, dt))


def psum(nc, c, name, shape=(P, 512), dt=F32):
    return c.enter_context(nc.psum_tensor(name, list(shape), dt))


def sems(nc, c, prefix, names):
    made = {n: nc.alloc_semaphore(prefix + "_" + n) for n in names.split()}


    def clear():
        nc.clear_and_free_semaphores(list(made.values()))
        nc.all_engine_barrier()
    c.callback(clear)
    return namedtuple("Semaphores", list(made))(**made)


def modulation(nc, g):
    SLOTS = 6
    with ExitStack() as c:
        cc = sbuf(nc, c, "cc", [P, KD, 2])
        cs = sbuf(nc, c, "cs", [P, KD, 2])
        csb = sbuf(nc, c, "csb", [P, KD, P])
        wcol = sbuf(nc, c, "wcol", [P, KD, 2 * D])
        bcol = sbuf(nc, c, "bcol", [P, 2 * KD])
        n1 = sbuf(nc, c, "n1", [P, KD])
        wrow = sbuf(nc, c, "wrow", [P, SLOTS, 2 * D])
        rows = sbuf(nc, c, "rows", [P, 4, D])
        brow = sbuf(nc, c, "brow", [P, 4 * D])
        n2 = sbuf(nc, c, "n2", [P, D])
        ps = psum(nc, c, "mod_ps", (P, 8, 512))
        s = sems(nc, c, "mod", "small srow wcol silu bc col row fin rowfin st used " + " ".join(f"w{n}" for n in range(SLOTS)))
        s_w = list(s[-SLOTS:])
        pcol = ps[:, 0, 0:4 * KD].rearrange("p (m s) -> p m s", s=2)
        with nc.Block() as block:
            @block.sync
            def _(sp):
                sp.dma_start(cc[:], g.cc).then_inc(s.small, 16)
                sp.dma_start(bcol[:], g.b_mod_col).then_inc(s.small, 16)
                sp.dma_start(n1[:], g.norm1).then_inc(s.small, 16)
                sp.dma_start(wcol[:], g.w_mod_col).then_inc(s.wcol, 16)
                for k in range(2 * KD):
                    wait(sp, s.used, k - SLOTS + 1)
                    sp.dma_start(wrow[:, k % SLOTS], g.w_mod_row[k]).then_inc(s_w[k % SLOTS], 16)
                sp.wait_ge(s.rowfin, 9)
                sp.dma_start(g.rows_d, rows[:]).then_inc(s.st, 16)
                sp.wait_ge(s.st, 16)

            @block.gpsimd
            def _(pool):
                pool.dma_start(brow[:], g.b_mod_row.partition_broadcast(P)).then_inc(s.srow, 16)
                pool.dma_start(n2[:], g.norm2.partition_broadcast(P)).then_inc(s.srow, 16)

            @block.scalar
            def _(act):
                act.wait_ge(s.small, 48)
                nc.scalar.activation(cs[:], cc[:], ACT.Silu).then_inc(s.silu, 1)

            @block.tensor
            def _(pe):
                pe.wait_ge(s.silu, 1)
                pe.wait_ge(s.wcol, 16)
                for m in range(2 * KD):
                    for k in range(KD):
                        last = nc.tensor.matmul(pcol[:, m], wcol[:, k, m * P:(m + 1) * P], cs[:, k],
                                                start=(k == 0), stop=(k == KD - 1))
                last.then_inc(s.col, 1)
                pe.wait_ge(s.bc, 1)
                pe.wait_ge(s.fin, 3)
                for half in range(2):
                    for k in range(KD):
                        n = half * KD + k
                        pe.wait_ge(s_w[n % SLOTS], 16 * (n // SLOTS + 1))
                        for j in range(4):
                            last = nc.tensor.matmul(ps[:, half * 4 + j], csb[:, k], wrow[:, n % SLOTS, j * 512:(j + 1) * 512],
                                                    start=(k == 0), stop=(k == KD - 1))
                        last.then_inc(s.used, 1)
                    last = None

            @block.vector
            def _(dve):
                own = Steps(dve, s.fin)
                dve.wait_ge(s.silu, 1)
                nc.vector.tensor_copy(csb[:], cs[:, :, 0:1].broadcast_to([P, KD, P])).then_inc(s.bc, 1)
                dve.wait_ge(s.small, 48)
                dve.wait_ge(s.srow, 32)
                dve.wait_ge(s.col, 1)
                own.done(nc.vector.tensor_tensor(g.mod1[:, 0], pcol[:, 0:KD], bcol[:, 0:KD, None].broadcast_to([P, KD, 2]), ALU.add))
                own.done(nc.vector.tensor_tensor(g.mod1[:, 1], pcol[:, KD:], bcol[:, KD:, None].broadcast_to([P, KD, 2]), ALU.add))
                own.settle()
                own.done(nc.vector.scalar_tensor_tensor(g.mod1[:, 1], g.mod1[:, 1], 1.0, n1[:, :, None].broadcast_to([P, KD, 2]),
                                                        ALU.add, ALU.mult))
                own = Steps(dve, s.rowfin)
                for half in range(2):
                    dve.wait_ge(s.used, (half + 1) * KD)
                    for j in range(half * 4, half * 4 + 4):
                        own.done(nc.vector.tensor_tensor(rows[:, j // 2, (j % 2) * 512:(j % 2 + 1) * 512], ps[:, j],
                                                         brow[:, j * 512:(j + 1) * 512], ALU.add))
                own.settle()
                own.done(nc.vector.scalar_tensor_tensor(rows[:, 2], rows[:, 2], 1.0, n2[:], ALU.add, ALU.mult))


def first_norm(nc, g):
    with ExitStack() as c:
        sq = sbuf(nc, c, "sq", [P, 2, KD, 512])
        rs = sbuf(nc, c, "rs", [P, 2, 512])
        ps = psum(nc, c, "n_ps", (P, 2, 512))
        s = sems(nc, c, "n1", "ld0 ld1 ld2 ld3 ld4 sq sum root rec mul h st")
        ld = [s.ld0, s.ld1, s.ld2, s.ld3, s.ld4]
        with nc.Block() as block:
            @block.sync
            def _(sp):
                for b, (t0, w) in enumerate(BLOCKS):
                    sp.dma_start(g.hT[:, :, t0:t0 + w], g.xT[:, :, t0:t0 + w]).then_inc(ld[b], 16)
                for b, (t0, w) in enumerate(BLOCKS):
                    sp.wait_ge(s.h, KD * (b + 1))
                    if b:
                        sp.dma_start(g.h_d[:, :, t0:t0 + w], g.hT[:, :, t0:t0 + w]).then_inc(s.st, 16)
                sp.wait_ge(s.st, 16 * (len(BLOCKS) - 1))

            @block.scalar
            def _(act):
                def square(b):
                    t0, w = BLOCKS[b]
                    act.wait_ge(ld[b], 16)
                    wait(act, s.sum, b - 1)
                    nc.scalar.activation(sq[:, b % 2, :, 0:w], g.hT[:, :, t0:t0 + w], ACT.Square).then_inc(s.sq, 1)

                def root(b):
                    w = BLOCKS[b][1]
                    act.wait_ge(s.sum, b + 1)
                    wait(act, s.mul, b - 1)
                    nc.scalar.activation(rs[:, b % 2, 0:w], ps[:, b % 2, 0:w], ACT.Sqrt, bias=g.eps[:, 0:1], scale=1.0 / D).then_inc(s.root, 1)

                def modulate(b):
                    t0, w = BLOCKS[b]
                    act.wait_ge(s.mul, b + 1)
                    which = 1 if b == 0 else 0
                    for k in range(KD):
                        nc.scalar.activation(g.hT[:, k, t0:t0 + w], g.hT[:, k, t0:t0 + w], ACT.Identity,
                                             bias=g.mod1[:, 0, k, which:which + 1],
                                             scale=g.mod1[:, 1, k, which:which + 1]).then_inc(s.h, 1)
                for b in range(len(BLOCKS) + 2):
                    if b < len(BLOCKS):
                        square(b)
                    if 0 < b <= len(BLOCKS):
                        root(b - 1)
                    if b > 1:
                        modulate(b - 2)

            @block.tensor
            def _(pe):
                for b, (t0, w) in enumerate(BLOCKS):
                    pe.wait_ge(s.sq, b + 1)
                    wait(pe, s.root, b - 1)
                    for k in range(KD):
                        last = nc.tensor.matmul(ps[:, b % 2, 0:w], g.ones, sq[:, b % 2, k, 0:w], start=(k == 0), stop=(k == KD - 1))
                    last.then_inc(s.sum, 1)

            @block.vector
            def _(dve):
                for b, (t0, w) in enumerate(BLOCKS):
                    dve.wait_ge(s.root, b + 1)
                    nc.vector.reciprocal(rs[:, b % 2, 0:w], rs[:, b % 2, 0:w]).then_inc(s.rec, 1)
                    dve.wait_ge(s.rec, b + 1)
                    nc.vector.tensor_tensor(g.hT[:, :, t0:t0 + w], g.hT[:, :, t0:t0 + w],
                                            rs[:, b % 2, None, 0:w].broadcast_to([P, KD, w]), ALU.mult).then_inc(s.mul, 1)


BANKS = 3
NB = len(BLOCKS)
TG = [(j, min(4, NT - j)) for j in range(0, NT, 4)]
NG = len(TG)
NROT = NB - 1


def before(b):
    if b >= BANKS:
        return b - BANKS, 0
    return max(x for x in range(NB) if x % BANKS == b), 1


def windows(eng, window):
    for kind in range(3):
        window((0, kind), (0, kind - 1) if kind > 0 else None, (0, kind - 2) if kind > 1 else None)
    with eng.Fori(1, H) as h:
        for kind in range(3):
            window((h, kind), (h - (kind == 0), (kind + 2) % 3), (h - (kind < 2), (kind + 1) % 3))
    window(None, (H - 1, 2), (H - 1, 1))
    window(None, None, (H - 1, 2))


def delta_inputs(nc, g):
    with ExitStack() as c:
        w = sbuf(nc, c, "wq", [P, 3, KD, P])
        raw = sbuf(nc, c, "raw", [P, 3, CONVW])
        cv = sbuf(nc, c, "cv", [P, CONVO])
        sl = sbuf(nc, c, "sl", [P, 3, T])
        tt = sbuf(nc, c, "turned", [P, NT, P])
        rs = sbuf(nc, c, "rsb", [P, T])
        rope = sbuf(nc, c, "ropeb", [P, 2, SEQ])
        tmp = sbuf(nc, c, "tmp", [P, 512])
        cw = sbuf(nc, c, "cw", [P, H, 3, CONV])
        ps = psum(nc, c, "p_ps", (P, BANKS, 512))
        pn = psum(nc, c, "pn_ps", (P, 2, 512))
        pr = psum(nc, c, "pr_ps")
        pt = psum(nc, c, "pt_ps", (P, 2, 512))
        s = sems(nc, c, "di", "w0 w1 w2 tab zero conv proj rawp cdone silu sq sum root rec nrm perm mul rot tr trc stq stk stv stt")
        s_w = [s.w0, s.w1, s.w2]
        s_st = [s.stq, s.stk]
        dst = (g.q_d, g.k_d, g.kt_d, g.vt_d)

        with nc.Block() as block:
            @block.sync
            def _(sp):
                sp.dma_start(cw[:], g.conv_w).then_inc(s.tab, 16)
                sp.dma_start(rope[:], g.rope).then_inc(s.tab, 16)

                def store(h, tensor, src, sem):
                    sp.dma_start(tensor[0:NT, :, h].rearrange("n p c -> p n c"), src).then_inc(sem, 16)
                    sp.dma_start(tensor[NT:POS, :, h].rearrange("n p c -> p n c"), src[:, 0:CT]).then_inc(sem, 16)

                def stores(h):
                    for kind in range(2):
                        sp.wait_ge(s.rot, NROT * (2 * h + kind + 1))
                        store(h, dst[kind], sl[:, kind].rearrange("p (n c) -> p n c", c=P), s_st[kind])
                    for kind in range(2):
                        sp.wait_ge(s.trc, NG * (2 * h + kind + 1))
                        store(h, dst[2 + kind], tt[:], s.stt)
                with nc.sync.Fori(0, H) as h:
                    stores(h)
                for sem, n in ((s.stq, 32 * H), (s.stk, 32 * H), (s.stt, 64 * H)):
                    sp.wait_ge(sem, n)

            @block.gpsimd
            def _(pool):
                for kind in range(3):
                    pool.dma_start(w[:, kind], g.w_ch[kind * H]).then_inc(s_w[kind], 16)
                with nc.gpsimd.Fori(0, H - 1) as h:
                    for kind in range(3):
                        pool.wait_ge(s.proj, NB * (3 * h + kind + 1))
                        pool.dma_start(w[:, kind], g.w_ch[kind * H + h + 1]).then_inc(s_w[kind], 16)

            @block.tensor
            def _(pe):
                def project(h, kind, b):
                    t = 3 * h + kind
                    t0, wd = BLOCKS[b]
                    if b == 0:
                        pe.wait_ge(s_w[kind], 16 * h + 16)
                    bb, back = before(b)
                    pe.wait_ge(s.rawp, NB * (t + 1 - back) + bb + 1)
                    for k in range(KD):
                        last = nc.tensor.matmul(ps[:, b % BANKS, 0:wd], w[:, kind, k], g.hT[:, k, t0:t0 + wd],
                                                start=(k == 0), stop=(k == KD - 1))
                    last.then_inc(s.proj, 1)

                def turn_pairs(h, kind, b):
                    r = 2 * h + kind
                    t0, wd = BLOCKS[b + 1]
                    pe.wait_ge(s.nrm, r + 1)
                    wait(pe, s.rot, NROT * r + b)
                    nc.tensor.matmul(pr[:, 0:wd], g.rot, sl[:, kind, t0:t0 + wd], start=True, stop=True).then_inc(s.perm, 1)

                def sums(h, kind):
                    r = 2 * h + kind
                    pe.wait_ge(s.sq, r + 1)
                    for b, (t0, wd) in enumerate(BLOCKS):
                        wait(pe, s.root, NB * r + max(b - 1, 0))
                        nc.tensor.matmul(pn[:, b % 2, 0:wd], g.ones, cv[:, t0:t0 + wd], start=True, stop=True).then_inc(s.sum, 1)

                def transpose(h, kind):
                    m = 2 * h + kind - 1
                    if kind == 1:
                        pe.wait_ge(s.rot, NROT * (2 * h + 2))
                    else:
                        pe.wait_ge(s.silu, 2 * (3 * h + 3))
                    for j, (n0, cnt) in enumerate(TG):
                        wait(pe, s.trc, NG * m + max(j - 1, 0))
                        for i in range(cnt):
                            last = nc.tensor.transpose(pt[:, j % 2, i * P:(i + 1) * P],
                                                       sl[:, kind, (n0 + i) * P:(n0 + i + 1) * P], g.ident)
                        last.then_inc(s.tr, 1)

                def window(new, one, two):
                    for b in range(NB):
                        if new:
                            project(*new, b)
                        if two and two[1] < 2 and b > 0:
                            turn_pairs(*two, b - 1)
                    if one and one[1] < 2:
                        sums(*one)
                    if two and two[1] > 0:
                        transpose(*two)
                windows(nc.tensor, window)

            @block.scalar
            def _(act):
                act.sem_inc(s.rawp, NB)
                act.wait_ge(s.zero, 1)

                def copy_raw(h, kind, blocks):
                    t = 3 * h + kind
                    for b in blocks:
                        t0, wd = BLOCKS[b]
                        if b == 0:
                            wait(act, s.cdone, t - 2)
                        act.wait_ge(s.proj, NB * t + b + 1)
                        at = t0 + PAD * (1 if b == 0 else 2)
                        nc.scalar.activation(raw[:, kind, at:at + wd], ps[:, b % BANKS, 0:wd], ACT.Copy).then_inc(s.rawp, 1)

                def activate(h, kind):
                    t = 3 * h + kind
                    act.wait_ge(s.cdone, t + 1)
                    if kind < 2:
                        wait(act, s_st[kind], 32 * h)
                    if kind > 0:
                        wait(act, s.tr, NG * (2 * h + kind - 2))
                    own = Steps(act, s.silu, 2 * t)
                    own.done(nc.scalar.activation(sl[:, kind, 0:CTX], cv[:, 0:CTX], ACT.Silu))
                    own.done(nc.scalar.activation(sl[:, kind, CTX:T], cv[:, CTX + PAD:CONVO], ACT.Silu))
                    if kind < 2:
                        own.settle()
                        nc.scalar.activation(cv[:, 0:T], sl[:, kind], ACT.Square).then_inc(s.sq, 1)

                def logs(h, kind):
                    r = 2 * h + kind
                    wait(act, s.nrm, r)
                    for b, (t0, wd) in enumerate(BLOCKS):
                        act.wait_ge(s.sum, NB * r + b + 1)
                        nc.scalar.activation(rs[:, t0:t0 + wd], pn[:, b % 2, 0:wd], ACT.Ln, bias=g.eps[:, 0:1]).then_inc(s.root, 1)

                def reciprocal_roots(h, kind):
                    r = 2 * h + kind
                    act.wait_ge(s.root, NB * (r + 1))
                    nc.scalar.activation(rs[:], rs[:], ACT.Exp, scale=-0.5).then_inc(s.rec, 1)

                def copy_turned(h, kind):
                    m = 2 * h + kind - 1
                    wait(act, s.stt, 32 * m)
                    for j, (n0, cnt) in enumerate(TG):
                        act.wait_ge(s.tr, NG * m + j + 1)
                        nc.scalar.activation(tt[:, n0:n0 + cnt], pt[:, j % 2, 0:cnt * P], ACT.Copy).then_inc(s.trc, 1)

                def window(new, one, two):
                    if new:
                        copy_raw(*new, range(BANKS))
                    if one:
                        activate(*one)
                    if new:
                        copy_raw(*new, range(BANKS, NB))
                    if one and one[1] < 2:
                        logs(*one)
                    if two and two[1] > 0:
                        copy_turned(*two)
                    if one and one[1] < 2:
                        reciprocal_roots(*one)
                windows(nc.scalar, window)

            @block.vector
            def _(dve):
                nc.vector.memset(raw[:], 0.0).then_inc(s.zero, 1)
                dve.wait_ge(s.tab, 32)

                def convolve(h, kind, taps):
                    t = 3 * h + kind
                    if 0 in taps:
                        dve.wait_ge(s.rawp, NB * (t + 2))
                        wait(dve, s.silu, 2 * t)
                        if kind == 1:
                            dve.wait_ge(s.sum, NB * (2 * h + 1))
                        if kind == 2:
                            dve.wait_ge(s.sum, NB * (2 * h + 2))
                    for i in taps:
                        if i == 0:
                            ins = nc.vector.tensor_scalar(cv[:], raw[:, kind, 0:CONVO], cw[:, h, kind, 0:1], None, ALU.mult)
                        else:
                            dve.wait_ge(s.conv, (CONV - 1) * t + i)
                            ins = nc.vector.scalar_tensor_tensor(cv[:], raw[:, kind, i:i + CONVO], cw[:, h, kind, i:i + 1], cv[:],
                                                                 ALU.mult, ALU.add)
                        ins.then_inc(s.conv if i < CONV - 1 else s.cdone, 1)

                def norm(h, kind):
                    dve.wait_ge(s.rec, 2 * h + kind + 1)
                    nc.vector.scalar_tensor_tensor(sl[:, kind], rs[:], DK ** -0.5 if kind == 0 else 1.0, sl[:, kind],
                                                   ALU.mult, ALU.mult).then_inc(s.nrm, 1)

                def rotate(h, kind, b):
                    t0, wd = BLOCKS[b + 1]
                    n = NROT * (2 * h + kind) + b
                    dve.wait_ge(s.perm, n + 1)
                    wait(dve, s.rot, n)
                    own = Steps(dve, s.mul, 2 * n)
                    own.done(nc.vector.tensor_tensor(tmp[:], pr[:], rope[:, 1, b * 512:(b + 1) * 512], ALU.mult))
                    own.done(nc.vector.tensor_tensor(sl[:, kind, t0:t0 + wd], sl[:, kind, t0:t0 + wd],
                                                     rope[:, 0, b * 512:(b + 1) * 512], ALU.mult))
                    own.settle()
                    nc.vector.tensor_tensor(sl[:, kind, t0:t0 + wd], sl[:, kind, t0:t0 + wd], tmp[:],
                                            ALU.add).then_inc(s.rot, 1)

                def window(new, one, two):
                    two = two if two and two[1] < 2 else None
                    if one:
                        convolve(*one, (0, 1))
                    if two:
                        norm(*two)
                    if one:
                        convolve(*one, (2, 3))
                    if two:
                        rotate(*two, 0)
                    if one:
                        convolve(*one, (4,))
                    if two:
                        for b in range(1, NROT):
                            rotate(*two, b)
                windows(nc.vector, window)


def mixer_inputs(nc, g):
    LB = BLOCKS[1:]
    NL = len(LB)
    REST = [(16, g.qn[:, 0], False), (17, g.qn[:, 1], False), (20, g.uT[:, 0], False), (21, g.uT[:, 1], False),
            (18, g.kn[:, 0], True), (19, g.kn[:, 1], True)]
    NORM = [(g.qn[:, j, 512 * b:512 * (b + 1)], 0) for j in range(HP) for b in range(NL)]
    NORM += [(g.kn[:, j, t0:t0 + wd], 1) for j in range(HP) for t0, wd in BLOCKS]
    assert len(NORM) == NT
    with ExitStack() as c:
        w = sbuf(nc, c, "wz", [P, 2, KD, P])
        wt = sbuf(nc, c, "wt", [P, KD, 2 * P + 16])
        zb = sbuf(nc, c, "zb", [P, 2, SEQ])
        vb = sbuf(nc, c, "vb", [P, NT, 2 * P])
        sq = sbuf(nc, c, "sqn", [P, 2, 512])
        rs = sbuf(nc, c, "rsn", [P, 2, 512])
        nw = sbuf(nc, c, "nw", [P, 2])
        ps = psum(nc, c, "z_ps", (P, 5, 512))
        pn = psum(nc, c, "zn_ps")
        pt = psum(nc, c, "zt_ps", (P, 2, 512))
        s = sems(nc, c, "mi", "w0 w1 wt blk blkc ev evc z0 z1 tok vcp acp sq sum root rec nrm st")
        s_w, s_z = [s.w0, s.w1], [s.z0, s.z1]
        NZ = H
        with nc.Block() as block:
            @block.sync
            def _(sp):
                sp.dma_start(nw[:], g.na_norm).then_inc(s.wt, 16)
                sp.dma_start(wt[:], g.w_tok).then_inc(s.wt, 16)
                with nc.sync.Fori(0, NZ // 2) as i:
                    for u in range(2):
                        sp.wait_ge(s.ev, NL * (2 * i + u + 2))
                        sp.dma_start(g.z_d[2 * i + u], zb[:, u]).then_inc(s_z[u], 16)
                sp.wait_ge(s.vcp, NT)
                sp.dma_start(g.v_d.rearrange("(n p) c -> p n c", p=P), vb[:]).then_inc(s.st, 16)
                sp.wait_ge(s.z0, 16 * NZ // 2)
                sp.wait_ge(s.z1, 16 * NZ // 2)
                sp.wait_ge(s.st, 16)

            @block.gpsimd
            def _(pool):
                for n in range(NZ + len(REST)):
                    if n >= 2:
                        pool.wait_ge(s.blk, NL * (n - 1))
                    pool.dma_start(w[:, n % 2], g.w_ch[12 + n if n < NZ else REST[n - NZ][0]]).then_inc(s_w[n % 2], 16)

            @block.tensor
            def _(pe):
                def project(u, b, t0, wd):
                    for k in range(KD):
                        last = nc.tensor.matmul(ps[:, b, 0:wd], w[:, u, k], g.hT[:, k, t0:t0 + wd],
                                                start=(k == 0), stop=(k == KD - 1))
                    return last

                with nc.tensor.Fori(0, NZ // 2) as i:
                    for u in range(2):
                        pe.wait_ge(s_w[u], 16 * i + 16)
                        for b, (t0, wd) in enumerate(LB):
                            pe.wait_ge(s.ev, NL * (2 * i + u) + b + 1)
                            project(u, b, t0, wd).then_inc(s.blk, 1)
                ctxs = 0
                for n, (_, _, ctx) in enumerate(REST, NZ):
                    pe.wait_ge(s_w[n % 2], 16 * (n // 2 + 1))
                    if ctx:
                        if ctxs:
                            pe.wait_ge(s.evc, ctxs)
                        project(n % 2, NL, *BLOCKS[0]).then_inc(s.blkc, 1)
                        ctxs += 1
                    for b, (t0, wd) in enumerate(LB):
                        pe.wait_ge(s.ev, NL * n + b + 1)
                        project(n % 2, b, t0, wd).then_inc(s.blk, 1)
                pe.wait_ge(s.wt, 32)
                for i in range(NT):
                    if i >= 2:
                        pe.wait_ge(s.vcp, i - 1)
                        pe.wait_ge(s.acp, i - 1)
                    for k in range(KD):
                        last = nc.tensor.matmul(pt[:, i % 2, 0:2 * P + 16], g.hT[:, k, i * P:(i + 1) * P], wt[:, k],
                                                start=(k == 0), stop=(k == KD - 1))
                    last.then_inc(s.tok, 1)
                    wd = NORM[i][0].shape[-1]
                    pe.wait_ge(s.sq, i + 1)
                    if i:
                        pe.wait_ge(s.root, i)
                    nc.tensor.matmul(pn[:, 0:wd], g.blk, sq[:, i % 2, 0:wd], start=True, stop=True).then_inc(s.sum, 1)

            @block.scalar
            def _(act):
                act.sem_inc(s.ev, NL)
                with nc.scalar.Fori(0, NZ // 2) as i:
                    for u in range(2):
                        act.wait_ge(s_z[u], 16 * i)
                        for b in range(NL):
                            act.wait_ge(s.blk, NL * (2 * i + u) + b + 1)
                            nc.scalar.activation(zb[:, u, b * 512:(b + 1) * 512], ps[:, b], ACT.Silu).then_inc(s.ev, 1)
                ctxs = 0
                for n, (_, dst, ctx) in enumerate(REST, NZ):
                    if ctx:
                        ctxs += 1
                        act.wait_ge(s.blkc, ctxs)
                        nc.scalar.activation(dst[:, 0:CTX], ps[:, NL, 0:CTX], ACT.Copy).then_inc(s.evc, 1)
                    for b, (t0, wd) in enumerate(LB):
                        act.wait_ge(s.blk, NL * n + b + 1)
                        t0 -= 0 if ctx else CTX
                        nc.scalar.activation(dst[:, t0:t0 + wd], ps[:, b], ACT.Copy).then_inc(s.ev, 1)

                def root(i):
                    wd = NORM[i][0].shape[-1]
                    act.wait_ge(s.sum, i + 1)
                    if i >= 2:
                        act.wait_ge(s.nrm, i - 1)
                    nc.scalar.activation(rs[:, i % 2, 0:wd], pn[:, 0:wd], ACT.Sqrt, bias=g.eps[:, 0:1],
                                         scale=1.0 / DH).then_inc(s.root, 1)
                act.wait_ge(s.ev, NL * (NZ + len(REST) + 1))
                act.wait_ge(s.evc, 2)
                for i in range(NT):
                    view, _ = NORM[i]
                    wd = view.shape[-1]
                    if i >= 2:
                        act.wait_ge(s.sum, i - 1)
                    nc.scalar.activation(sq[:, i % 2, 0:wd], view, ACT.Square).then_inc(s.sq, 1)
                    act.wait_ge(s.tok, i + 1)
                    nc.scalar.activation(vb[:, i], pt[:, i % 2, 0:2 * P], ACT.Copy).then_inc(s.vcp, 1)
                    nc.scalar.activation(g.ab[:, i], pt[:, i % 2, 2 * P:2 * P + 16], ACT.Copy).then_inc(s.acp, 1)
                    if i:
                        root(i - 1)
                root(NT - 1)

            @block.vector
            def _(dve):
                dve.wait_ge(s.wt, 32)
                nc.vector.tensor_scalar(nw[:, 0:1], nw[:, 0:1], DH ** -0.5, None, ALU.mult).then_inc(s.rec, 1)

                def norm(i):
                    view, which = NORM[i]
                    wd = view.shape[-1]
                    dve.wait_ge(s.root, i + 1)
                    nc.vector.reciprocal(rs[:, i % 2, 0:wd], rs[:, i % 2, 0:wd]).then_inc(s.rec, 1)
                    dve.wait_ge(s.rec, i + 2)
                    nc.vector.scalar_tensor_tensor(view, view, nw[:, which:which + 1], rs[:, i % 2, 0:wd],
                                                   ALU.mult, ALU.mult).then_inc(s.nrm, 1)
                for i in range(NT):
                    norm(i)


def decays(nc, g):
    with ExitStack() as c:
        par = sbuf(nc, c, "par", [P, 2, 8])
        x, y, t, acc = (sbuf(nc, c, "dec" + n, [P, NT, 8]) for n in "xyta")
        ps = psum(nc, c, "dec_ps", (P, 4, POS * H))
        s = sems(nc, c, "de", "par ea ay beta own sum ex")
        with nc.Block() as block:
            @block.gpsimd
            def _(pool):
                pool.dma_start(par[:, 0], g.a_log.partition_broadcast(P)).then_inc(s.par, 16)
                pool.dma_start(par[:, 1], g.dt_bias.partition_broadcast(P)).then_inc(s.par, 16)

            @block.scalar
            def _(act):
                act.wait_ge(s.par, 32)
                nc.scalar.activation(par[:, 0], par[:, 0], ACT.Exp).then_inc(s.ea, 1)
                act.wait_ge(s.own, 2)
                nc.scalar.activation(y[:], y[:], ACT.Exp, scale=-1.0).then_inc(s.ay, 1)
                act.wait_ge(s.sum, 1)
                for d in range(2):
                    dst = g.begc[:, d], g.esfx[:, d]
                    for j in range(2):
                        nc.scalar.activation(dst[j], ps[:, 2 * d + j].rearrange("p (n h) -> p n h", h=H),
                                             ACT.Exp).then_inc(s.ex, 1)
                nc.scalar.activation(acc[:], g.ab[:, :, 8:16], ACT.Sigmoid).then_inc(s.beta, 1)

            @block.vector
            def _(dve):
                own = Steps(dve, s.own)
                v = nc.vector
                dve.wait_ge(s.par, 32)
                own.done(v.tensor_tensor(x[:], g.ab[:, :, 0:8], par[:, 1:2].broadcast_to([P, NT, 8]), ALU.add))
                own.settle()
                own.done(v.scalar_tensor_tensor(y[:], x[:], -1.0, x[:], ALU.mult, ALU.max))
                own.done(v.tensor_scalar(x[:], x[:], 0.0, None, ALU.max))
                dve.wait_ge(s.ay, 1)
                own.settle()
                own.done(v.tensor_scalar(t[:], y[:], 2.0, None, ALU.add))
                own.settle()
                own.done(v.reciprocal(t[:], t[:]))
                own.settle()
                own.done(v.tensor_tensor(y[:], y[:], t[:], ALU.mult))
                own.settle()
                own.done(v.tensor_tensor(t[:], y[:], y[:], ALU.mult))
                terms = 8
                own.settle()
                own.done(v.tensor_scalar(acc[:], t[:], 2.0 / (2 * terms + 1), 2.0 / (2 * terms - 1), ALU.mult, ALU.add))
                for m in range(terms - 2, -1, -1):
                    own.settle()
                    own.done(v.tensor_tensor(acc[:], acc[:], t[:], ALU.mult))
                    own.settle()
                    own.done(v.tensor_scalar(acc[:], acc[:], 2.0 / (2 * m + 1), None, ALU.add))
                own.settle()
                own.done(v.tensor_tensor(acc[:], acc[:], y[:], ALU.mult))
                own.settle()
                own.done(v.tensor_tensor(x[:], x[:], acc[:], ALU.add))
                own.settle()
                dve.wait_ge(s.ea, 1)
                for d in range(2):
                    own.done(v.scalar_tensor_tensor(g.gd[:, d, 0:NT], x[:, :, d * H:(d + 1) * H], -1.0,
                                                    par[:, 0:1, d * H:(d + 1) * H].broadcast_to([P, NT, H]), ALU.mult, ALU.mult))
                own.settle()
                own.done(v.tensor_copy(g.gd[:, :, NT:POS], g.gd[:, :, 0:CT]))
                dve.wait_ge(s.beta, 1)
                for d in range(2):
                    own.done(v.tensor_copy(g.beta[:, d, 0:NT], acc[:, :, d * H:(d + 1) * H]))
                own.settle()
                own.done(v.tensor_copy(g.beta[:, :, NT:POS], g.beta[:, :, 0:CT]))
                own.settle()
                own.done(v.tensor_tensor(g.begc[:], g.begc[:], g.beta[:], ALU.mult))
                own.settle()

            @block.tensor
            def _(pe):
                pe.wait_ge(s.own, 27)
                for d in range(2):
                    for j in range(2):
                        last = nc.tensor.matmul(ps[:, 2 * d + j], g.dirt(d, j), g.gd[:, d].rearrange("p n h -> p (n h)"),
                                                start=True, stop=True)
                last.then_inc(s.sum, 1)


def delta_rule(nc, g):
    STEPS = NT
    W = H * P
    with ExitStack() as c:
        def two(name):
            return [sbuf(nc, c, f"{name}{d}", [P, H, P]) for d in range(2)]
        lq, lk, lkt, lvt = ([[sbuf(nc, c, f"{n}{d}{u}", [P, H, P]) for u in range(2)] for d in range(2)]
                            for n in ("lq", "lk", "lkt", "lvt"))
        gt, dg, dec, eg, mt, tm, um, xm, qk, qg, kbg, vb, kg, ub, wb, vn, st = map(two, (
            "gt", "dg", "dec", "eg", "mt", "tm", "um", "xm", "qk", "qg", "kbg", "vbd", "kgd", "ub", "wb", "vn", "st"))
        ob = [[sbuf(nc, c, f"ob{d}{u}", [P, H, P]) for u in range(2)] for d in range(2)]
        bank = [[psum(nc, c, f"dr{d}{b}", (P, H, P)) for b in "abcd"] for d in range(2)]
        names = "ld0 ld1 gt dg mat exp kk qkp mt mt1 qkv qk px vx pb pc vt vu uw wt ws vn op su sup oe st0 st1 pool z tm1 um1 um0".split()
        s = [sems(nc, c, f"dr{d}", " ".join(names)) for d in range(2)]

        def heads(mask):
            return mask[:, None, :].broadcast_to([P, H, P])

        with nc.Block() as block:
            def pos(d, n):
                return n if d == 0 else n * -1 + (POS - 1)

            def col(t, d, at):
                return t[:, d, bass.ds(at[d], 1)].rearrange("p a h -> p (a h)")[:, :, None].broadcast_to([P, H, P])

            @block.sync
            def _(sp):
                def load(d, at, u):
                    for src, dst in ((g.q_d, lq), (g.k_d, lk), (g.kt_d, lkt), (g.vt_d, lvt)):
                        sp.dma_start(dst[d][u][:], src[at]).then_inc((s[d].ld0, s[d].ld1)[u], 16)

                def store(d, n, at, u):
                    sp.wait_ge(s[d].oe, n + 1)
                    sp.dma_start(g.o_d[d, at], ob[d][u][:]).then_inc((s[d].st0, s[d].st1)[u], 16)
                for u in range(2):
                    for d in range(2):
                        load(d, pos(d, u), u)
                with nc.sync.Fori(0, STEPS // 2 - 1) as i:
                    for u in range(2):
                        for d in range(2):
                            here, ahead = nc.sync.snap(pos(d, 2 * i + u)), nc.sync.snap(pos(d, 2 * i + u + 2))
                            sp.wait_ge(s[d].su, 2 * i + u + 1)
                            load(d, ahead, u)
                            store(d, 2 * i + u, here, u)
                for u in range(2):
                    for d in range(2):
                        store(d, STEPS - 2 + u, pos(d, STEPS - 2 + u), u)
                for d in range(2):
                    sp.wait_ge(s[d].st0, 16 * STEPS // 2)
                    sp.wait_ge(s[d].st1, 16 * STEPS // 2)

            @block.gpsimd
            def _(pool):
                tt = nc.gpsimd.tensor_tensor
                for d in range(2):
                    nc.gpsimd.memset(st[d][:], 0.0).then_inc(s[d].z, 1)

                with nc.gpsimd.Fori(0, STEPS // 2) as i:
                    for u in range(2):
                        n = 2 * i + u
                        at = [nc.gpsimd.snap(pos(d, n)) for d in range(2)]
                        for d in range(2):
                            q = s[d]
                            pool.wait_ge(q.mat, n)
                            tt(dg[d][:], heads(g.ident), col(g.beta, d, at), ALU.mult).then_inc(q.dg, 1)
                        for d in range(2):
                            q = s[d]
                            pool.wait_ge(q.uw, n)
                            pool.wait_ge(q.mt, n + 1)
                            tt(um[d][:], mt[d][:], heads(g.level(1 - d, 0)), ALU.mult).then_inc(q.um1, 1)
                            pool.wait_ge(q.um1, n + 1)
                            tt(um[d][:], heads(g.ident), um[d][:], ALU.subtract).then_inc(q.um0, 1)
                        for d in range(2):
                            q = s[d]
                            pool.wait_ge((q.ld0, q.ld1)[u], 64 * i + 64)
                            pool.wait_ge(q.uw, n)
                            tt(kbg[d][:], lkt[d][u][:], col(g.begc, d, at), ALU.mult).then_inc(q.pool, 1)
                            tt(vb[d][:], lvt[d][u][:], col(g.beta, d, at), ALU.mult).then_inc(q.pool, 1)
                            pool.wait_ge(q.su, n)
                            tt(kg[d][:], lkt[d][u][:], col(g.esfx, d, at), ALU.mult).then_inc(q.pool, 1)
                            pool.wait_ge(q.op, n)
                            pool.wait_ge(q.exp, 2 * n + 2)
                            tt(qg[d][:], lq[d][u][:], eg[d][:], ALU.mult).then_inc(q.pool, 1)
                            pool.wait_ge(q.qkv, n + 1)
                            tt(qk[d][:], qk[d][:], heads(g.dirt(d, 0)), ALU.mult).then_inc(q.qk, 1)

            @block.scalar
            def _(act):
                def step(i, u):
                    n = 2 * i + u
                    for d in range(2):
                        q, (A, B, C_, D_) = s[d], bank[d]
                        act.wait_ge(q.mat, n + 1)
                        act.wait_ge(q.qkv, n)
                        nc.scalar.activation(dec[d][:], A[:], ACT.Exp).then_inc(q.exp, 1)
                        act.wait_ge(q.sup, n)
                        act.wait_ge(q.pool, 4 * n)
                        nc.scalar.activation(eg[d][:], B[:], ACT.Exp).then_inc(q.exp, 1)
                    for d in range(2):
                        q, (A, B, C_, D_) = s[d], bank[d]
                        act.wait_ge(q.uw, n + 1)
                        act.wait_ge(q.ws, n)
                        nc.scalar.activation(wb[d][:], A[:], ACT.Copy).then_inc(q.wt, 1)
                        act.wait_ge(q.vn, n)
                        nc.scalar.activation(ub[d][:], D_[:], ACT.Copy).then_inc(q.wt, 1)
                    for d in range(2):
                        q, (A, B, C_, D_) = s[d], bank[d]
                        act.wait_ge(q.op, n + 1)
                        act.wait_ge((q.st0, q.st1)[u], 16 * i)
                        nc.scalar.activation(ob[d][u][:], C_[:], ACT.Copy).then_inc(q.oe, 1)

                with nc.scalar.Fori(0, STEPS // 2) as i:
                    for u in range(2):
                        step(i, u)

            @block.tensor
            def _(pe):
                def each(out, lhs, rhs):
                    for h in range(H):
                        last = nc.tensor.matmul(out[:, h], lhs[:, h], g.ident if rhs is None else rhs[:, h], start=True, stop=True)
                    return last

                with nc.tensor.Fori(0, STEPS // 2) as i:
                    for u in range(2):
                        n = 2 * i + u
                        for d in range(2):
                            q, (A, B, C_, D_) = s[d], bank[d]
                            flat = gt[d][:].rearrange("p h i -> p (h i)")
                            pe.wait_ge(q.gt, n + 1)
                            pe.wait_ge(q.dg, n + 1)
                            pe.wait_ge(q.wt, 2 * n)
                            pe.wait_ge(q.vn, n)
                            pe.wait_ge(q.oe, n)
                            nc.tensor.matmul(A[:].rearrange("p h i -> p (h i)"), g.dirt(d, 1), flat, start=True, stop=True)
                            nc.tensor.matmul(B[:].rearrange("p h i -> p (h i)"), g.ones, flat, start=True, stop=True)
                            nc.tensor.matmul(C_[:].rearrange("p h i -> p (h i)"), g.dirt(d, 1),
                                             dg[d][:].rearrange("p h i -> p (h i)"), start=True, stop=True).then_inc(q.mat, 1)
                            pe.wait_ge((q.ld0, q.ld1)[u], 64 * i + 64)
                            pe.wait_ge(q.sup, n)
                            each(D_, lk[d][u], lk[d][u]).then_inc(q.kk, 1)
                        for d in range(2):
                            q, (A, B, C_, D_) = s[d], bank[d]
                            pe.wait_ge(q.mt, n + 1)
                            each(B, mt[d], None).then_inc(q.px, 1)
                        for d in range(2):
                            q, (A, B, C_, D_) = s[d], bank[d]
                            each(C_, lk[d][u], lq[d][u]).then_inc(q.qkp, 1)
                        for lev in range(1, N_LEV):
                            for d in range(2):
                                q, (A, B, C_, D_) = s[d], bank[d]
                                pe.wait_ge(q.vt, (N_LEV - 1) * n + lev)
                                each(A, mt[d], tm[d]).then_inc(q.px, 1)
                            for d in range(2):
                                q, (A, B, C_, D_) = s[d], bank[d]
                                pe.wait_ge(q.vx, (N_LEV - 1) * n + lev)
                                if lev == 1:
                                    pe.wait_ge(q.um0, n + 1)
                                    pe.wait_ge(q.qkv, n + 1)
                                else:
                                    pe.wait_ge(q.vu, (N_LEV - 1) * n + lev - 1)
                                if lev < N_LEV - 1:
                                    each(B, um[d], xm[d]).then_inc(q.pb, 1)
                                each(C_, xm[d], um[d]).then_inc(q.pc, 1)
                        for d in range(2):
                            q, (A, B, C_, D_) = s[d], bank[d]
                            pe.wait_ge(q.vu, (N_LEV - 1) * (n + 1))
                            pe.wait_ge(q.pool, 4 * n + 2)
                            each(D_, um[d], vb[d])
                            each(A, kbg[d], um[d]).then_inc(q.uw, 1)
                        for d in range(2):
                            q, (A, B, C_, D_) = s[d], bank[d]
                            pe.wait_ge(q.wt, 2 * n + 1)
                            pe.wait_ge(q.sup, n)
                            pe.wait_ge(q.z, 1)
                            each(B, wb[d], st[d]).then_inc(q.ws, 1)
                        for d in range(2):
                            q, (A, B, C_, D_) = s[d], bank[d]
                            pe.wait_ge(q.vn, n + 1)
                            pe.wait_ge(q.pool, 4 * n + 4)
                            pe.wait_ge(q.qk, n + 1)
                            for h in range(H):
                                nc.tensor.matmul(C_[:, h], st[d][:, h], qg[d][:, h], start=True, stop=False)
                                last = nc.tensor.matmul(C_[:, h], vn[d][:, h], qk[d][:, h], start=False, stop=True)
                            last.then_inc(q.op, 1)
                            each(D_, kg[d], vn[d]).then_inc(q.su, 1)

            @block.vector
            def _(dve):
                v = nc.vector

                def gates(at):
                    for d in range(2):
                        v.tensor_tensor(gt[d][:], heads(g.dirt(d, 0)), col(g.gd, d, at), ALU.mult).then_inc(s[d].gt, 1)
                gates([pos(d, 0) for d in range(2)])
                with nc.vector.Fori(0, STEPS // 2) as i:
                    for u in range(2):
                        n = 2 * i + u
                        ahead = [nc.vector.snap(pos(d, n + 1)) for d in range(2)]
                        for d in range(2):
                            q, (A, B, C_, D_) = s[d], bank[d]
                            dve.wait_ge(q.exp, 2 * n + 2)
                            dve.wait_ge(q.px, N_LEV * n)
                            v.tensor_tensor(mt[d][:], dec[d][:], C_[:], ALU.mult).then_inc(q.mt1, 1)
                            dve.wait_ge(q.mt1, n + 1)
                            dve.wait_ge(q.kk, n + 1)
                            v.tensor_tensor(mt[d][:], mt[d][:], D_[:], ALU.mult).then_inc(q.mt, 1)
                        for d in range(2):
                            q, (A, B, C_, D_) = s[d], bank[d]
                            dve.wait_ge(q.px, N_LEV * n + 1)
                            v.tensor_tensor(tm[d][:], B[:], heads(g.level(d, 0)), ALU.mult).then_inc(q.tm1, 1)
                            dve.wait_ge(q.tm1, n + 1)
                            v.scalar_tensor_tensor(tm[d][:], tm[d][:], -1.0, heads(g.ident), ALU.mult, ALU.add).then_inc(q.vt, 1)
                        for lev in range(1, N_LEV):
                            for d in range(2):
                                q, (A, B, C_, D_) = s[d], bank[d]
                                if lev == 1:
                                    dve.wait_ge(q.qkp, n + 1)
                                    dve.wait_ge(q.op, n)
                                    v.tensor_tensor(qk[d][:], C_[:], dec[d][:], ALU.mult).then_inc(q.qkv, 1)
                                dve.wait_ge(q.px, N_LEV * n + lev + 1)
                                v.tensor_tensor(xm[d][:], A[:], heads(g.level(d, lev)), ALU.mult).then_inc(q.vx, 1)
                            for d in range(2):
                                q, (A, B, C_, D_) = s[d], bank[d]
                                if lev < N_LEV - 1:
                                    dve.wait_ge(q.pb, (N_LEV - 2) * n + lev)
                                    v.tensor_tensor(tm[d][:], tm[d][:], B[:], ALU.subtract).then_inc(q.vt, 1)
                                dve.wait_ge(q.pc, (N_LEV - 1) * n + lev)
                                v.tensor_tensor(um[d][:], um[d][:], C_[:], ALU.subtract).then_inc(q.vu, 1)
                        for d in range(2):
                            q, (A, B, C_, D_) = s[d], bank[d]
                            dve.wait_ge(q.ws, n + 1)
                            dve.wait_ge(q.wt, 2 * n + 2)
                            dve.wait_ge(q.su, n)
                            v.tensor_tensor(vn[d][:], ub[d][:], B[:], ALU.subtract).then_inc(q.vn, 1)
                        gates(ahead)
                        for d in range(2):
                            q, (A, B, C_, D_) = s[d], bank[d]
                            last_tok = P - 1 if d == 0 else 0
                            dve.wait_ge(q.su, n + 1)
                            for h in range(H):
                                last = v.scalar_tensor_tensor(st[d][:, h], st[d][:, h], eg[d][:, h, last_tok:last_tok + 1],
                                                              D_[:, h], ALU.mult, ALU.add)
                            last.then_inc(q.sup, 1)


def wait(eng, sem, value):
    if not isinstance(value, int) or value > 0:
        eng.wait_ge(sem, value)


def attention(nc, g):
    UNITS = ROWS * HP
    LOC = WR * GRID
    KEYS = LOC + CTX
    KT = KEYS // P
    FREE = g.hT.rearrange("p k t -> p (k t)")
    v0 = FREE[:, 0:NT * 2 * P].rearrange("p (n c) -> p n c", c=2 * P)
    v1 = FREE[:, NT * 2 * P:(NT + LT - 1) * 2 * P].rearrange("p (n c) -> p n c", c=2 * P)
    first_in, last_in = WR // 4, (ROWS - WR // 2) // 2

    def place(i, k):
        odd, hp = k // 2, k % 2
        r = 2 * i + odd
        if isinstance(i, int):
            rs = min(max(r - WR // 2, 0), ROWS - WR)
            shift = r - rs
            vi = (rs - rs % 2) // 2
            return r, rs, vi, rs % 2, WR - 1 - shift
        return r, r - WR // 2, i - WR // 4, odd, WR - 1 - WR // 2

    def units(eng, body):
        for i in range(first_in + 1):
            for k in range(4):
                body(i, k)
        with eng.Fori(first_in + 1, last_in) as i:
            for k in range(4):
                body(i, k)
        for i in range(last_in, ROWS // 2):
            for k in range(4):
                body(i, k)

    def early(i, k, n):
        return isinstance(i, int) and 4 * i + k < n

    def back(i, k, n):
        return (i, k - n) if k >= n else (i - 1, k - n + 4)

    def late(i, k, n):
        return isinstance(i, int) and 4 * i + k + n >= UNITS

    def ahead(i, k, n):
        return (i, k + n) if k + n < 4 else (i + 1, k + n - 4)

    with ExitStack() as c:
        rpad = sbuf(nc, c, "rpad", [H * 15, 127])
        bt = sbuf(nc, c, "bt", [P, HP, 15, GRID])
        qb = sbuf(nc, c, "qb", [P, 2, 2 * GRID])
        sb = sbuf(nc, c, "scores", [P, 2, KEYS])
        pb = sbuf(nc, c, "probs", [P, 2, KEYS])
        pt = sbuf(nc, c, "probs_t", [P, 2, KT, P])
        mx = sbuf(nc, c, "mx", [P, 2, 4])
        ob = sbuf(nc, c, "ao", [P, 2, P])
        oc = sbuf(nc, c, "aoT", [P, 2, HP, GRID])
        loc = psum(nc, c, "loc_ps", (P, 2, 512))
        cx = psum(nc, c, "cx_ps", (P, 2, 512))
        tp = psum(nc, c, "tp_ps", (P, 2, 512))
        po = psum(nc, c, "po_ps")
        pot = psum(nc, c, "pot_ps")
        s = sems(nc, c, "at", "v pad z rp sk bt0 qb sc cx add mx nm ex rc tp ptd pta o oe ot ote st0 st1")
        s_st = [s.st0, s.st1]
        with nc.Block() as block:
            @block.sync
            def _(sp):
                sp.dma_start(v0, g.v_d.rearrange("(n p) c -> p n c", p=P)).then_inc(s.v, 16)
                sp.dma_start(v1, g.v_d[CTX + GRID:T - GRID].rearrange("(n p) c -> p n c", p=P)).then_inc(s.v, 16)
                sp.wait_ge(s.z, 1)
                sp.dma_start(rpad[:, 48:79], g.rpb).then_inc(s.rp, 16)
                sp.wait_ge(s.rp, 16)
                sp.dma_start(g.skew_d, rpad[:, None, :].broadcast_to([H * 15, GRID, 127])).then_inc(s.sk, 16)
                sp.wait_ge(s.sk, 16)
                for h in range(H):
                    src = g.skew_d[h * 15:(h + 1) * 15].rearrange("r j c -> r (j c)")
                    src = src[:, 63:63 + GRID * 126].rearrange("r (j c) -> j r c", c=126)[:, :, 0:GRID]
                    half = h % 2
                    sp.dma_start(bt[half * GRID:(half + 1) * GRID, h // 2], src).then_inc(s.bt0, 16)

                dst = g.oc_d.rearrange("(q p) (r t) -> p r q t", q=HP, t=GRID)

                def store(i, odd):
                    r = 2 * i + odd
                    sp.wait_ge(s.ote, 2 * (4 * i + 2 * odd + 2))
                    sp.dma_start(dst[:, bass.ds(r, 1)].rearrange("p r q t -> p (r q) t"), oc[:, odd]).then_inc(s_st[odd], 16)
                with nc.sync.Fori(0, ROWS // 2) as i:
                    for odd in range(2):
                        store(i, odd)
                for sem in s_st:
                    sp.wait_ge(sem, 8 * ROWS)

            @block.gpsimd
            def _(pool):
                nc.gpsimd.memset(rpad[:], 0.0).then_inc(s.z, 1)

                def body(i, k):
                    U = 4 * i + k
                    r = place(i, k)[0]
                    at = r * GRID if isinstance(i, int) else nc.gpsimd.snap(r * GRID)
                    wait(pool, s.sc, U - 1)
                    nc.gpsimd.tensor_tensor(qb[:, k % 2].rearrange("p (a t) -> p a t", a=2),
                                            g.qn[:, k % 2, bass.ds(at, GRID)][:, None, :].broadcast_to([P, 2, GRID]),
                                            g.blk.rearrange("p (a t) -> p a t", a=2), ALU.mult).then_inc(s.qb, 1)
                units(nc.gpsimd, body)

            @block.tensor
            def _(pe):
                def scores(i, k):
                    U, u = 4 * i + k, k % 2
                    _, rs, _, _, _ = place(i, k)
                    pe.wait_ge(s.qb, U + 1)
                    wait(pe, s.add, U - 1)
                    wait(pe, s.cx, U - 1)
                    nc.tensor.matmul(loc[:, u, 0:LOC], qb[:, u], g.kn[:, k % 2, bass.ds(CTX + rs * GRID, LOC)], start=True, stop=True)
                    nc.tensor.matmul(cx[:, u, 0:CTX], qb[:, u], g.kn[:, k % 2, 0:CTX], start=True, stop=True).then_inc(s.sc, 1)

                def turn(i, k):
                    U, u = 4 * i + k, k % 2
                    pe.wait_ge(s.ex, U + 1)
                    for b in range(2):
                        wait(pe, (s.ptd, s.pta)[b], U)
                        for j in range(KT // 2):
                            n = b * (KT // 2) + j
                            last = nc.tensor.transpose(tp[:, b, j * P:(j + 1) * P], pb[:, u, n * P:(n + 1) * P], g.ident)
                        last.then_inc(s.tp, 1)

                def values(i, k):
                    U, u, hp = 4 * i + k, k % 2, k % 2
                    _, _, vi, shifted, _ = place(i, k)
                    pe.wait_ge(s.ptd, U + 1)
                    pe.wait_ge(s.pta, U + 1)
                    wait(pe, s.oe, U)
                    cols = slice(hp * P, (hp + 1) * P)
                    for n in range(KT):
                        if n < KT - CT:
                            v = v1[:, bass.ds(vi + n, 1), cols] if shifted else v0[:, bass.ds(vi + n + CT, 1), cols]
                            v = v.rearrange("p a c -> p (a c)")
                        else:
                            v = v0[:, n - (KT - CT), cols]
                        last = nc.tensor.matmul(po[:, 0:P], pt[:, u, n], v, start=(n == 0), stop=(n == KT - 1))
                    last.then_inc(s.o, 1)

                def turn_out(i, k):
                    U, u = 4 * i + k, k % 2
                    pe.wait_ge(s.oe, U + 1)
                    wait(pe, s.ote, 2 * U)
                    nc.tensor.transpose(pot[:, 0:P], ob[:, u], g.ident).then_inc(s.ot, 1)

                def body(i, k):
                    turn(i, k)
                    if not early(i, k, 1):
                        turn_out(*back(i, k, 1))
                    if not late(i, k, 2):
                        scores(*ahead(i, k, 2))
                    values(i, k)
                pe.wait_ge(s.v, 32)
                scores(0, 0)
                scores(0, 1)
                units(nc.tensor, body)
                turn_out(ROWS // 2 - 1, 3)

            @block.scalar
            def _(act):
                def context(i, k):
                    U, u = 4 * i + k, k % 2
                    act.wait_ge(s.sc, U + 1)
                    wait(act, s.ex, U - 1)
                    nc.scalar.activation(sb[:, u, LOC:KEYS], cx[:, u, 0:CTX], ACT.Copy).then_inc(s.cx, 1)

                def exps(i, k):
                    U, u = 4 * i + k, k % 2
                    act.wait_ge(s.nm, U + 1)
                    wait(act, s.tp, 2 * (U - 1))
                    wait(act, s.rc, U - 1)
                    nc.scalar.activation(pb[:, u], sb[:, u], ACT.Exp, bias=mx[:, u, 1:2], accum_out=mx[:, u, 2:3]).then_inc(s.ex, 1)

                def copy_pt(i, k):
                    U, u = 4 * i + k, k % 2
                    act.wait_ge(s.tp, 2 * U + 2)
                    wait(act, s.o, U - 1)
                    nc.scalar.activation(pt[:, u, KT // 2:KT], tp[:, 1, 0:KT // 2 * P].rearrange("p (n c) -> p n c", c=P), ACT.Copy).then_inc(s.pta, 1)

                def out(i, k):
                    U, u = 4 * i + k, k % 2
                    act.wait_ge(s.o, U + 1)
                    act.wait_ge(s.rc, U + 1)
                    wait(act, s.ot, U - 1)
                    nc.scalar.activation(ob[:, u], po[:, 0:P], ACT.Copy, scale=mx[:, u, 3:4]).then_inc(s.oe, 1)

                def out_t(i, k):
                    U, odd, hp = 4 * i + k, k // 2, k % 2
                    act.wait_ge(s.ot, U + 1)
                    wait(act, s_st[odd], 16 * i)
                    for a in range(2):
                        half = slice(a * DH, (a + 1) * DH)
                        nc.scalar.activation(oc[half, odd, hp], pot[half, half], ACT.Copy).then_inc(s.ote, 1)

                def body(i, k):
                    copy_pt(i, k)
                    if not late(i, k, 2):
                        context(*ahead(i, k, 2))
                    if not early(i, k, 1):
                        out_t(*back(i, k, 1))
                    out(i, k)
                    if not late(i, k, 2):
                        exps(*ahead(i, k, 2))
                for k in range(2):
                    context(0, k)
                    exps(0, k)
                units(nc.scalar, body)
                out_t(ROWS // 2 - 1, 3)

            @block.vector
            def _(dve):
                v = nc.vector

                def softmax(i, k):
                    U, u = 4 * i + k, k % 2
                    dr = place(i, k)[4]
                    dve.wait_ge(s.sc, U + 1)
                    wait(dve, s.ex, U - 1)
                    v.tensor_tensor(sb[:, u, 0:LOC], loc[:, u, 0:LOC], bt[:, k % 2, dr:dr + WR].rearrange("p r c -> p (r c)"),
                                    ALU.add).then_inc(s.add, 1)
                    dve.wait_ge(s.add, U + 1)
                    dve.wait_ge(s.cx, U + 1)
                    v.reduce_max(mx[:, u, 0:1], sb[:, u], AX_X).then_inc(s.mx, 1)
                    dve.wait_ge(s.mx, U + 1)
                    v.tensor_scalar(mx[:, u, 1:2], mx[:, u, 0:1], -1.0, None, ALU.mult).then_inc(s.nm, 1)

                def rest(i, k):
                    U, u = 4 * i + k, k % 2
                    dve.wait_ge(s.ex, U + 1)
                    wait(dve, s.oe, U - 1)
                    v.reciprocal(mx[:, u, 3:4], mx[:, u, 2:3]).then_inc(s.rc, 1)
                    dve.wait_ge(s.tp, 2 * U + 1)
                    wait(dve, s.o, U - 1)
                    v.tensor_copy(pt[:, u, 0:KT // 2], tp[:, 0, 0:KT // 2 * P].rearrange("p (n c) -> p n c", c=P)).then_inc(s.ptd, 1)

                def body(i, k):
                    rest(i, k)
                    if not late(i, k, 2):
                        softmax(*ahead(i, k, 2))
                dve.wait_ge(s.bt0, 64)
                for hp in range(HP):
                    v.tensor_tensor(bt[:, hp], bt[:, hp], g.window[:, None, :].broadcast_to([P, 15, GRID]), ALU.add).then_inc(s.pad, 1)
                dve.wait_ge(s.pad, 2)
                softmax(0, 0)
                softmax(0, 1)
                units(nc.vector, body)


def fourier(nc, g):
    N1, N2 = P, SEQ // P
    LO = P // N2
    HI = N1 // LO
    FREE = g.hT.rearrange("p k t -> p (k t)")
    ab = FREE[:, 0:2 * N2 * FN].rearrange("p (s n c) -> p s n c", s=2, n=N2)
    zin = FREE[:, 2 * N2 * FN:4 * N2 * FN].rearrange("p (s h c) -> p s h c", s=2, h=HI)
    CH = N2 // 2
    with ExitStack() as c:
        ft = sbuf(nc, c, "ft", [P, F_W])
        zc = sbuf(nc, c, "zc", [P, 2, 4, 512])
        zs = sbuf(nc, c, "zs", [P, 2, 2, 512])
        y = sbuf(nc, c, "yf", [P, 2, 512])
        ybt = sbuf(nc, c, "ybt", [P, 2, SEQ])
        pa = psum(nc, c, "fa_ps", (P, 2, 512))
        pz = psum(nc, c, "fz_ps", (P, 2, 2, 512))
        pq = psum(nc, c, "fq_ps", (P, 2, 512))
        s = sems(nc, c, "fo", "ft pa ae pz m zz zst0 zst1 re py ye pq qe st")
        c4 = ft[:, F_C4:F_C4 + FN]
        dft = [ft[:, F_N1 + j * P:F_N1 + (j + 1) * P] for j in range(3)]
        twc, tws = (ft[:, F_TW + j * N2:F_TW + (j + 1) * N2] for j in range(2))
        k2c, k2s = (ft[:, F_K2 + j * P:F_K2 + (j + 1) * P] for j in range(2))
        with nc.Block() as block:
            @block.sync
            def _(sp):
                sp.dma_start(ft[:], g.ftab).then_inc(s.ft, 16)
                for q in range(CH):
                    sp.wait_ge(s.zz, 2 * q + 2)
                    sp.dma_start(g.z2_d[:, :, 2 * q:2 * q + 2].rearrange("s k n c -> k s (n c)"), zs[:, q % 2]).then_inc((s.zst0, s.zst1)[q % 2], 16)
                sp.wait_ge(s.zst0, 16 * CH // 2)
                sp.wait_ge(s.zst1, 16 * CH // 2)
                for n in range(N2):
                    for j in range(2):
                        sp.dma_start(zin[n * LO:(n + 1) * LO, j], g.z2_d[j, :, n].rearrange("(h l) c -> l h c", l=LO)).then_inc(s.re, 16)
                sp.wait_ge(s.qe, 2 * HI // 2)
                sp.dma_start(g.yb_d.rearrange("(a p) t -> p a t", p=P), ybt[:]).then_inc(s.st, 16)
                sp.wait_ge(s.st, 16)

            @block.tensor
            def _(pe):
                pe.wait_ge(s.ft, 16)
                for n in range(N2):
                    wait(pe, s.ae, n - 1)
                    for cc in range(2):
                        last = nc.tensor.matmul(pa[:, n % 2, cc * FN:(cc + 1) * FN], g.uT[:, cc, n:SEQ:N2], c4, start=True, stop=True)
                    last.then_inc(s.pa, 1)
                pe.wait_ge(s.ae, N2)
                for q in range(CH):
                    wait(pe, s.m, 4 * (q - 1))
                    a, b = (ab[:, j, 2 * q:2 * q + 2].rearrange("p n c -> p (n c)") for j in range(2))
                    re, im = pz[:, q % 2, 0], pz[:, q % 2, 1]
                    nc.tensor.matmul(re, dft[0], a, start=True, stop=False)
                    nc.tensor.matmul(re, dft[2], b, start=False, stop=True)
                    nc.tensor.matmul(im, dft[0], b, start=True, stop=False)
                    nc.tensor.matmul(im, dft[1], a, start=False, stop=True).then_inc(s.pz, 1)
                pe.wait_ge(s.re, 16 * 2 * N2)
                for q in range(HI // 2 + 1):
                    if q < HI // 2:
                        wait(pe, s.ye, q - 1)
                        for j in range(2):
                            last = nc.tensor.matmul(pa[:, q % 2], (k2c, k2s)[j], zin[:, j, 2 * q:2 * q + 2].rearrange("p h c -> p (h c)"),
                                                    start=(j == 0), stop=(j == 1))
                        last.then_inc(s.py, 1)
                    if q:
                        r = q - 1
                        pe.wait_ge(s.ye, r + 1)
                        wait(pe, s.qe, 2 * (r - 1))
                        for j in range(4):
                            last = nc.tensor.transpose(pq[:, r % 2, j * P:(j + 1) * P], y[:, r % 2, j * P:(j + 1) * P], g.ident)
                        last.then_inc(s.pq, 1)

            @block.scalar
            def _(act):
                for n in range(N2):
                    act.wait_ge(s.pa, n + 1)
                    nc.scalar.activation(ab[:, :, n].rearrange("p s (a x) -> p a s x", a=2),
                                         pa[:, n % 2].rearrange("p (a s x) -> p a s x", a=2, s=2), ACT.Copy).then_inc(s.ae, 1)
                for q in range(HI // 2):
                    act.wait_ge(s.py, q + 1)
                    wait(act, s.pq, q - 1)
                    nc.scalar.activation(y[:, q % 2], pa[:, q % 2], ACT.Copy).then_inc(s.ye, 1)

            @block.vector
            def _(dve):
                v = nc.vector
                for q in range(CH):
                    u = q % 2
                    dve.wait_ge(s.pz, q + 1)
                    wait(dve, s.zz, 2 * (q - 1))
                    tw = [t[:, 2 * q:2 * q + 2, None].broadcast_to([P, 2, FN]) for t in (twc, tws)]
                    for j, (part, t) in enumerate(((0, 0), (1, 1), (1, 0), (0, 1))):
                        v.tensor_tensor(zc[:, u, j].rearrange("p (n c) -> p n c", n=2), pz[:, u, part].rearrange("p (n c) -> p n c", n=2),
                                        tw[t], ALU.mult).then_inc(s.m, 1)
                for q in range(HI // 2):
                    dve.wait_ge(s.pq, q + 1)
                    for j in range(2):
                        k1 = (2 * q + j) * LO
                        out = ybt[:].rearrange("p a (k t) -> p a k t", t=N1)[:, :, :, k1:k1 + LO]
                        v.tensor_copy(out, pq[:, q % 2, j * FN:(j + 1) * FN].rearrange("p (a k t) -> p a k t", a=2, t=LO)).then_inc(s.qe, 1)

            @block.gpsimd
            def _(pool):
                for q in range(CH):
                    u = q % 2
                    pool.wait_ge(s.m, 4 * q + 4)
                    wait(pool, (s.zst0, s.zst1)[u], 16 * (q // 2))
                    nc.gpsimd.tensor_tensor(zs[:, u, 0], zc[:, u, 0], zc[:, u, 1], ALU.subtract).then_inc(s.zz, 1)
                    nc.gpsimd.tensor_tensor(zs[:, u, 1], zc[:, u, 2], zc[:, u, 3], ALU.add).then_inc(s.zz, 1)


def merge(nc, g):
    NBK = SEQ // 512
    BT = 512 // P
    NBR = 3
    NC = NBR + 1
    WB = NBR
    BRANCH = [(0, H), (H, H + 2), (H + 2, KD)]
    with ExitStack() as c:
        hb = sbuf(nc, c, "hb", [P, KD, 512])
        of = sbuf(nc, c, "of", [P, 2, BT * H * P])
        zt = sbuf(nc, c, "zt", [P, H, 512])
        ob = sbuf(nc, c, "obr", [P, KD, 512])
        hh, hl, oh, ol = (sbuf(nc, c, n, [P, KD, 512], F32R) for n in ("hb_high", "hb_low", "obr_high", "obr_low"))
        w = sbuf(nc, c, "wm", [P, NC, KD * P])
        wh, wl = (sbuf(nc, c, n, [P, NC, KD * P], F32R) for n in ("wm_high", "wm_low"))
        gnw = sbuf(nc, c, "gnw", [P, 1])
        sg = sbuf(nc, c, "sg", [P, NBR, 512])
        pr = sbuf(nc, c, "prm", [P, NBR, 512])
        yb = sbuf(nc, c, "yTb", [P, 2, 512])
        pg = [psum(nc, c, f"pg{n}") for n in range(NBR)]
        pbr = [psum(nc, c, f"pbr{n}") for n in range(NBR)]
        pn = [psum(nc, c, f"pnm{n}") for n in range(2)]
        s = sems(nc, c, "me", "cst ldo ldh w0 w1 w2 w3 wh wl hh hl oh ol osum sq sum root rec oa gate sig br prod add y y0 y1 held")
        s_w, s_y = [s.w0, s.w1, s.w2, s.w3], [s.y0, s.y1]
        scans = [of[:, d].rearrange("p (b h i) -> p b h i", b=BT, h=H) for d in range(2)]
        roots, squares = (of[:, d].rearrange("p (h t) -> p h t", h=H) for d in range(2))
        SIG0, PROD0, WL0 = NBR, NBR, NC

        def blocks(eng, block):
            block(0, True)
            with eng.Fori(1, NBK - 1) as b:
                block(b, True)
            block(NBK - 1, False)

        def tiles(eng, b, more, tile):
            for u in range(2):
                tile(b * KD + u, u, u == 0, None, False)
            with eng.Fori(1, KD // 2 - 1) as jj:
                for u in range(2):
                    tile(b * KD + jj * 2 + u, u, False, None, False)
            for u in range(2):
                tile(b * KD + KD - 2 + u, u, False, u if more else None, not more and u == 1)

        with nc.Block() as block:
            @block.sync
            def _(sp):
                sp.dma_start(gnw[:], g.gdn_norm).then_inc(s.cst, 16)
                with nc.sync.Fori(0, NBK) as b:
                    with nc.sync.Fori(0, KD) as j:
                        m = b * KD + j
                        at = nc.sync.snap(j + 0)
                        for n in range(NC):
                            sp.wait_ge(s.wl, NC * m + n + 1)
                            sp.dma_start(w[:, n], g.w_br[at] if n == WB else g.w_gates[at, :, n]).then_inc(s_w[n], 16)

            @block.gpsimd
            def _(pool):
                def load_delta(b):
                    pos, t0 = b * BT + CT, b * 512
                    for d in range(2):
                        pool.dma_start(scans[d], g.o_d[d, bass.ds(pos, BT)].rearrange("n p h c -> p n h c")).then_inc(s.ldo, 16)
                    pool.dma_start(zt[:], g.z_d[:, :, bass.ds(t0, 512)].rearrange("h p t -> p h t")).then_inc(s.ldo, 16)

                def load_rest(b):
                    t0 = b * 512
                    pool.dma_start(hb[:], g.h_d[:, :, bass.ds(t0 + CTX, 512)]).then_inc(s.ldh, 16)
                    pool.dma_start(ob[:, H:H + 2], g.yb_d[:, bass.ds(t0, 512)].rearrange("(a p) t -> p a t", p=P)).then_inc(s.ldh, 16)
                    pool.dma_start(ob[:, H + 2:KD], g.oc_d[:, bass.ds(t0, 512)].rearrange("(a p) t -> p a t", p=P)).then_inc(s.ldh, 16)

                def stores(b):
                    t0 = b * 512 if isinstance(b, int) else nc.gpsimd.snap(b * 512)
                    with nc.gpsimd.Fori(0, KD // 2) as jj:
                        for u in range(2):
                            j = nc.gpsimd.snap(jj * 2 + u)
                            pool.wait_ge(s.y, b * KD + jj * 2 + u + 1)
                            hold(pool, s.held)
                            pool.dma_start(g.y_d[:, bass.ds(j, 1), bass.ds(t0, 512)].rearrange("p a t -> p (a t)"), yb[:, u]).then_inc(s_y[u], 16)
                load_rest(0)
                load_delta(0)
                with nc.gpsimd.Fori(0, NBK - 1) as b:
                    ahead = nc.gpsimd.snap(b + 1)
                    pool.wait_ge(s.oa, b + 1)
                    hold(pool, s.held)
                    load_delta(ahead)
                    pool.wait_ge(s.ol, KD * (b + 1))
                    hold(pool, s.held)
                    load_rest(ahead)
                    stores(b)
                stores(NBK - 1)
                for u in range(2):
                    pool.wait_ge(s_y[u], 16 * NBK * KD // 2)

            @block.tensor
            def _(pe):
                def sums(b, heads):
                    pe.wait_ge(s.sq, b + 1)
                    for h in heads:
                        wait(pe, s.root, H * b + h - 1)
                        nc.tensor.matmul(pn[h % 2][:], g.ones, squares[:, h], start=True, stop=True).then_inc(s.sum, 1)

                def product(bank, n, rights, ks, split, b):
                    rh, rl = rights
                    for k in ks:
                        if split is not None:
                            pe.wait_ge(split, KD * b + k + 1)
                        high, low = (x[:, n, k * P:(k + 1) * P] for x in (wh, wl))
                        nc.tensor.matmul(bank[:], high, rh[:, k], start=(k == ks[0]), stop=False)
                        nc.tensor.matmul(bank[:], high, rl[:, k], start=False, stop=False)
                        last = nc.tensor.matmul(bank[:], low, rh[:, k], start=False, stop=(k == ks[-1]))
                    return last

                def block(b, more):
                    def gate(m, br, first):
                        pe.wait_ge(s.wl, NC * m + br + 1 + WL0)
                        pe.wait_ge(s.sig, NBR * m + br + 1)
                        product(pg[br], br, (hh, hl), range(KD), s.hl if first and br == 0 else None, b).then_inc(s.gate, 1)

                    def tile(m, u, first, near, last):
                        start = isinstance(m, int) and m == 0
                        if start:
                            gate(m, 0, first)
                            sums(0, range(H))
                            gate(m, 1, first)
                            gate(m, 2, first)
                        for br in range(NBR):
                            if not start:
                                gate(m, br, first)
                            if br == 0:
                                pe.wait_ge(s.wl, NC * m + WB + 1 + WL0)
                            pe.wait_ge(s.prod, NBR * m + br + 1)
                            product(pbr[br], WB, (oh, ol), range(*BRANCH[br]), s.ol if first else None, b).then_inc(s.br, 1)
                            if near == 0 and br < 2:
                                sums(b + 1, (2 * br, 2 * br + 1))
                    tiles(nc.tensor, b, more, tile)
                blocks(nc.tensor, block)

            @block.scalar
            def _(act):
                act.sem_inc(s.sig, SIG0)
                a = nc.scalar.activation

                def square(b):
                    act.wait_ge(s.osum, b + 1)
                    a(squares, ob[:, 0:H], ACT.Square).then_inc(s.sq, 1)

                def root(b, heads):
                    for h in heads:
                        act.wait_ge(s.sum, H * b + h + 1)
                        a(roots[:, h], pn[h % 2][:], ACT.Sqrt, bias=g.eps[:, 0:1], scale=1.0 / DK).then_inc(s.root, 1)

                def high_chunk(m, n):
                    act.wait_ge(s_w[n], 16 * m + 16)
                    a(wh[:, n], w[:, n], ACT.Copy).then_inc(s.wh, 1)

                def high_h(b):
                    act.wait_ge(s.ldh, 48 * b + 48)
                    for k in range(KD):
                        a(hh[:, k], hb[:, k], ACT.Copy).then_inc(s.hh, 1)

                def high_o(b):
                    act.wait_ge(s.oa, b + 1)
                    for k in range(KD):
                        a(oh[:, k], ob[:, k], ACT.Copy).then_inc(s.oh, 1)

                def block(b, more):
                    def tile(m, u, first, near, last):
                        if near == 0:
                            square(b + 1)
                        for br in range(NBR):
                            act.wait_ge(s.gate, NBR * m + br + 1)
                            act.wait_ge(s.prod, NBR * m + br + 1)
                            a(sg[:, br], pg[br][:], ACT.Sigmoid).then_inc(s.sig, 1)
                            if not last:
                                high_chunk(m + 1, br)
                            if near == 0 and br > 0:
                                root(b + 1, (2 * br - 2, 2 * br - 1))
                        if near == 1:
                            high_h(b + 1)
                        if not last:
                            act.wait_ge(s.br, NBR * m + NBR)
                            high_chunk(m + 1, WB)
                        if near == 1:
                            high_o(b + 1)
                    tiles(nc.scalar, b, more, tile)
                high_chunk(0, 0)
                high_h(0)
                square(0)
                for n in range(1, NC):
                    high_chunk(0, n)
                root(0, range(H))
                high_o(0)
                blocks(nc.scalar, block)

            @block.vector
            def _(dve):
                v = nc.vector
                dve.sem_inc(s.prod, PROD0)
                dve.sem_inc(s.wl, WL0)
                dve.wait_ge(s.cst, 16)
                da = ob[:, 0:H]

                def add_scans(b):
                    dve.wait_ge(s.ldo, 48 * b + 48)
                    v.tensor_tensor(da.rearrange("p h (b i) -> p b h i", i=P), scans[0], scans[1], ALU.add).then_inc(s.osum, 1)

                def invert(b, h):
                    dve.wait_ge(s.root, H * b + h + 1)
                    v.reciprocal(roots[:, h], roots[:, h]).then_inc(s.rec, 1)

                def norm(b):
                    dve.wait_ge(s.rec, (H + 1) * b + H)
                    v.scalar_tensor_tensor(da, da, gnw[:, 0:1], roots, ALU.mult, ALU.mult).then_inc(s.rec, 1)
                    dve.wait_ge(s.rec, (H + 1) * b + H + 1)
                    v.tensor_tensor(da, da, zt[:], ALU.mult).then_inc(s.oa, 1)

                def low_chunk(m, n):
                    dve.wait_ge(s.wh, NC * m + n + 1)
                    v.tensor_tensor(wl[:, n], w[:, n], wh[:, n], ALU.subtract).then_inc(s.wl, 1)

                def low_h(b):
                    for k in range(KD):
                        dve.wait_ge(s.hh, KD * b + k + 1)
                        v.tensor_tensor(hl[:, k], hb[:, k], hh[:, k], ALU.subtract).then_inc(s.hl, 1)

                def low_o(b):
                    for k in range(KD):
                        dve.wait_ge(s.oh, KD * b + k + 1)
                        v.tensor_tensor(ol[:, k], ob[:, k], oh[:, k], ALU.subtract).then_inc(s.ol, 1)

                def block(b, more):
                    def tile(m, u, first, near, last):
                        if near == 0:
                            add_scans(b + 1)
                        for br in range(NBR):
                            if not last:
                                low_chunk(m + 1, br)
                            if br == 0:
                                wait(dve, s.y, m)
                            dve.wait_ge(s.sig, NBR * m + br + 1 + SIG0)
                            dve.wait_ge(s.br, NBR * m + br + 1)
                            v.tensor_tensor(pr[:, br], sg[:, br], pbr[br][:], ALU.mult).then_inc(s.prod, 1)
                            if near == 0 and br > 0:
                                invert(b + 1, br - 1)
                            if near == 1 and br < 2:
                                invert(b + 1, 2 + br)
                            if near == 1 and br == 1:
                                norm(b + 1)
                        if near == 1:
                            low_h(b + 1)
                        if not last:
                            low_chunk(m + 1, WB)
                        dve.wait_ge(s.prod, NBR * m + NBR + PROD0)
                        v.tensor_tensor(pr[:, 0], pr[:, 0], pr[:, 1], ALU.add).then_inc(s.add, 1)
                        dve.wait_ge(s.add, m + 1)
                        dve.wait_ge(s_y[u], (m - u) * 8)
                        v.tensor_tensor(yb[:, u], pr[:, 0], pr[:, 2], ALU.add).then_inc(s.y, 1)
                        if near == 1:
                            low_o(b + 1)
                    tiles(nc.vector, b, more, tile)
                low_chunk(0, 0)
                low_h(0)
                add_scans(0)
                for n in range(1, NC):
                    low_chunk(0, n)
                for h in range(H):
                    invert(0, h)
                norm(0)
                low_o(0)
                blocks(nc.vector, block)


def project_out(nc, g):
    with ExitStack() as c:
        wo = sbuf(nc, c, "wo", [P, KD, D])
        wh, wl = (sbuf(nc, c, n, [P, KD, D], F32R) for n in ("wo_high", "wo_low"))
        y = sbuf(nc, c, "yp", [P, 2, KD, P])
        yh, yl = (sbuf(nc, c, n, [P, 2, KD, P], F32R) for n in ("yp_high", "yp_low"))
        rows = sbuf(nc, c, "rowsm", [P, 3, D])
        wr = sbuf(nc, c, "wr", [P, KD, E])
        xt = sbuf(nc, c, "xt", [P, 2, D])
        h2 = sbuf(nc, c, "h2", [P, 2, D])
        h2T = sbuf(nc, c, "h2T", [P, KD, P])
        st = sbuf(nc, c, "stat", [P, 2])
        po = [[psum(nc, c, f"po{u}{n}") for n in range(2)] for u in range(2)]
        pt = [psum(nc, c, f"ptp{n}") for n in range(2)]
        pl = psum(nc, c, "plp")
        s = sems(nc, c, "po", "cst rt " + " ".join(f"wo{k}" for k in range(KD)) + " wh wl y0 y1 yh yl x0 x1 out half x1d ssq sr h2a h2 tr trc lg lgc st0 st1 held")
        s_wo = list(s[2:2 + KD])
        s_ld, s_x, s_st = [s.y0, s.y1], [s.x0, s.x1], [s.st0, s.st1]

        def steps(eng, step):
            for u in range(2):
                step(u, u, True)
            with eng.Fori(1, LT // 2 - 1) as i:
                for u in range(2):
                    step(2 * i + u, u, True)
            for u in range(2):
                step(LT - 2 + u, u, u == 0)

        def first(t):
            return isinstance(t, int) and t == 0

        with nc.Block() as block:
            @block.sync
            def _(sp):
                def load_y(t, u):
                    wait(sp, s.yl, t - 1)
                    sp.dma_start(y[:, u], g.y_d[:, :, bass.ds(t * P, P)]).then_inc(s_ld[u], 16)

                def load_x(t, u):
                    wait(sp, s_st[u], 16 * (t - u))
                    sp.dma_start(xt[:, u], g.x[bass.ds(t * P, P)]).then_inc(s_x[u], 16)
                load_y(0, 0)
                load_y(1, 1)
                for k in range(KD):
                    sp.dma_start(wo[:, k], g.w_out[:, k]).then_inc(s_wo[k], 16)
                sp.dma_start(rows[:], g.rows_d[:, 0:3]).then_inc(s.cst, 16)
                sp.dma_start(wr[:], g.w_router).then_inc(s.rt, 16)
                load_x(0, 0)
                load_x(1, 1)
                load_y(2, 0)
                load_y(3, 1)
                with nc.sync.Fori(1, LT // 2 - 1) as i:
                    for u in range(2):
                        t, later = nc.sync.snap(2 * i + u), nc.sync.snap(2 * i + u + 2)
                        load_x(t, u)
                        load_y(later, u)
                for u in range(2):
                    load_x(LT - 2 + u, u)

            @block.gpsimd
            def _(pool):
                with nc.gpsimd.Fori(0, LT // 2) as i:
                    for u in range(2):
                        at = nc.gpsimd.snap(i * 2 * P + u * P)
                        pool.wait_ge(s.h2, 2 * i + u + 1)
                        hold(pool, s.held)
                        pool.dma_start(g.out[bass.ds(at, P)], xt[:, u]).then_inc(s_st[u], 16)
                        pool.dma_start(g.h2_d[bass.ds(at, P)], h2[:, u]).then_inc(s_st[u], 16)
                for u in range(2):
                    pool.wait_ge(s_st[u], 16 * LT)

            @block.tensor
            def _(pe):
                def project(t, u, half, load):
                    wait(pe, s.half, 2 * t + half - 3)
                    pe.wait_ge(s.yl, t + 1)
                    for k in range(KD):
                        if load:
                            pe.wait_ge(s.wl, k + 1)
                        high, low = yh[:, u, k], yl[:, u, k]
                        rh, rl = (x[:, k, half * 512:(half + 1) * 512] for x in (wh, wl))
                        nc.tensor.matmul(po[u][half][:], high, rh, start=(k == 0), stop=False)
                        nc.tensor.matmul(po[u][half][:], high, rl, start=False, stop=False)
                        last = nc.tensor.matmul(po[u][half][:], low, rh, start=False, stop=(k == KD - 1))
                    last.then_inc(s.out, 1)

                def turn(t, u):
                    pe.wait_ge(s.h2, t + 1)
                    wait(pe, s.trc, 2 * t)
                    for q in range(2):
                        for j in range(4):
                            k = 4 * q + j
                            last = nc.tensor.transpose(pt[q][:, j * P:(j + 1) * P], h2[:, u, k * P:(k + 1) * P], g.ident)
                        last.then_inc(s.tr, 1)

                def route(t):
                    if first(t):
                        pe.wait_ge(s.rt, 16)
                    pe.wait_ge(s.trc, 2 * t + 2)
                    wait(pe, s.lgc, t)
                    for k in range(KD):
                        last = nc.tensor.matmul(pl[:, 0:E], h2T[:, k], wr[:, k], start=(k == 0), stop=(k == KD - 1))
                    last.then_inc(s.lg, 1)

                def step(t, u, more):
                    project(t, u, 0, first(t))
                    if not isinstance(t, int) or t > 1:
                        route(t - 2)
                    project(t, u, 1, False)
                    if not first(t):
                        turn(t - 1, 1 - u)
                steps(nc.tensor, step)
                route(LT - 2)
                turn(LT - 1, (LT - 1) % 2)
                route(LT - 1)

            @block.scalar
            def _(act):
                a = nc.scalar.activation

                def high(t, u):
                    act.wait_ge(s_ld[u], 8 * (t - u) + 16)
                    wait(act, s.out, 2 * t - 2)
                    a(yh[:, u], y[:, u], ACT.Copy).then_inc(s.yh, 1)

                def spread(t, u):
                    act.wait_ge(s.x1d, t + 1)
                    a(h2[:, u], xt[:, u], ACT.Square, accum_out=st[:, 0:1]).then_inc(s.ssq, 1)
                    act.wait_ge(s.ssq, t + 1)
                    wait(act, s.h2, t)
                    a(st[:, 1:2], st[:, 0:1], ACT.Sqrt, bias=g.eps[:, 0:1], scale=1.0 / D).then_inc(s.sr, 1)

                def logits(t):
                    at = t if isinstance(t, int) else nc.scalar.snap(t)
                    act.wait_ge(s.lg, t + 1)
                    a(g.logits[:, bass.ds(at, 1)].rearrange("p a e -> p (a e)"), pl[:, 0:E], ACT.Copy).then_inc(s.lgc, 1)

                def turned(t):
                    wait(act, s.lg, t)
                    for q in range(2):
                        act.wait_ge(s.tr, 2 * t + q + 1)
                        a(h2T[:, 4 * q:4 * q + 4], pt[q][:].rearrange("p (k t) -> p k t", k=4), ACT.Copy).then_inc(s.trc, 1)

                def step(t, u, more):
                    if first(t):
                        high(t + 1, 1 - u)
                        for k in range(KD):
                            act.wait_ge(s_wo[k], 16)
                            a(wh[:, k], wo[:, k], ACT.Copy).then_inc(s.wh, 1)
                        return
                    spread(t - 1, 1 - u)
                    if more:
                        high(t + 1, 1 - u)
                    if not isinstance(t, int) or t > 1:
                        logits(t - 2)
                    turned(t - 1)
                high(0, 0)
                steps(nc.scalar, step)
                spread(LT - 1, (LT - 1) % 2)
                logits(LT - 2)
                turned(LT - 1)
                logits(LT - 1)

            @block.vector
            def _(dve):
                v = nc.vector
                dve.wait_ge(s.cst, 16)

                def low(t, u):
                    dve.wait_ge(s.yh, t + 1)
                    v.tensor_tensor(yl[:, u], y[:, u], yh[:, u], ALU.subtract).then_inc(s.yl, 1)

                def residual(t, u):
                    dve.wait_ge(s_x[u], 8 * (t - u) + 16)
                    wait(dve, s.tr, 2 * t - 2)
                    for half in range(2):
                        cols = slice(half * 512, (half + 1) * 512)
                        dve.wait_ge(s.out, 2 * t + half + 1)
                        v.tensor_tensor(h2[:, u, cols], po[u][half][:], rows[:, 0, cols], ALU.mult).then_inc(s.half, 1)
                    dve.wait_ge(s.half, 2 * t + 2)
                    v.tensor_tensor(xt[:, u], xt[:, u], h2[:, u], ALU.add).then_inc(s.x1d, 1)

                def norm(t, u):
                    dve.wait_ge(s.sr, t + 1)
                    v.reciprocal(st[:, 1:2], st[:, 1:2]).then_inc(s.h2a, 1)
                    dve.wait_ge(s.h2a, 2 * t + 1)
                    v.scalar_tensor_tensor(h2[:, u], xt[:, u], st[:, 1:2], rows[:, 2], ALU.mult, ALU.mult).then_inc(s.h2a, 1)
                    dve.wait_ge(s.h2a, 2 * t + 2)
                    v.tensor_tensor(h2[:, u], h2[:, u], rows[:, 1], ALU.add).then_inc(s.h2, 1)

                def step(t, u, more):
                    if not first(t):
                        residual(t - 1, 1 - u)
                    if first(t):
                        low(t + 1, 1 - u)
                        for k in range(KD):
                            dve.wait_ge(s.wh, k + 1)
                            v.tensor_tensor(wl[:, k], wo[:, k], wh[:, k], ALU.subtract).then_inc(s.wl, 1)
                    else:
                        norm(t - 1, 1 - u)
                        if more:
                            low(t + 1, 1 - u)
                low(0, 0)
                steps(nc.vector, step)
                residual(LT - 1, (LT - 1) % 2)
                norm(LT - 1, (LT - 1) % 2)


def choose(nc, g):
    HT = LT // 2
    NS = CAP // P
    with ExitStack() as c:
        lg2 = sbuf(nc, c, "lg2", [P, HT, 2 * E])
        aff = sbuf(nc, c, "aff", [2 * E, SEQ // 2])
        red = sbuf(nc, c, "redc", [P, LT])
        val = sbuf(nc, c, "val", [2 * E, CAP])
        idx = sbuf(nc, c, "idx", [2 * E, CAP], U32)
        idf = sbuf(nc, c, "idf", [2 * E, CAP])
        tv = sbuf(nc, c, "tv", [P, NS, 2, 2 * E])
        low = sbuf(nc, c, "lowidx", [P, NS, E])
        first = sbuf(nc, c, "isfirst", [P, NS, E])
        ps = psum(nc, c, "aff_ps", (P, 2, 512))
        pt = psum(nc, c, "ct_ps")
        pf = psum(nc, c, "cf_ps")
        s = sems(nc, c, "ch", "own ex aff tr trc top mi idf ct tv fl mg")
        with nc.Block() as block:
            @block.scalar
            def _(act):
                act.wait_ge(s.own, 2)
                nc.scalar.activation(g.logits, g.logits, ACT.Exp).then_inc(s.ex, 1)
                for q in range(2):
                    act.wait_ge(s.tr, q + 1)
                    nc.scalar.activation(aff[:, q * 512:(q + 1) * 512], ps[0:2 * E, q], ACT.Copy).then_inc(s.trc, 1)

            @block.tensor
            def _(pe):
                pe.wait_ge(s.aff, 1)
                for q in range(2):
                    for j in range(4):
                        last = nc.tensor.transpose(ps[0:2 * E, q, j * P:(j + 1) * P], lg2[:, 4 * q + j], g.ident)
                    last.then_inc(s.tr, 1)
                pe.wait_ge(s.idf, 1)
                for part in range(NS):
                    for j, rows in enumerate((val, idf)):
                        at = (2 * part + j) * 2 * E
                        last = nc.tensor.transpose(pt[:, at:at + 2 * E], rows[:, part * P:(part + 1) * P], g.ident[0:2 * E, 0:2 * E])
                last.then_inc(s.ct, 1)
                pe.wait_ge(s.tv, 1)
                nc.tensor.matmul(pf[:, 0:NS * 4 * E], g.flip, tv[:].rearrange("p a j e -> p (a j e)"), start=True, stop=True).then_inc(s.fl, 1)

            @block.vector
            def _(dve):
                v = nc.vector
                own = Steps(dve, s.own)
                lg = g.logits
                wide = red[:, :, None].broadcast_to([P, LT, E])
                own.done(v.tensor_reduce(red[:], lg, AX_X, ALU.max))
                own.settle()
                own.done(v.tensor_tensor(lg, lg, wide, ALU.subtract))
                dve.wait_ge(s.ex, 1)
                own.done(v.tensor_reduce(red[:], lg, AX_X, ALU.add))
                own.settle()
                own.done(v.reciprocal(red[:], red[:]))
                own.settle()
                for half in range(2):
                    at = slice(half * HT, (half + 1) * HT)
                    last = v.tensor_tensor(lg2[:, :, half * E:(half + 1) * E], lg[:, at], wide[:, at], ALU.mult)
                last.then_inc(s.aff, 1)
                dve.wait_ge(s.trc, 2)
                own = Steps(dve, s.top)
                for r in range(CAP // 8):
                    at = slice(8 * r, 8 * r + 8)
                    own.done(v.max(val[:, at], aff[:]))
                    own.settle()
                    v.max_index(idx[:, at], val[:, at], aff[:]).then_inc(s.mi, 1)
                    own.done(v.match_replace(aff[:], val[:, at], aff[:], -1.0))
                    own.settle()
                dve.wait_ge(s.mi, CAP // 8)
                v.tensor_copy(idf[:], idx[:]).then_inc(s.idf, 1)
                dve.wait_ge(s.ct, 1)
                v.tensor_copy(tv[:].rearrange("p a j e -> p (a j e)"), pt[:, 0:NS * 4 * E]).then_inc(s.tv, 1)
                dve.wait_ge(s.tv, 1)
                dve.wait_ge(s.fl, 1)
                own = Steps(dve, s.mg)
                flipped = pf[:, 0:NS * 4 * E].rearrange("p (a j e) -> p a j e", j=2, e=2 * E)
                for part in range(NS):
                    a_val, a_idx = tv[:, part, 0, 0:E], tv[:, part, 1, 0:E]
                    b_val, b_idx = flipped[:, NS - 1 - part, 0, E:2 * E], flipped[:, NS - 1 - part, 1, E:2 * E]
                    own.done(v.tensor_tensor(first[:, part], a_val, b_val, ALU.is_ge))
                    own.done(v.tensor_tensor(g.top_aff[:, part], a_val, b_val, ALU.max))
                    own.done(v.tensor_scalar(low[:, part], b_idx, float(SEQ // 2), None, ALU.add))
                    own.settle()
                    own.done(v.tensor_tensor(tv[:, part, 1, E:2 * E], a_idx, low[:, part], ALU.subtract))
                    own.settle()
                    own.done(v.tensor_tensor(first[:, part], first[:, part], tv[:, part, 1, E:2 * E], ALU.mult))
                    own.settle()
                    own.done(v.tensor_tensor(low[:, part], low[:, part], first[:, part], ALU.add))
                    own.settle()
                    own.done(v.tensor_copy(g.top_idx[:, part], low[:, part]))
                own.settle()


def experts(nc, g):
    NF = FE // P
    NW = 3 * NF
    HALF = CAP // P
    RAW, CUT = NW // 2, NF
    LEAD = CUT - 1
    TURN = 5
    with ExitStack() as c:
        w = sbuf(nc, c, "we", [P, RAW, D])
        wh, wl = (sbuf(nc, c, n, [P, CUT, D], F32R) for n in ("we_high", "we_low"))
        gt2 = sbuf(nc, c, "gt2", [P, D])
        ti = sbuf(nc, c, "ti", [P, 2, HALF], U32)
        ta = sbuf(nc, c, "ta", [P, 2, HALF])
        xe = sbuf(nc, c, "xe", [P, HALF, D])
        xh, xl = (sbuf(nc, c, n, [P, 2, KD, CAP], F32R) for n in ("xe_high", "xe_low"))
        hid = sbuf(nc, c, "hid", [P, 2, CAP])
        hh, hl = (sbuf(nc, c, n, [P, NF, CAP], F32R) for n in ("hid_high", "hid_low"))
        sg = sbuf(nc, c, "sge", [P, 2, CAP])
        yb = sbuf(nc, c, "ybe", [P, HALF, D])
        pg = [psum(nc, c, f"eg{n}") for n in range(2)]
        pu = [psum(nc, c, f"eu{n}") for n in range(2)]
        py = [[psum(nc, c, f"ey{a}{n}") for n in range(2)] for a in range(HALF)]
        s = sems(nc, c, "ex", "cst pick ga0 ga1 tr xh xl used wh wl sig hid hh hl yb sc0 sc1 held " + " ".join(f"w{n}" for n in range(RAW)))
        s_w = list(s[-RAW:])
        s_ga, s_sc = [s.ga0, s.ga1], [s.sc0, s.sc1]

        with nc.Block() as block:
            @block.sync
            def _(sp):
                sp.dma_start(gt2[:], g.rows_d[:, 3]).then_inc(s.cst, 16)
                for n in range(RAW):
                    sp.dma_start(w[:, n], g.w_ex[0, n]).then_inc(s_w[n], 16)

                def load(e, n):
                    sp.wait_ge(s.wl, NW * e + n - RAW + 1)
                    sp.dma_start(w[:, n % RAW], g.w_ex[e, n]).then_inc(s_w[n % RAW], 16)
                for n in range(RAW, NW):
                    load(0, n)
                with nc.sync.Fori(1, E) as e:
                    for n in range(NW):
                        load(e, n)

            @block.gpsimd
            def _(pool):
                def gather(e, u):
                    pool.wait_ge(s.pick, 2 * e + 2)
                    wait(pool, s.tr, 4 * e)
                    hold(pool, s.held)
                    for a in range(HALF):
                        pool.indirect_dma_start(xe[:, a], None, g.h2_d,
                                                bass.IndirectOffsetOnAxis(ap=ti[:, u, a:a + 1], axis=0)).then_inc(s_ga[u], 16)

                def scatter(e, u, others):
                    pool.wait_ge(s.yb, 4 * e + 4)
                    pool.wait_ge(s_sc[1 - u], others)
                    hold(pool, s.held)
                    for a in range(HALF):
                        pool.indirect_dma_start(g.out, bass.IndirectOffsetOnAxis(ap=ti[:, u, a:a + 1], axis=0), yb[:, a], None,
                                                compute_op=ALU.add).then_inc(s_sc[u], 16)

                def pair(i, last):
                    scatter(2 * i, 0, 32 * i)
                    if not last:
                        gather(2 * i + 2, 0)
                    scatter(2 * i + 1, 1, 32 * i + 32)
                    if not last:
                        gather(2 * i + 3, 1)
                for u in range(2):
                    gather(u, u)
                with nc.gpsimd.Fori(0, E // 2 - 1) as i:
                    pair(i, False)
                pair(E // 2 - 1, True)
                for u in range(2):
                    pool.wait_ge(s_sc[u], 32 * E // 2)

            @block.tensor
            def _(pe):
                def turn(e, u):
                    pe.wait_ge(s_ga[u], 32 * ((e - u) // 2) + 32 if isinstance(e, int) else e * 16 + (2 - u) * 16)
                    wait(pe, s.yb, 4 * (e - 1) if not isinstance(e, int) or e > 1 else 0)
                    for a in range(HALF):
                        for q in range(2):
                            for j in range(4):
                                k = 4 * q + j
                                last = nc.tensor.transpose(py[a][q][:, j * P:(j + 1) * P], xe[:, a, k * P:(k + 1) * P], g.ident)
                            last.then_inc(s.tr, 1)

                def expert(e, u, last_one):
                    pe.wait_ge(s.xl, 4 * e + 4)
                    for f in range(NF):
                        for n, bank, free in ((2 * f, pg[f % 2], s.sig), (2 * f + 1, pu[f % 2], s.hid)):
                            pe.wait_ge(s.wl, NW * e + n + 1)
                            pe.wait_ge(free, NF * e + f + 1)
                            for k in range(KD):
                                high, low = (x[:, n % CUT, k * P:(k + 1) * P] for x in (wh, wl))
                                nc.tensor.matmul(bank[:, 0:CAP], high, xh[:, u, k], start=(k == 0), stop=False)
                                nc.tensor.matmul(bank[:, 0:CAP], high, xl[:, u, k], start=False, stop=False)
                                last = nc.tensor.matmul(bank[:, 0:CAP], low, xh[:, u, k], start=False, stop=(k == KD - 1))
                            last.then_inc(s.used, 1)
                        if f == TURN and not last_one:
                            turn(e + 1, 1 - u)
                    if not last_one:
                        pe.wait_ge(s.xl, 4 * e + 8)
                    else:
                        pe.wait_ge(s.yb, 4 * e)
                    for f in range(NF):
                        n = 2 * NF + f
                        pe.wait_ge(s.wl, NW * e + n + 1)
                        pe.wait_ge(s.hl, NF * e + f + 1)
                        for a in range(HALF):
                            high, low = (x[:, f, a * P:(a + 1) * P] for x in (hh, hl))
                            for lhs, rhs in ((high, wh), (high, wl), (low, wh)):
                                for q in range(2):
                                    last = nc.tensor.matmul(py[a][q][:], lhs, rhs[:, n % CUT, q * 512:(q + 1) * 512],
                                                            start=(f == 0 and lhs is high and rhs is wh),
                                                            stop=(f == NF - 1 and lhs is low))
                        last.then_inc(s.used, 1)
                turn(0, 0)
                with nc.tensor.Fori(0, E // 2 - 1) as i:
                    for u in range(2):
                        expert(2 * i + u, u, False)
                expert(E - 2, 0, False)
                expert(E - 1, 1, True)

            @block.scalar
            def _(act):
                act.sem_inc(s.sig, 2)

                def high_rows(e, u):
                    for a in range(HALF):
                        for q in range(2):
                            act.wait_ge(s.tr, 4 * e + 2 * a + q + 1)
                            nc.scalar.activation(xh[:, u, 4 * q:4 * q + 4, a * P:(a + 1) * P],
                                                 py[a][q][:].rearrange("p (k t) -> p k t", k=4), ACT.Copy).then_inc(s.xh, 1)

                def high_chunk(e, n):
                    act.wait_ge(s_w[n % RAW], 32 * e + 16 * (n // RAW + 1))
                    if not isinstance(e, int) or NW * e + n >= CUT:
                        act.wait_ge(s.used, NW * e + n - CUT + 1)
                    nc.scalar.activation(wh[:, n % CUT], w[:, n % RAW], ACT.Copy).then_inc(s.wh, 1)

                def expert(e, u, last_one):
                    for f in range(NF):
                        act.wait_ge(s.used, NW * e + 2 * f + 1)
                        act.wait_ge(s.hid, NF * e + f + 1)
                        nc.scalar.activation(sg[:, f % 2], pg[f % 2][:, 0:CAP], ACT.Silu).then_inc(s.sig, 1)
                        high_chunk(e, 2 * f + LEAD)
                        act.wait_ge(s.hid, NF * e + f + 1 + 2)
                        nc.scalar.activation(hh[:, f], hid[:, f % 2], ACT.Copy).then_inc(s.hh, 1)
                        high_chunk(e, 2 * f + 1 + LEAD)
                        if f == TURN and not last_one:
                            high_rows(e + 1, 1 - u)
                    for n in range(2 * NF + LEAD, NW + LEAD):
                        if n < NW or not last_one:
                            high_chunk(e, n)
                for n in range(LEAD):
                    high_chunk(0, n)
                high_rows(0, 0)
                with nc.scalar.Fori(0, E // 2 - 1) as i:
                    for u in range(2):
                        expert(2 * i + u, u, False)
                expert(E - 2, 0, False)
                expert(E - 1, 1, True)

            @block.vector
            def _(dve):
                v = nc.vector
                dve.sem_inc(s.hid, 2)
                dve.wait_ge(s.cst, 16)

                def pick(e, u, added):
                    at = e if isinstance(e, int) else nc.vector.snap(e)
                    wait(dve, s_sc[u], added)
                    v.tensor_copy(ti[:, u], g.top_idx[:, :, bass.ds(at, 1)].rearrange("p a e -> p (a e)")).then_inc(s.pick, 1)
                    v.tensor_copy(ta[:, u], g.top_aff[:, :, bass.ds(at, 1)].rearrange("p a e -> p (a e)")).then_inc(s.pick, 1)

                def low_rows(e, u):
                    for a in range(HALF):
                        for q in range(2):
                            dve.wait_ge(s.xh, 4 * e + 2 * a + q + 1)
                            at = (slice(None), u, slice(4 * q, 4 * q + 4), slice(a * P, (a + 1) * P))
                            v.tensor_tensor(xl[at], py[a][q][:].rearrange("p (k t) -> p k t", k=4), xh[at], ALU.subtract).then_inc(s.xl, 1)

                def low_chunk(e, n):
                    dve.wait_ge(s.wh, NW * e + n + 1)
                    v.tensor_tensor(wl[:, n % CUT], w[:, n % RAW], wh[:, n % CUT], ALU.subtract).then_inc(s.wl, 1)

                def expert(i, u, last_one):
                    e = 2 * i + u
                    for f in range(NF):
                        dve.wait_ge(s.used, NW * e + 2 * f + 2)
                        dve.wait_ge(s.sig, NF * e + f + 1 + 2)
                        v.tensor_tensor(hid[:, f % 2], sg[:, f % 2], pu[f % 2][:, 0:CAP], ALU.mult).then_inc(s.hid, 1)
                        low_chunk(e, 2 * f + LEAD)
                        dve.wait_ge(s.hh, NF * e + f + 1)
                        v.tensor_tensor(hl[:, f], hid[:, f % 2], hh[:, f], ALU.subtract).then_inc(s.hl, 1)
                        low_chunk(e, 2 * f + 1 + LEAD)
                        if f == TURN and not last_one:
                            low_rows(e + 1, 1 - u)
                        if f == 1 and not last_one and (u == 1 or not isinstance(i, int) or i > 0):
                            pick(e + 1, 1 - u, 32 * (i + u))
                    for n in range(2 * NF + LEAD, NW + LEAD):
                        if n < NW or not last_one:
                            low_chunk(e, n)
                    dve.wait_ge(s.used, NW * (e + 1))
                    dve.wait_ge(s.pick, 2 * e + 2)
                    wait(dve, s_sc[1 - u], 32 * (i + u))
                    for a in range(HALF):
                        for q in range(2):
                            cols = slice(q * 512, (q + 1) * 512)
                            v.scalar_tensor_tensor(yb[:, a, cols], py[a][q][:], ta[:, u, a:a + 1], gt2[:, cols],
                                                   ALU.mult, ALU.mult).then_inc(s.yb, 1)
                pick(0, 0, 0)
                pick(1, 1, 0)
                for n in range(LEAD):
                    low_chunk(0, n)
                low_rows(0, 0)
                expert(0, 0, False)
                expert(0, 1, False)
                with nc.vector.Fori(1, E // 2 - 1) as i:
                    for u in range(2):
                        expert(i, u, False)
                expert(E // 2 - 1, 0, False)
                expert(E // 2 - 1, 1, True)


def shape_tables():
    i = np.arange(P)
    t = np.zeros((P, C_W), np.float32)
    t[:, C_ID:C_ID + P] = np.eye(P)
    t[:, C_FLIP:C_FLIP + P] = np.eye(P)[::-1]
    t[:, C_ONE:C_ONE + P] = 1.0
    t[:, C_BLK:C_BLK + P] = (i[:, None] // DH) == (i[None, :] // DH)
    nf = DK // 4
    for half in range(2):
        for f in range(nf):
            a, b = half * 2 * nf + f, half * 2 * nf + nf + f
            t[b, C_ROT + a] = -1.0
            t[a, C_ROT + b] = 1.0
    l, m = i[:, None], i[None, :]
    for d in range(2):
        before, after = (l <= m, l > m) if d == 0 else (l >= m, l < m)
        at = C_DIR + d * N_DIRT * P
        t[:, at:at + P] = before
        t[:, at + P:at + 2 * P] = after
        for lev in range(N_LEV):
            size = 1 << lev
            pair = (l // (2 * size)) == (m // (2 * size))
            up, low = (l // size) % 2 == 1, (m // size) % 2 == 0
            mask = pair & up & low if d == 0 else pair & ~up & ~low
            at = C_LEV + (d * N_LEV + lev) * P
            t[:, at:at + P] = mask
    start = np.clip(np.arange(GRID) - WC // 2, 0, GRID - WC)
    j, col = i[:, None] % GRID, np.arange(GRID)[None, :]
    t[:, C_WIN:C_WIN + GRID] = np.where((col >= start[j]) & (col < start[j] + WC), 0.0, NEG)
    f = np.zeros((P, F_W), np.float64)
    same = (l // 64) == (m // 64)
    ang = 2 * np.pi * ((l % 64) * (m % 64) % 64) / 64
    f[:, F_C4:F_C4 + P] = same * np.cos(ang) / np.sqrt(SEQ * 64)
    f[:, F_C4 + P:F_C4 + 2 * P] = same * np.sin(ang) / np.sqrt(SEQ * 64)
    ang = 2 * np.pi * (l * m % P) / P
    for n, table in enumerate((np.cos(ang), np.sin(ang), -np.sin(ang))):
        f[:, F_N1 + n * P:F_N1 + (n + 1) * P] = table
    n2 = SEQ // P
    ang = 2 * np.pi * (i[:, None] * np.arange(n2)[None, :]) / SEQ
    f[:, F_TW:F_TW + n2], f[:, F_TW + n2:F_TW + 2 * n2] = np.cos(ang), np.sin(ang)
    lo = P // n2
    ang = 2 * np.pi * ((l // lo) * (m // lo) % n2) / n2
    same = (l % lo) == (m % lo)
    f[:, F_K2:F_K2 + P], f[:, F_K2 + P:F_K2 + 2 * P] = same * np.cos(ang), -1.0 * same * np.sin(ang)
    tok = np.arange(SEQ)
    inv = 10000.0 ** (-np.arange(nf) / nf)
    where = np.stack([tok // GRID, tok % GRID])
    ang = where[:, None, :] * inv[None, :, None]
    ang = np.repeat(ang[:, None], 2, axis=1).reshape(P, SEQ)
    rope = np.stack([np.cos(ang), np.sin(ang)], axis=1).astype(np.float32)
    return {"consts": t, "rope": rope, "ftab": f.astype(np.float32)}


def expert_chunks(i):
    gate, up = (i[n][0].reshape(E, KD, P, FE // P, P).transpose(0, 3, 2, 1, 4).reshape(E, FE // P, 1, P, D)
                for n in ("w_e_gate", "w_e_up"))
    down = i["w_e_down"][0].reshape(E, FE // P, P, D)
    first = np.concatenate([gate, up], axis=2).reshape(E, 2 * FE // P, P, D)
    return np.concatenate([first, down], axis=1)


def layouts(i):
    tokens = np.concatenate([i["ctx"][0], i["x"][0]], axis=0)

    def col(v):
        return v.reshape(-1, P).T

    def tiles(m):
        return m.reshape(KD, P, -1, P).transpose(2, 1, 0, 3)

    w_in = i["w_in"][0]
    cuts = np.cumsum([0, 512, 512, 512, 512, 8, 8, 256, 256, 256, 256, 3 * D])
    part = [w_in[:, a:b] for a, b in zip(cuts[:-1], cuts[1:])]
    q, k, v, z, a, b, u, qn, kn, vn, gr = part
    wm, bm = i["w_mod"][0], i["b_mod"][0]
    out = {
        "xT": tokens.T.reshape(KD, P, T).transpose(1, 0, 2),
        "x": i["x"][0],
        "cc": np.stack([col(i["c"][0]), col(i["c_ctx"])], axis=-1),
        "w_mod_col": wm[:, :2 * D].reshape(KD, P, 2 * D).transpose(1, 0, 2),
        "w_mod_row": wm[:, 2 * D:].reshape(KD, P, 2, 2 * D).transpose(2, 0, 1, 3).reshape(2 * KD, P, 2 * D),
        "b_mod_col": col(bm[:2 * D]),
        "b_mod_row": bm[2 * D:],
        "norm1": col(i["norm1_w"][0]),
        "norm2": i["norm2_w"][0],
        "w_ch": tiles(np.concatenate([q, k, v, z, qn, kn, u], axis=1)),
        "w_tok": np.concatenate([vn, a, b], axis=1).reshape(KD, P, -1).transpose(1, 0, 2),
        "conv_w": i["conv_w"][0].reshape(CONV, 3, H, P).transpose(3, 2, 1, 0),
        "na_norm": np.stack([np.tile(i["na_qn_w"][0], 2), np.tile(i["na_kn_w"][0], 2)], axis=-1),
        "gdn_norm": i["gdn_norm_w"][0].reshape(P, 1),
        "w_gates": tiles(gr).reshape(3, KD, P, KD, P).transpose(1, 2, 0, 3, 4),
        "w_br": tiles(np.concatenate([i["w_br_a"][0], i["w_br_b"][0], i["w_br_c"][0]], axis=0)),
        "w_out": i["w_out"][0].reshape(KD, P, D).transpose(1, 0, 2),
        "w_router": i["w_router"][0].reshape(KD, P, E).transpose(1, 0, 2),
        "w_ex": expert_chunks(i),
        "rpb": i["na_rpb"][0].reshape(H * 15, 31),
        "a_log": i["a_log"][0].reshape(-1),
        "dt_bias": i["dt_bias"][0].reshape(-1),
    }
    out.update(shape_tables())
    return {n: np.ascontiguousarray(a) for n, a in out.items()}


def shared(tensors):
    class Shared(namedtuple("Tensors", list(tensors))):
        pass
    return Shared(**tensors)


SCRATCH = {
    "rows_d": (P, 4, D),
    "h_d": (P, KD, T),
    "q_d": (POS, P, H, P), "k_d": (POS, P, H, P), "kt_d": (POS, P, H, P), "vt_d": (POS, P, H, P),
    "z_d": (H, P, SEQ),
    "v_d": (T, 2 * P),
    "h2_d": (SEQ, D),
    "skew_d": (H * 15, GRID, 127),
    "oc_d": (2 * P, SEQ),
    "z2_d": (2, P, SEQ // P, FN),
    "yb_d": (2 * P, SEQ),
    "y_d": (P, KD, SEQ),
    "o_d": (2, POS, P, H, P),
}


def program(nc, g, stages=99):
    with ExitStack() as c:
        consts = sbuf(nc, c, "consts_sb", [P, C_W])
        eps = sbuf(nc, c, "eps_sb", [P, 1])
        g.eps = eps[:]
        g.ident, g.ones, g.blk, g.rot = (consts[:, at:at + P] for at in (C_ID, C_ONE, C_BLK, C_ROT))
        g.window = consts[:, C_WIN:C_WIN + GRID]
        g.flip = consts[:, C_FLIP:C_FLIP + P]
        g.dirt = lambda d, j: consts[:, C_DIR + (d * N_DIRT + j) * P:C_DIR + (d * N_DIRT + j + 1) * P]
        g.level = lambda d, lev: consts[:, C_LEV + (d * N_LEV + lev) * P:C_LEV + (d * N_LEV + lev + 1) * P]
        g.gd, g.beta, g.begc, g.esfx = (sbuf(nc, c, n, [P, 2, POS, H])[:] for n in ("gd", "beta", "begc", "esfx"))
        g.ab = sbuf(nc, c, "ab", [P, NT, 16])[:]
        load_tables(nc, g, consts, eps)
        with ExitStack() as c1:
            g.mod1 = sbuf(nc, c1, "mod1", [P, 2, KD, 2])[:]
            modulation(nc, g)
            g.hT = sbuf(nc, c1, "hT", [P, KD, T])[:]
            first_norm(nc, g)
            if stages < 2:
                return
            delta_inputs(nc, g)
            g.qn = sbuf(nc, c1, "qn", [P, HP, SEQ])[:]
            g.kn = sbuf(nc, c1, "kn", [P, HP, T])[:]
            g.uT = sbuf(nc, c1, "uT", [P, 2, SEQ])[:]
            mixer_inputs(nc, g)
            if stages >= 2.5:
                attention(nc, g)
                fourier(nc, g)
        if stages < 3:
            return
        decays(nc, g)
        delta_rule(nc, g)
        if stages < 4:
            return
        g.logits = sbuf(nc, c, "logits", [P, LT, E])[:]
        g.top_aff = sbuf(nc, c, "top_aff", [P, CAP // P, E])[:]
        g.top_idx = sbuf(nc, c, "top_idx", [P, CAP // P, E], U32)[:]
        merge(nc, g)
        project_out(nc, g)
        choose(nc, g)
        experts(nc, g)


def load_tables(nc, g, consts, eps):
    with ExitStack() as c:
        s = sems(nc, c, "tab", "ld eps")
        with nc.Block() as block:
            @block.sync
            def _(sp):
                sp.dma_start(consts[:], g.consts).then_inc(s.ld, 16)
                sp.wait_ge(s.ld, 16)

            @block.vector
            def _(dve):
                nc.vector.memset(eps[:], EPS).then_inc(s.eps, 1)
                dve.wait_ge(s.eps, 1)


def kernel(**inputs):
    import concourse.bacc as bacc
    from concourse.bass_utils import run_bass_kernel_spmd

    nc = bacc.Bacc("TRN2", target_bir_lowering=False, num_devices=1)
    arrays = {"in_" + n: a for n, a in layouts({n: np.asarray(a) for n, a in inputs.items()}).items()}
    tensors = {n[3:]: nc.dram_tensor(n, a.shape, mybir.dt.from_np(a.dtype), kind="ExternalInput").ap() for n, a in arrays.items()}
    tensors.update({n: nc.dram_tensor(n, list(shape), F32).ap() for n, shape in SCRATCH.items()})
    tensors["out"] = nc.dram_tensor("out", (SEQ, D), F32, kind="ExternalOutput").ap()
    g = shared(tensors)
    program(nc, g)
    r = run_bass_kernel_spmd(nc, [arrays], core_ids=[0])
    return r.results[0]["out"].reshape(1, SEQ, D)
```
